# Optimizing a Trainium2 kernel written in Bass

```python
import math
import jax
import jax.numpy as jnp
from jax import lax
import numpy as np
import jax, jax.numpy as jnp

D_MODEL = 1024
BATCH = 1
SEQ = 256
DEPTH = 2

MEM_LEN = 256
GRID_W = 64
CHUNK = 128
Q_BLOCK = 128
EPS = 1e-6
GM_GROUPS = 4
GM_GROUP_DIM = 128
GM_WIDTH = GM_GROUPS * GM_GROUP_DIM
HEAD_DIM = 64
N_Q_HEADS = 8
N_KV_HEADS = 2
Q_PER_KV = N_Q_HEADS // N_KV_HEADS
ATT_WIDTH = N_Q_HEADS * HEAD_DIM
KV_WIDTH = N_KV_HEADS * HEAD_DIM
ROPE_THETA = 10000.0
MIX_WIDTH = GM_WIDTH + ATT_WIDTH
IN_WIDTH = 2 * GM_WIDTH + ATT_WIDTH + 2 * KV_WIDTH
SPLITS = (GM_WIDTH, 2 * GM_WIDTH, 2 * GM_WIDTH + ATT_WIDTH, 2 * GM_WIDTH + ATT_WIDTH + KV_WIDTH)
X_HEADS = 4
X_HEAD_DIM = D_MODEL // X_HEADS
N_EXPERTS = 16
EC_FACTOR = 2
EXPERT_FF = 1024


def rms_norm(x, g):
    xf = x.astype(jnp.float32)
    y = xf * lax.rsqrt(jnp.mean(xf * xf, axis=-1, keepdims=True) + EPS)
    return (y * g.astype(jnp.float32)).astype(x.dtype)

def axial_rope_tables(seq_len):
    rows = seq_len // GRID_W
    row_id = jnp.repeat(jnp.arange(rows, dtype=jnp.float32), GRID_W)
    col_id = jnp.tile(jnp.arange(GRID_W, dtype=jnp.float32), rows)
    n_pairs = HEAD_DIM // 4
    freqs = jnp.exp(-math.log(ROPE_THETA) * jnp.arange(n_pairs, dtype=jnp.float32) / n_pairs)
    ang = jnp.concatenate([row_id[:, None] * freqs[None, :], col_id[:, None] * freqs[None, :]], axis=-1)
    return jnp.cos(ang), jnp.sin(ang)

def apply_rope(x, cos, sin):
    b, s, h, d = x.shape
    xf = x.astype(jnp.float32).reshape(b, s, h, d // 2, 2)
    x0, x1 = xf[..., 0], xf[..., 1]
    c = cos[None, :, None, :]
    sn = sin[None, :, None, :]
    out = jnp.stack([x0 * c - x1 * sn, x0 * sn + x1 * c], axis=-1)
    return out.reshape(b, s, h, d).astype(x.dtype)

def gmlp_group(u, v, v_norm_g, w_s, b_s):
    b, s, _ = u.shape
    v = rms_norm(v, v_norm_g).reshape(b, s // CHUNK, CHUNK, GM_GROUPS, GM_GROUP_DIM)
    mixed = jnp.einsum('gij,bnjgc->bnigc', w_s, v) + b_s.T[None, None, :, :, None]
    return u * mixed.reshape(b, s, GM_WIDTH)

def gqa_group(q, k, v, q_norm_g, k_norm_g, cos, sin):
    b, s, _ = q.shape
    q = q.reshape(b, s, N_Q_HEADS, HEAD_DIM)
    k = k.reshape(b, s, N_KV_HEADS, HEAD_DIM)
    v = v.reshape(b, s, N_KV_HEADS, HEAD_DIM)
    q = apply_rope(rms_norm(q, q_norm_g), cos, sin) * (HEAD_DIM ** -0.5)
    k = apply_rope(rms_norm(k, k_norm_g), cos, sin)
    n_blk = s // Q_BLOCK
    q_blocks = q.reshape(b, n_blk, Q_BLOCK, N_KV_HEADS, Q_PER_KV, HEAD_DIM).transpose(1, 0, 3, 4, 2, 5)

    def attend(qb):
        sc = jnp.einsum('bkgqd,bskd->bkgqs', qb, k, preferred_element_type=jnp.float32)
        p = jax.nn.softmax(sc, axis=-1).astype(v.dtype)
        return jnp.einsum('bkgqs,bskd->bkgqd', p, v)

    o = lax.map(attend, q_blocks)
    return o.transpose(1, 0, 4, 2, 3, 5).reshape(b, s, ATT_WIDTH)

def memory_cross_attention(h, mem_n, w_q, w_kv, w_o):
    b, s, _ = h.shape
    m = mem_n.shape[1]
    q = (h @ w_q).reshape(b, s, X_HEADS, X_HEAD_DIM) * (X_HEAD_DIM ** -0.5)
    kv = (mem_n @ w_kv).reshape(b, m, 2, X_HEADS, X_HEAD_DIM)
    k, v = kv[:, :, 0], kv[:, :, 1]
    sc = jnp.einsum('bshd,bmhd->bhsm', q, k, preferred_element_type=jnp.float32)
    p = jax.nn.softmax(sc, axis=-1).astype(v.dtype)
    o = jnp.einsum('bhsm,bmhd->bshd', p, v).reshape(b, s, D_MODEL)
    return o @ w_o

def expert_choice_moe(h, w_router, w_gate, w_up, w_down):
    b, s, _ = h.shape
    cap = EC_FACTOR * s // N_EXPERTS
    logits = jnp.einsum('bsd,de->bse', h, w_router, preferred_element_type=jnp.float32)
    aff = jax.nn.softmax(logits, axis=-1)
    gates, idx = lax.top_k(aff.transpose(0, 2, 1), cap)
    b_ix = jnp.arange(b)[:, None, None]
    xs = h[b_ix, idx]
    a = jnp.einsum('becd,edf->becf', xs, w_gate)
    u = jnp.einsum('becd,edf->becf', xs, w_up)
    y = jnp.einsum('becf,efd->becd', jax.nn.silu(a) * u, w_down)
    y = y * gates[..., None].astype(y.dtype)
    return jnp.zeros_like(h).at[b_ix, idx].add(y)

def first_inputs(seed: int = 0) -> dict:
    key = jax.random.key(seed)
    ks = jax.random.split(key, 24)

    def nrm(k, shape, scale):
        return jax.random.normal(k, shape, jnp.float32) * scale

    def gain(k, shape):
        return 1.0 + 0.05 * jax.random.normal(k, shape, jnp.float32)

    L, D = DEPTH, D_MODEL
    return {
        'x': nrm(ks[0], (BATCH, SEQ, D), 1.0),
        'mem': nrm(ks[1], (BATCH, MEM_LEN, D), 1.0),
        'mix_norm_g': gain(ks[2], (L, D)),
        'w_in': nrm(ks[3], (L, D, IN_WIDTH), D ** -0.5),
        'gm_v_norm_g': gain(ks[4], (L, GM_WIDTH)),
        'gm_w_s': nrm(ks[5], (L, GM_GROUPS, CHUNK, CHUNK), CHUNK ** -0.5),
        'gm_b_s': gain(ks[6], (L, GM_GROUPS, CHUNK)),
        'q_norm_g': gain(ks[7], (L, HEAD_DIM)),
        'k_norm_g': gain(ks[8], (L, HEAD_DIM)),
        'branch_norm_g': gain(ks[9], (L, 2, GM_WIDTH)),
        'w_out': nrm(ks[10], (L, MIX_WIDTH, D), MIX_WIDTH ** -0.5),
        'xattn_norm_g': gain(ks[11], (L, D)),
        'mem_norm_g': gain(ks[12], (D,)),
        'xattn_w_q': nrm(ks[13], (L, D, D), D ** -0.5),
        'xattn_w_kv': nrm(ks[14], (L, D, 2 * D), D ** -0.5),
        'xattn_w_o': nrm(ks[15], (L, D, D), D ** -0.5),
        'ffn_norm_g': gain(ks[16], (L, D)),
        'w_router': nrm(ks[17], (L, D, N_EXPERTS), D ** -0.5),
        'w_gate': nrm(ks[18], (L, N_EXPERTS, D, EXPERT_FF), D ** -0.5),
        'w_up': nrm(ks[19], (L, N_EXPERTS, D, EXPERT_FF), D ** -0.5),
        'w_down': nrm(ks[20], (L, N_EXPERTS, EXPERT_FF, D), EXPERT_FF ** -0.5),
        'final_norm_g': gain(ks[21], (D,)),
    }

def first_block(x, mem, mix_norm_g, w_in, gm_v_norm_g, gm_w_s, gm_b_s, q_norm_g, k_norm_g,
              branch_norm_g, w_out, xattn_norm_g, mem_norm_g, xattn_w_q, xattn_w_kv, xattn_w_o,
              ffn_norm_g, w_router, w_gate, w_up, w_down, final_norm_g):
    cos, sin = axial_rope_tables(x.shape[1])
    mem_n = rms_norm(mem, mem_norm_g)
    for l in range(DEPTH):
        h = rms_norm(x, mix_norm_g[l])
        proj = h @ w_in[l]
        u, v, q, k, vv = jnp.split(proj, SPLITS, axis=-1)
        gm = gmlp_group(jax.nn.gelu(u), jax.nn.gelu(v), gm_v_norm_g[l], gm_w_s[l], gm_b_s[l])
        at = gqa_group(q, k, vv, q_norm_g[l], k_norm_g[l], cos, sin)
        merged = jnp.concatenate([rms_norm(gm, branch_norm_g[l, 0]), rms_norm(at, branch_norm_g[l, 1])], axis=-1)
        x = x + merged @ w_out[l]
        x = x + memory_cross_attention(rms_norm(x, xattn_norm_g[l]), mem_n,
                                       xattn_w_q[l], xattn_w_kv[l], xattn_w_o[l])
        x = x + expert_choice_moe(rms_norm(x, ffn_norm_g[l]), w_router[l], w_gate[l], w_up[l], w_down[l])
    return rms_norm(x, final_norm_g)


RWKV_HEADS = 8
RWKV_HEAD_DIM = 64
RWKV_DIM = RWKV_HEADS * RWKV_HEAD_DIM
DECAY_LORA = 64
ICLR_LORA = 64
GATE_LORA = 128
LNX_EPS = 64e-5
MLA_HEADS = 8
QK_NOPE_DIM = 64
QK_ROPE_DIM = 32
V_HEAD_DIM = 64
Q_LORA_RANK = 256
KV_LORA_RANK = 128
NEG_INF = -1e30
FFN_DIM = 2816
CONV_WIDTH = 3
NORM_EPS = 1e-6
MAX_POS_OFFSET = 1024

SHIFT_COLS = 3 * RWKV_DIM + DECAY_LORA + ICLR_LORA + GATE_LORA
MLA_COLS = Q_LORA_RANK + KV_LORA_RANK + QK_ROPE_DIM
GATE_COLS = 2 * D_MODEL
IN_COLS = SHIFT_COLS + MLA_COLS + GATE_COLS


def _rmsnorm(x, g, eps=NORM_EPS):
    xf = x.astype(jnp.float32)
    xf = xf * lax.rsqrt(jnp.mean(xf * xf, axis=-1, keepdims=True) + eps)
    return xf.astype(x.dtype) * g

def _token_shift(x):
    return jnp.pad(x, ((0, 0), (1, 0), (0, 0)))[:, :-1]

def _rope_tables(positions, dtype):
    inv_freq = jnp.power(ROPE_THETA, -jnp.arange(0, QK_ROPE_DIM, 2, dtype=jnp.float32) / QK_ROPE_DIM)
    ang = positions.astype(jnp.float32)[..., None] * inv_freq
    return jnp.cos(ang).astype(dtype), jnp.sin(ang).astype(dtype)

def _rope(x, cos, sin):
    half = x.shape[-1] // 2
    x1, x2 = x[..., :half], x[..., half:]
    return jnp.concatenate([x1 * cos - x2 * sin, x1 * sin + x2 * cos], axis=-1)

def _wkv7_scan(r, w, k, v, a, b):
    B, S, H, N = r.shape

    def step(state, inp):
        r_t, w_t, k_t, v_t, a_t, b_t = inp
        sa = jnp.einsum('bhij,bhj->bhi', state, a_t)
        state = (state * w_t[:, :, None, :]
                 + sa[..., None] * b_t[:, :, None, :]
                 + v_t[..., None] * k_t[:, :, None, :])
        y_t = jnp.einsum('bhij,bhj->bhi', state, r_t)
        return state, y_t

    xs = tuple(jnp.moveaxis(t, 1, 0) for t in (r, w, k, v, a, b))
    s0 = jnp.zeros((B, H, N, N), jnp.float32)
    _, y = lax.scan(step, s0, xs)
    return jnp.moveaxis(y, 0, 1)

def _rwkv7_time_mix(p_r, p_k, p_v, p_w, p_a, p_g, decay_base, w_decay_up, iclr_base,
                    w_iclr_up, w_gate_up, k_k, k_a, r_k, lnx_w, lnx_b):
    B, S, _ = p_r.shape
    H, N = RWKV_HEADS, RWKV_HEAD_DIM
    dt = p_r.dtype

    def heads(t):
        return t.reshape(B, S, H, N)

    log_w = -jax.nn.softplus(-(decay_base + jnp.tanh(p_w) @ w_decay_up)) - 0.5
    decay = jnp.exp(-jnp.exp(log_w.astype(jnp.float32)))
    iclr = jax.nn.sigmoid(iclr_base + p_a @ w_iclr_up)
    gate = jax.nn.sigmoid(p_g) @ w_gate_up
    kk = heads((p_k * k_k).astype(jnp.float32))
    kk = kk * lax.rsqrt(jnp.sum(kk * kk, axis=-1, keepdims=True) + 1e-12)
    k = p_k * (1.0 + (iclr - 1.0) * k_a)
    r_h, k_h, v_h = heads(p_r), heads(k), heads(p_v)
    a_h = heads(iclr).astype(jnp.float32)
    y = _wkv7_scan(r_h.astype(jnp.float32), heads(decay), k_h.astype(jnp.float32),
                   v_h.astype(jnp.float32), -kk, kk * a_h)
    mu = jnp.mean(y, axis=-1, keepdims=True)
    var = jnp.mean(jnp.square(y - mu), axis=-1, keepdims=True)
    y = ((y - mu) * lax.rsqrt(var + LNX_EPS)).reshape(B, S, RWKV_DIM).astype(dt) * lnx_w + lnx_b
    bonus = (jnp.sum(r_h * k_h * r_k, axis=-1, keepdims=True) * v_h).reshape(B, S, RWKV_DIM)
    return (y + bonus) * gate

def _mla(q_lat, kv_lat, k_pe, cos, sin, q_norm, w_q_up, kv_norm, w_kv_up):
    B, S, _ = q_lat.shape
    H = MLA_HEADS
    q = (_rmsnorm(q_lat, q_norm) @ w_q_up).reshape(B, S, H, QK_NOPE_DIM + QK_ROPE_DIM)
    q_nope, q_pe = q[..., :QK_NOPE_DIM], q[..., QK_NOPE_DIM:]
    q_pe = _rope(q_pe, cos[:, :, None, :], sin[:, :, None, :])
    k_pe = _rope(k_pe, cos, sin)
    kv = (_rmsnorm(kv_lat, kv_norm) @ w_kv_up).reshape(B, S, H, QK_NOPE_DIM + V_HEAD_DIM)
    k_nope, v = kv[..., :QK_NOPE_DIM], kv[..., QK_NOPE_DIM:]

    n_blocks = S // Q_BLOCK
    qn_blocks = jnp.moveaxis(q_nope.reshape(B, n_blocks, Q_BLOCK, H, QK_NOPE_DIM), 1, 0)
    qr_blocks = jnp.moveaxis(q_pe.reshape(B, n_blocks, Q_BLOCK, H, QK_ROPE_DIM), 1, 0)
    starts = jnp.arange(n_blocks, dtype=jnp.int32) * Q_BLOCK
    key_pos = jnp.arange(S, dtype=jnp.int32)
    scale = (QK_NOPE_DIM + QK_ROPE_DIM) ** -0.5

    def attend(args):
        qn, qr, q0 = args
        s = (jnp.einsum('bqhd,bkhd->bhqk', qn, k_nope)
             + jnp.einsum('bqhr,bkr->bhqk', qr, k_pe)).astype(jnp.float32) * scale
        q_pos = q0 + jnp.arange(Q_BLOCK, dtype=jnp.int32)
        s = jnp.where(key_pos[None, :] <= q_pos[:, None], s, NEG_INF)
        p = jax.nn.softmax(s, axis=-1).astype(v.dtype)
        return jnp.einsum('bhqk,bkhd->bqhd', p, v)

    o = lax.map(attend, (qn_blocks, qr_blocks, starts))
    return jnp.moveaxis(o, 0, 1).reshape(B, S, H * V_HEAD_DIM)

def _mixer_block(n, cos, sin, w_in, mu_shift, decay_base, w_decay_up, iclr_base, w_iclr_up,
                 w_gate_up, k_k, k_a, r_k, lnx_w, lnx_b, w_out_rwkv, q_norm, w_q_up, kv_norm,
                 w_kv_up, w_out_mla, w_out):
    p = n @ w_in
    p_rw = p[..., :SHIFT_COLS]
    p_rw = p_rw + (_token_shift(p_rw) - p_rw) * mu_shift
    rw_splits = [RWKV_DIM, 2 * RWKV_DIM, 3 * RWKV_DIM, 3 * RWKV_DIM + DECAY_LORA,
                 3 * RWKV_DIM + DECAY_LORA + ICLR_LORA]
    p_r, p_k, p_v, p_w, p_a, p_g = jnp.split(p_rw, rw_splits, axis=-1)
    p_mla = p[..., SHIFT_COLS:SHIFT_COLS + MLA_COLS]
    q_lat, kv_lat, k_pe = jnp.split(p_mla, [Q_LORA_RANK, Q_LORA_RANK + KV_LORA_RANK], axis=-1)
    gate_a, gate_b = jnp.split(p[..., SHIFT_COLS + MLA_COLS:], 2, axis=-1)

    y_a = _rwkv7_time_mix(p_r, p_k, p_v, p_w, p_a, p_g, decay_base, w_decay_up, iclr_base,
                          w_iclr_up, w_gate_up, k_k, k_a, r_k, lnx_w, lnx_b) @ w_out_rwkv
    y_b = _mla(q_lat, kv_lat, k_pe, cos, sin, q_norm, w_q_up, kv_norm, w_kv_up) @ w_out_mla
    merged = jax.nn.sigmoid(gate_a) * y_a + jax.nn.sigmoid(gate_b) * y_b
    return merged @ w_out

def _conv_ffn(n, w_ffn_up, conv_w, conv_b, w_ffn_down):
    S = n.shape[1]
    u_gate, u_val = jnp.split(n @ w_ffn_up, 2, axis=-1)
    up = jnp.pad(u_gate, ((0, 0), (CONV_WIDTH - 1, 0), (0, 0)))
    c = conv_b
    for j in range(CONV_WIDTH):
        c = c + conv_w[j] * up[:, j:j + S]
    return (jax.nn.gelu(c, approximate=False) * u_val) @ w_ffn_down

def second_inputs(seed: int = 0) -> dict:
    key = jax.random.key(seed)
    ks = jax.random.split(key, 32)
    f32 = jnp.float32

    def nrm(k, shape, fan_in, s=1.0):
        return jax.random.normal(k, shape, f32) * (s * fan_in ** -0.5)

    def gain(k, shape):
        return 1.0 + 0.02 * jax.random.normal(k, shape, f32)

    H, N = RWKV_HEADS, RWKV_HEAD_DIM
    offs = jax.random.randint(ks[1], (BATCH, 1), 0, MAX_POS_OFFSET, dtype=jnp.int32)
    positions = offs + jnp.arange(SEQ, dtype=jnp.int32)[None, :]
    return {
        'x': jax.random.normal(ks[0], (BATCH, SEQ, D_MODEL), f32),
        'positions': positions,
        'attn_norm': gain(ks[2], (DEPTH, D_MODEL)),
        'w_in': nrm(ks[3], (DEPTH, D_MODEL, IN_COLS), D_MODEL),
        'mu_shift': jax.random.uniform(ks[4], (DEPTH, SHIFT_COLS), f32),
        'decay_base': jax.random.uniform(ks[5], (DEPTH, RWKV_DIM), f32, minval=-4.0, maxval=1.0),
        'w_decay_up': nrm(ks[6], (DEPTH, DECAY_LORA, RWKV_DIM), DECAY_LORA),
        'iclr_base': 0.1 * jax.random.normal(ks[7], (DEPTH, RWKV_DIM), f32),
        'w_iclr_up': nrm(ks[8], (DEPTH, ICLR_LORA, RWKV_DIM), ICLR_LORA),
        'w_gate_up': nrm(ks[9], (DEPTH, GATE_LORA, RWKV_DIM), GATE_LORA),
        'k_k': 0.85 + 0.05 * jax.random.normal(ks[10], (DEPTH, RWKV_DIM), f32),
        'k_a': 1.0 + 0.05 * jax.random.normal(ks[11], (DEPTH, RWKV_DIM), f32),
        'r_k': 0.1 * jax.random.normal(ks[12], (DEPTH, H, N), f32),
        'lnx_w': gain(ks[13], (DEPTH, RWKV_DIM)),
        'lnx_b': 0.02 * jax.random.normal(ks[14], (DEPTH, RWKV_DIM), f32),
        'w_out_rwkv': nrm(ks[15], (DEPTH, RWKV_DIM, D_MODEL), RWKV_DIM),
        'q_norm': gain(ks[16], (DEPTH, Q_LORA_RANK)),
        'w_q_up': nrm(ks[17], (DEPTH, Q_LORA_RANK, MLA_HEADS * (QK_NOPE_DIM + QK_ROPE_DIM)), Q_LORA_RANK),
        'kv_norm': gain(ks[18], (DEPTH, KV_LORA_RANK)),
        'w_kv_up': nrm(ks[19], (DEPTH, KV_LORA_RANK, MLA_HEADS * (QK_NOPE_DIM + V_HEAD_DIM)), KV_LORA_RANK),
        'w_out_mla': nrm(ks[20], (DEPTH, MLA_HEADS * V_HEAD_DIM, D_MODEL), MLA_HEADS * V_HEAD_DIM),
        'w_out': nrm(ks[21], (DEPTH, D_MODEL, D_MODEL), D_MODEL),
        'ffn_norm': gain(ks[22], (DEPTH, D_MODEL)),
        'w_ffn_up': nrm(ks[23], (DEPTH, D_MODEL, 2 * FFN_DIM), D_MODEL),
        'conv_w': nrm(ks[24], (DEPTH, CONV_WIDTH, FFN_DIM), CONV_WIDTH),
        'conv_b': 0.02 * jax.random.normal(ks[25], (DEPTH, FFN_DIM), f32),
        'w_ffn_down': nrm(ks[26], (DEPTH, FFN_DIM, D_MODEL), FFN_DIM),
        'final_norm': gain(ks[27], (D_MODEL,)),
    }

def second_block(x, positions, attn_norm, w_in, mu_shift, decay_base, w_decay_up, iclr_base,
              w_iclr_up, w_gate_up, k_k, k_a, r_k, lnx_w, lnx_b, w_out_rwkv, q_norm, w_q_up,
              kv_norm, w_kv_up, w_out_mla, w_out, ffn_norm, w_ffn_up, conv_w, conv_b,
              w_ffn_down, final_norm):
    cos, sin = _rope_tables(positions, x.dtype)
    h = x
    for l in range(DEPTH):
        n = _rmsnorm(h, attn_norm[l])
        h = h + _mixer_block(n, cos, sin, w_in[l], mu_shift[l], decay_base[l], w_decay_up[l],
                             iclr_base[l], w_iclr_up[l], w_gate_up[l], k_k[l], k_a[l], r_k[l],
                             lnx_w[l], lnx_b[l], w_out_rwkv[l], q_norm[l], w_q_up[l], kv_norm[l],
                             w_kv_up[l], w_out_mla[l], w_out[l])
        n = _rmsnorm(h, ffn_norm[l])
        h = h + _conv_ffn(n, w_ffn_up[l], conv_w[l], conv_b[l], w_ffn_down[l])
    return _rmsnorm(h, final_norm)


def setup_inputs(seed=0):
    out = dict(first_inputs(seed))
    for name, value in second_inputs(seed + 1).items():
        if name != "x":
            out[name + "_2"] = value
    return out


def reference(
    x, mem, mix_norm_g, w_in, gm_v_norm_g, gm_w_s, gm_b_s, q_norm_g, k_norm_g, branch_norm_g,
    w_out, xattn_norm_g, mem_norm_g, xattn_w_q, xattn_w_kv, xattn_w_o, ffn_norm_g, w_router,
    w_gate, w_up, w_down, final_norm_g, positions_2, attn_norm_2, w_in_2, mu_shift_2,
    decay_base_2, w_decay_up_2, iclr_base_2, w_iclr_up_2, w_gate_up_2, k_k_2, k_a_2, r_k_2,
    lnx_w_2, lnx_b_2, w_out_rwkv_2, q_norm_2, w_q_up_2, kv_norm_2, w_kv_up_2, w_out_mla_2,
    w_out_2, ffn_norm_2, w_ffn_up_2, conv_w_2, conv_b_2, w_ffn_down_2, final_norm_2,
):
    x = first_block(
        x, mem, mix_norm_g, w_in, gm_v_norm_g, gm_w_s, gm_b_s, q_norm_g, k_norm_g,
        branch_norm_g, w_out, xattn_norm_g, mem_norm_g, xattn_w_q, xattn_w_kv, xattn_w_o,
        ffn_norm_g, w_router, w_gate, w_up, w_down, final_norm_g,
    )
    return second_block(
        x, positions_2, attn_norm_2, w_in_2, mu_shift_2, decay_base_2, w_decay_up_2,
        iclr_base_2, w_iclr_up_2, w_gate_up_2, k_k_2, k_a_2, r_k_2, lnx_w_2, lnx_b_2,
        w_out_rwkv_2, q_norm_2, w_q_up_2, kv_norm_2, w_kv_up_2, w_out_mla_2, w_out_2,
        ffn_norm_2, w_ffn_up_2, conv_w_2, conv_b_2, w_ffn_down_2, final_norm_2,
    )


_drawn_inputs = setup_inputs


def setup_inputs(seed=0):
    import zlib

    import numpy as np

    out = dict(_drawn_inputs(seed))
    spreads = {}
    factors = {'xattn_norm_g': 4.088,
     'attn_norm_2': 2.767,
     'iclr_base_2': 2.971,
     'lnx_w_2': 6.483,
     'lnx_b_2': 6.608,
     'q_norm_2': 8.0,
     'kv_norm_2': 7.12,
     'conv_b_2': 3.676,
     'final_norm_2': 7.883,
     'ffn_norm_2': 2.969}
    for name, (base, spread) in spreads.items():
        noise = np.random.default_rng([zlib.crc32(name.encode()), seed]).standard_normal(out[name].shape)
        drawn = base * np.exp(spread * noise) if base else spread * noise
        out[name] = jnp.asarray(drawn.astype(out[name].dtype))
    for name, factor in factors.items():
        out[name] = (out[name] * factor).astype(out[name].dtype)
    return out
```

```python
import math

import numpy as np

import concourse.bass as bass
from concourse import mybir
from concourse.alu_op_type import AluOpType as ALU

F32 = mybir.dt.float32
I32 = mybir.dt.int32
U32 = mybir.dt.uint32
ACT = mybir.ActivationFunctionType
AX = mybir.AxisListType

P = 128
D = 1024
KD = D // P
T = 256
NT = T // P
L = 2
EPS = 1e-6
BANK = 512

GM_W, GM_G = 512, 4
NQ, NKV, HD = 8, 2, 64
HEADS_QK = NQ + NKV
XH, XD = 4, 256
E, CAP, FF = 16, 32, 1024

RW = 512
PAIRS = RW // P
CH = 32
NCH = T // CH
CT = P // CH
SHIFT_TILES = 14
QL, KVL, PE_D, NOPE = 256, 128, 32, 64
MH = 8
QKD = NOPE + PE_D
LAT = QL + KVL + PE_D
FFN = 2816
NF = FFN // P
NUP = NF // 2
LNX_EPS = 64e-5

SLOTS = 6
SLAB = 4096


class Slab:
    def __init__(self, slot, landed, held):
        self.slot, self.landed, self.held = slot, landed, held


def ring_plan(dmas):
    landed, held = [0] * SLOTS, [0] * SLOTS
    plan = []
    for i, n in enumerate(dmas):
        s = i % SLOTS
        landed[s] += 16 * n
        plan.append(Slab(s, landed[s], held[s]))
        held[s] += 1
    return plan, landed, held


DENSE1 = [1] * 18
PLAN1, LANDED1, HELD1 = ring_plan(DENSE1)
W_IN1, W_OUT1, W_XQ, W_XK, W_XV, W_XO = 0, 4, 8, 10, 12, 14
LANDED1_LAYER = [n + 16 * E for n in LANDED1]
HELD1_LAYER = [n + E for n in HELD1]
DENSE2 = [1] * 4 + [3] + [1] * 4 + [1, 1] + [1] * 2 + [2] * 11 + [1] * 6
PLAN2, LANDED2, HELD2 = ring_plan(DENSE2)
W_IN2, W_LAT, W_GATES, W_ORW, W_OMLA, W_OUT2, W_UP, W_DN = 0, 4, 5, 9, 10, 11, 13, 24
assert len(DENSE1) % SLOTS == 0 and len(DENSE2) % SLOTS == 0

CONST_COLS = {}


def _const_layout():
    at = 0
    for name, width in (("ident", P), ("head_sum", P), ("ones", P), ("cos1", NT * HD // 2), ("sin1", NT * HD // 2),
                        ("iota_row", T), ("iota_col", NT), ("expert_diag", E), ("causal", 2 * P),
                        ("low16", P), ("up16", P), ("low32x", P), ("up32", P), ("up32d", P),
                        ("scan", T), ("freq", PE_D // 2), ("eps", 64), ("neg_half", 1), ("kk_eps", 1),
                        ("lnx_eps", 1)):
        CONST_COLS[name] = (at, width)
        at += width
    return at


NCONST = _const_layout()


def constants():
    c = np.zeros((P, NCONST), np.float32)

    def put(name, value):
        at, width = CONST_COLS[name]
        c[:, at:at + width] = np.asarray(value, np.float32).reshape(-1, width)

    i = np.arange(P)
    put("ident", np.eye(P))
    put("head_sum", i[:, None] // 64 == i[None, :] // 64)
    put("ones", np.ones((P, P)))
    n = HD // 4
    freqs = np.exp(-math.log(10000.0) * np.arange(n, dtype=np.float32) / n).astype(np.float32)
    t = np.arange(T)
    ang = np.concatenate([(t // 64).astype(np.float32)[:, None] * freqs, (t % 64).astype(np.float32)[:, None] * freqs], 1)
    put("cos1", np.cos(ang).reshape(NT, P, HD // 2).transpose(1, 0, 2).reshape(P, -1))
    put("sin1", np.sin(ang).reshape(NT, P, HD // 2).transpose(1, 0, 2).reshape(P, -1))
    put("iota_row", np.broadcast_to(np.arange(T), (P, T)))
    put("iota_col", i[:, None] + P * np.arange(NT)[None, :])
    put("expert_diag", np.eye(P)[:, :E])
    put("causal", np.concatenate([np.zeros((P, P)), np.where(i[None, :] <= i[:, None], 0.0, -1e30)], 1))
    r, s = i[:, None], i[None, :]
    put("low16", (s < r) & (r // 16 == s // 16))
    put("up16", (r < s) & (r // 16 == s // 16))
    put("low32x", (r // CH == s // CH) & (r // 16 == s // 16 + 1))
    put("up32", (r < s) & (r // CH == s // CH))
    put("up32d", (r <= s) & (r // CH == s // CH))
    put("scan", np.broadcast_to((t % CH != 0), (P, T)))
    put("freq", np.broadcast_to(np.power(np.float32(10000.0), -np.arange(0, PE_D, 2, dtype=np.float32) / PE_D), (P, PE_D // 2)))
    eps = np.full(64, EPS)
    eps[32:52] = 64 * EPS
    put("neg_half", np.full((P, 1), -0.5))
    put("kk_eps", np.full((P, 1), 1e-12))
    put("lnx_eps", np.full((P, 1), LNX_EPS))
    put("eps", np.broadcast_to(eps, (P, 64)))
    return c


def _layout(items):
    cols, at = {}, 0
    for name, width in items:
        cols[name] = (at, width)
        at += width
    return cols, at


PAR1, NPAR1 = _layout((("mix_g", 8), ("x_g", 8), ("ffn_g", 8), ("branch_g", 8), ("b_s", GM_G), ("router", KD * E),
                       ("w_s", GM_G * P), ("v_g", GM_W), ("qk_g", HEADS_QK * HD)))
PAR2, NPAR2 = _layout((("attn_g", 8), ("ffn_g", 8), ("mu", 14), ("decay_base", 4), ("iclr_base", 4), ("k_k", 4),
                       ("k_a", 4), ("r_k", 4), ("lnx_w", 4), ("lnx_b", 4), ("q_g", 2), ("kv_g", 1), ("conv_w", 3 * NF),
                       ("conv_b", NF), ("lora_up", RW), ("gate_up", RW)))
NPAR = max(NPAR1, NPAR2)


def columns(v):
    v = np.asarray(v)
    return np.swapaxes(v.reshape(*v.shape[:-1], -1, P), -1, -2)


def rows(v, heads=1):
    v = np.asarray(v)
    return np.broadcast_to(np.tile(v, (1, heads))[:, None, :], (v.shape[0], P, heads * v.shape[1]))


def lay_out(a):
    par1 = np.concatenate([
        columns(a["mix_norm_g"]), columns(a["xattn_norm_g"]), columns(a["ffn_norm_g"]),
        columns(np.reshape(a["branch_norm_g"], (L, 2 * GM_W))), np.swapaxes(a["gm_b_s"], 1, 2),
        np.reshape(a["w_router"], (L, KD, P, E)).transpose(0, 2, 1, 3).reshape(L, P, KD * E),
        np.asarray(a["gm_w_s"]).transpose(0, 3, 1, 2).reshape(L, P, GM_G * P),
        rows(a["gm_v_norm_g"]), rows(a["q_norm_g"], NQ), rows(a["k_norm_g"], NKV)], axis=2)
    par2 = np.concatenate([
        columns(a["attn_norm_2"]), columns(a["ffn_norm_2"]), columns(a["mu_shift_2"]), columns(a["decay_base_2"]),
        columns(a["iclr_base_2"]), columns(a["k_k_2"]), columns(a["k_a_2"]), columns(np.reshape(a["r_k_2"], (L, RW))),
        columns(a["lnx_w_2"]), columns(a["lnx_b_2"]), columns(a["q_norm_2"]), columns(a["kv_norm_2"]),
        columns(np.reshape(a["conv_w_2"], (L, 3 * FFN))), columns(a["conv_b_2"]),
        np.concatenate([a["w_decay_up_2"], a["w_iclr_up_2"]], axis=1), np.asarray(a["w_gate_up_2"])], axis=2)
    fix = np.concatenate([columns(a["mem_norm_g"]), rows(np.asarray(a["final_norm_g"])[None])[0],
                          rows(np.asarray(a["final_norm_2"])[None])[0]], axis=1)
    return {"par1": np.ascontiguousarray(par1), "par2": np.ascontiguousarray(par2), "fix": np.ascontiguousarray(fix),
            "consts": constants(),
            "positions": np.ascontiguousarray(np.reshape(a["positions_2"], (NT, P)).T)}


AREA = 18100

GROUPS = {}


def group(name, pre=(), first=(), mid=(), second=(), post=()):
    GROUPS[name] = (pre, first, mid, second, post)


group("inputs", pre=[("inputs_loaded", 80)])
group("par", first=[("par1_loaded", 16)], second=[("par2_loaded", 16)])
group("fin", first=[("fin1_loaded", 16)], second=[("fin2_loaded", 16)])
group("store", post=[("out_stored", 32)])
group("norm_sq", pre=[("m_sq", 2)], first=[("h1_sq", 2), ("v_sq", 2), ("br_sq", 4), ("h2_sq", 2), ("h3_sq", 2)],
      mid=[("f1_sq", 2)], second=[("n1_sq", 2), ("l_sq", 4), ("n2_sq", 2)], post=[("f2_sq", 2)])
group("norm_rstd", pre=[("m_rstd", 1)],
      first=[("h1_rstd", 1), ("v_rstd", 1), ("qk_rstd", 1), ("br_rstd", 1), ("h2_rstd", 1), ("h3_rstd", 1)],
      mid=[("f1_rstd", 1)], second=[("n1_rstd", 1), ("l_rstd", 1), ("n2_rstd", 1)],
      post=[("f2_rstd", 1)])
group("norm_xn", pre=[("m_xn", 2)], first=[("h1_xn", 2), ("v_norm", 2), ("br_xn", 4), ("h2_xn", 2), ("h3_xn", 2)],
      second=[("n1_xn", 2), ("l_norm", 4), ("n2_xn", 2)])
group("norm_T", pre=[("m_T", 4)], first=[("h1_T", 4), ("br_T", 4), ("h2_T", 4), ("h3_T", 4)],
      second=[("n1_T", 4), ("l_T", 2), ("n2_T", 4)])
group("norm_cols_a", pre=[("m_cols_a", 4)], first=[("h1_cols_a", 4), ("br_cols_a", 4), ("h2_cols_a", 4), ("h3_cols_a", 4)],
      second=[("n1_cols_a", 4), ("l_cols", 3), ("n2_cols_a", 4)])
group("norm_cols_d", pre=[("m_cols_d", 4)], first=[("h1_cols_d", 4), ("br_cols_d", 4), ("h2_cols_d", 4), ("h3_cols_d", 4)],
      second=[("n1_cols_d", 4), ("n2_cols_d", 4)])
group("mix_pe", first=[("uv_full", 4), ("qkv_full", 4), ("mix_full", 2), ("qk_T", 3)])
group("mix_act", first=[("uv_gelu", 4), ("q_cols", 2)])
group("mix_dve", first=[("qkv_rows", 4), ("qk_ss", 1), ("qk_rot", 1), ("k_cols", 1), ("gm_rows", 2 * GM_G)])
group("gqa_pe_scores", first=[("sc_full", 2)], second=[("s2_full", 2)])
group("gqa_pe_turn", first=[("pT_full", 8)], second=[("p2_T", 6)])
group("gqa_pe_out", first=[("at_full", 2)], second=[("o2_full", 2)])
group("gqa_act_exp", first=[("sc_exp", 2 * NQ)], second=[("s2_exp", 2 * MH)])
group("gqa_act_cols", first=[("pT_a", 4)], second=[("p2_cols_a", 3)])
group("gqa_dve_max", first=[("sc_max", 2)], second=[("s2_max", 2)])
group("gqa_dve_cols", first=[("pT_d", 4)], second=[("p2_cols_d", 3)])
group("mla_dve_rows", second=[("p2_rows", 2)])
group("gqa_dve_out", first=[("at_rows", 2)], second=[("o2_cols", 2)])
group("res_pe", first=[("out1_full", 4), ("out2_full", 4)], second=[("out3_full", 4), ("down_full", 4)])
group("res_dve", pre=[("x_start", 1)], first=[("x_mixed", 4), ("x_attended", 4), ("x_routed", 4)],
      mid=[("x_first", 2)], second=[("h_mixed", 4), ("h_ffn", 4)], post=[("y_final", 2)])
group("mem_pe", first=[("xq_full", 4), ("xk_full", 4), ("xv_full", 4), ("xs_full", 2), ("xpT_full", 4), ("xo_full", 4)])
group("mem_act", first=[("xq_cols", 4), ("xv_rows", 4), ("xs_exp", NT * XH), ("xpT_a", 2), ("xo_cols_a", 2)])
group("mem_dve", first=[("xk_cols", 4), ("xs_max", 2), ("xp_rows", 2), ("xpT_d", 2), ("xo_cols_d", 2)])
group("route_pe", first=[("router_full", 2), ("aff_T", 1), ("top_T", 1)])
group("route_act", first=[("router_exp", 2)])
group("route_dve", first=[("router_max", 1), ("aff_rows", 1), ("top_found", 1), ("onehot", 3)])
for n in ("tok_full", "gu_full", "gu_T", "acc_full", "tok_cols", "hid_cols", "pick", "gu_rows", "gate_silu",
          "dn_rows_a", "dn_rows_d"):
    group(n, first=[(n, E)])
group("dn_full", first=[("dn_full", 2 * E)])
group("rope_dve", mid=[("rope_ang", 1)])
group("rope_act", mid=[("rope_set", 2)])
group("rw_pe", second=[("rw_full", 7), ("lat_full", 2), ("lora_full", 4), ("kk_full", 2)])
group("rw_act", second=[("rw_scaled", 14), ("lora_in", 1), ("lora_sig", 8), ("kk_root", 2), ("decays", 3)])
group("rw_dve", second=[("mu_set", 1), ("rw_cols", 14), ("lat_rows", 2), ("kk_sq", 1), ("log_w", 1), ("log_c", 4), ("c_less", 1)])
for n, c in (("pair_in", 5), ("tok_T", 2), ("tok_d", 2), ("tok_a", 1), ("prod_full", 3), ("prod_masked", 7), ("inv_full", 11),
             ("inv_a", 4), ("inv_d", 7), ("u_full", 1), ("u_rows", 1), ("wu_full", 1), ("wu_rows", 1), ("gh_full", 1),
             ("gh_set", 4), ("q_full", 1), ("q_set", 1), ("state_full", NCH - 2), ("state_set", NCH - 2), ("y_full", 1),
             ("y_cols", 1)):
    group(n, second=[(n, c * PAIRS)])
group("gn_pe", second=[("gn_full", 2), ("bonus_full", 2), ("gateup_full", 2), ("var_full", 2)])
group("gn_act", second=[("gateup_in", 1), ("gn_sq", 2), ("gn_root", 2)])
group("gn_dve", second=[("bonus_in", 1), ("y_mid", 2), ("ya_cols", 2)])
group("mla_pe", second=[("q2_full", 4), ("kv2_full", 4), ("qk2_T", 8), ("gates_full", 8), ("br2_full", 8), ("up_full", 2 * NUP)])
group("mla_act", second=[("kv2_rows", 8), ("qk2_cols_a", 4), ("gates_sig", 8)])
group("mla_dve", second=[("q2_rows", 4), ("qk2_rot", 1), ("qk2_cols_d", 4), ("merged", 4)])
group("ffn_base", second=[("up_base", 2 * NUP)])
group("ffn_gelu", second=[("up_gelu", NUP)])
group("ffn_conv", second=[("up_conv", NUP)])
group("ffn_act", second=[("up_act", NUP)])


class Signals:

    def __init__(self, nc, ctx):
        self.of = {}
        for name, phases in GROUPS.items():
            sem = ctx.enter_context(nc.semaphore(name))
            base = 0
            for i, phase in enumerate(phases):
                per, at = sum(n for _, n in phase), 0
                for signal, n in phase:
                    assert signal not in self.of, signal
                    self.of[signal] = (sem, base, per, at, n)
                    at += n
                base += per * (L if i in (1, 3) else 1)

    def __call__(self, signal):
        return self.of[signal][0]

    def at(self, signal, l, k=None):
        sem, base, per, at, n = self.of[signal]
        k = n if k is None else k
        return sem, l * per + (base + at) + k

    def prev(self, signal, l):
        sem, base, per, at, n = self.of[signal]
        assert at + n == per and base > 0
        return sem, l * per + base


class Memory:

    def __init__(self, nc):
        self.nc = nc


def allocate(nc, ctx):
    m = Memory(nc)

    def sb(name, *shape, dt=F32):
        return ctx.enter_context(nc.sbuf_tensor(name, [P, *shape], dt))

    m.ring = sb("ring", SLOTS, SLAB)
    m.x = sb("x", NT, D)
    m.xn = sb("xn", NT, D)
    m.hT = sb("hT", KD, T)
    m.con = sb("con", NCONST)
    m.par = sb("par", NPAR)
    m.mem_g = sb("mem_g", KD)
    m.stat = sb("stat", 256)
    m.cs2 = sb("cs2", 2, NT, PE_D // 2)
    m.area = sb("area", AREA)
    m.top_i = sb("top_i", CAP, dt=U32)
    m.pos_i = sb("pos_i", NT, dt=I32)
    m.ps = ctx.enter_context(nc.psum_tensor("ps", [P, 8, BANK], F32))
    m.landed = [ctx.enter_context(nc.semaphore(f"slab_landed{s}")) for s in range(SLOTS)]
    m.free = [ctx.enter_context(nc.semaphore(f"slab_free{s}")) for s in range(SLOTS)]
    m.s = Signals(nc, ctx)
    m.at, m.prev = m.s.at, m.s.prev

    def const(name):
        at, width = CONST_COLS[name]
        return m.con[:, at:at + width]

    m.const = const
    m.ident = const("ident")

    def par(cols, name):
        at, width = cols[name]
        return m.par[:, at:at + width]

    m.par1 = lambda name: par(PAR1, name)
    m.par2 = lambda name: par(PAR2, name)
    used = [0]

    def view(*shape, at=None):
        n = int(np.prod(shape))
        if at is not None:
            used[0] = at
        a = m.area[:, used[0]:used[0] + n]
        used[0] += n
        assert used[0] <= AREA, used[0]
        if len(shape) == 1:
            return a
        names = "abcd"[:len(shape)]
        return a.rearrange(f"p ({' '.join(names)}) -> p {' '.join(names)}", **dict(zip(names[1:], shape[1:])))

    m.memT = view(KD, T, at=0)
    base = used[0]
    m.ug, m.vg = view(NT, GM_W), view(NT, GM_W)
    m.raw = view(NT, 768)
    m.rot, m.kd = view(NT, HEADS_QK, HD), view(NT, NKV, 2, HD)
    m.tmp = view(2, NT * HEADS_QK * HD // 2)
    m.qT, m.kT = view(NQ // 2, T), view(NKV, T)
    m.p, m.pT = view(NQ, T), view(NQ, 2, P)
    m.merged = view(NT, 2 * GM_W)
    m.xqT, m.xkT, m.xv = view(KD, T, at=base), view(KD, T), view(NT, D)
    m.xp, m.xpT = view(NT, XH, T), view(NT, XH, T)
    m.mem_rows = view(NT, D, at=base)
    m.aff = view(NT, E, at=base)
    m.work = view(2, T)
    m.gates, m.slots = view(CAP), view(CAP)
    m.rep = view(2, 4, CAP)
    m.diag = view(E, CAP)
    m.topc = view(2, E)
    m.onehot = view(NT, E * CAP)
    m.tokT, m.gu, m.sil, m.hid = view(KD, CAP), view(BANK), view(4, 64), view(4, 2, CAP)
    m.pick, m.dn = view(T), view(2, BANK)
    m.R, m.K, m.V = view(PAIRS, T, at=0), view(PAIRS, T), view(PAIRS, T)
    m.wa, m.gg = view(T), view(T)
    m.lat = view(NT, LAT)
    after_lat = used[0]
    m.KK, m.A, m.LW, m.C, m.E1 = (view(PAIRS, T) for _ in range(5))
    m.y = m.KK
    flat = m.xn[:, :, :].rearrange("p t d -> p (t d)")
    m.sq, m.rs = (flat[:, i * D:(i + 1) * D].rearrange("p (a b) -> p a b", b=T) for i in (0, 1))
    m.arp, m.btp, m.ktp, m.vtp = view(NT, 2, P), view(NT, P), view(NT, P), view(NT, P)
    m.rb = flat[:, 0:512].rearrange("p (a t b) -> p a t b", a=2, t=NT)
    m.WU = flat[:, 512:1024].rearrange("p (t w h b) -> p t w h b", t=NT, w=2, h=2)
    m.H = flat[:, 1024:2048].rearrange("p (n b) -> p n b", b=P)
    m.btok, m.kvtok = view(NT, P), view(2, NT, P)
    m.mat = {n: view(2, NT, P) for n in ("D", "DT", "D2", "D2T", "ID", "X", "Arb", "Aak", "Ark")}
    m.G, m.S = view(NCH, P), view(NCH - 2, P)
    m.QT = m.mat["Aak"][:, 0]
    m.yaT = m.V
    m.latT = view(3, T, at=after_lat)
    m.qm, m.km, m.vm = view(NT, MH + 1, QKD), view(NT, MH, QKD), view(NT, RW)
    m.pm = view(MH, T)
    m.qmT, m.kmT = view(MH, T), view(MH, T)
    m.pmT = m.xn[:, :, :].rearrange("p t (h k b) -> p (t h) k b", k=2, b=P)
    m.o2T = m.K
    m.pe_tmp = view(4, NT * (MH + 1) * PE_D // 2)
    m.sg = view(2, KD, T, at=after_lat)
    m.m1 = view(2, BANK)
    m.mT = m.xn[:, :, :].rearrange("p a (b c) -> p (a b) c", c=T)
    m.rope_tmp = view(4, NT * PE_D // 2, at=0)
    m.act = view(NF, T, at=0)
    m.cb = view(2, 2, T)
    m.fin = view(D, at=12288)
    return m


def slab(m, slot, k, n):
    return m.ring[:, slot, 0:k * n].rearrange("p (k n) -> p k n", n=n)


def act_squares(m, act, src, junk, sums, scale, done):
    for s, j, c in zip(src, junk, sums):
        m.nc.scalar.activation(j, s, ACT.Square, scale=scale, accum_out=c).then_inc(done, 1)


def pool_rstd(m, pool, mean, eps, out, done):
    m.nc.gpsimd.tensor_tensor(out, mean, eps, ALU.add)
    pool.drain()
    m.nc.gpsimd.tensor_tensor(out, out, m.const("neg_half").to_broadcast(list(out.shape)), ALU.pow).then_inc(done, 1)


def pe_columns(m, src, full):
    for b in range(4):
        for k in range(2):
            for t in range(NT):
                ins = m.nc.tensor.transpose(m.ps[:, b, k * T + t * P:k * T + (t + 1) * P],
                                            src[:, t, (2 * b + k) * P:(2 * b + k + 1) * P], m.ident)
        ins.then_inc(full, 1)


def act_columns(m, act, dst, gain, full, base, done):
    for b in (0, 1):
        act.wait_ge(full, base + b + 1)
        for k in (2 * b, 2 * b + 1):
            m.nc.scalar.activation(dst[:, k, :], m.ps[:, b, (k % 2) * T:(k % 2 + 1) * T], ACT.Copy,
                                   scale=gain[:, k:k + 1]).then_inc(done, 1)


def dve_columns(m, dve, dst, gain, full, base, done):
    for b in (2, 3):
        dve.wait_ge(full, base + b + 1)
        for k in (2 * b, 2 * b + 1):
            m.nc.vector.tensor_scalar(dst[:, k, :], m.ps[:, b, (k % 2) * T:(k % 2 + 1) * T], gain[:, k:k + 1], None,
                                      ALU.mult).then_inc(done, 1)


def dve_scale_rows(m, dst, src, rstd, done):
    for t in range(NT):
        m.nc.vector.tensor_scalar(dst[:, t, :], src[:, t, :], rstd[:, t:t + 1], None, ALU.mult).then_inc(done, 1)


def pe_rows(m, pe, out, lhs, w, ks, k0, start, stop):
    ins = None
    for t in range(NT):
        for i, k in enumerate(ks):
            ins = m.nc.tensor.matmul(out[t], lhs[:, k, t * P:(t + 1) * P], w[:, k - k0, :],
                                     start=start and i == 0, stop=stop and i == len(ks) - 1)
    return ins


def pe_cols(m, out, w, c, rhs, ks):
    ins = None
    for i, k in enumerate(ks):
        ins = m.nc.tensor.matmul(out, w[:, k, c:c + P], rhs[:, k, :], start=i == 0, stop=i == len(ks) - 1)
    return ins


def sync_start(m, sp):
    done = m.s("inputs_loaded")
    sp.dma_start(m.con[:, :], m.d["consts"]).then_inc(done, 16)
    sp.dma_start(m.mem_g[:, :], m.d["fix"][:, 0:KD]).then_inc(done, 16)
    sp.dma_start(m.pos_i[:, :], m.d["positions"]).then_inc(done, 16)
    sp.dma_start(m.mem_rows, m.d["mem"].rearrange("b (t p) d -> p (b t) d", p=P)).then_inc(done, 16)
    sp.dma_start(m.x[:, :, :], m.d["x"].rearrange("b (t p) d -> p (b t) d", p=P)).then_inc(done, 16)
    for s in range(SLOTS):
        sp.sem_inc(m.free[s], 1)


def scalar_start(m, act):
    act.wait_ge(*m.at("inputs_loaded", 0))
    act_squares(m, act, [m.mem_rows[:, t, :] for t in range(NT)], [m.xn[:, t, :] for t in range(NT)],
                [m.stat[:, t:t + 1] for t in range(NT)], D ** -0.5, m.s("m_sq"))
    act_columns(m, act, m.memT, m.mem_g, *m.at("m_T", 0, 0), m.s("m_cols_a"))


def gpsimd_rstd(m, pool, squares, c, width, eps, done):
    pool.wait_ge(*squares)
    at = CONST_COLS["eps"][0] + eps
    pool_rstd(m, pool, m.stat[:, c:c + width], m.con[:, at:at + width], m.stat[:, 64 + c:64 + c + width], done)


def gpsimd_start(m, pool):
    gpsimd_rstd(m, pool, m.at("m_sq", 0), 0, 2, 0, m.s("m_rstd"))


def vector_start(m, dve):
    dve.wait_ge(*m.at("m_rstd", 0))
    dve_scale_rows(m, m.xn, m.mem_rows, m.stat[:, 64:66], m.s("m_xn"))
    dve_columns(m, dve, m.memT, m.mem_g, *m.at("m_T", 0, 0), m.s("m_cols_d"))
    m.nc.vector.memset(m.stat[:, 255:256], 0.0).then_inc(m.s("x_start"), 1)


def tensor_start(m, pe):
    pe.wait_ge(*m.at("m_xn", 0))
    pe_columns(m, m.xn, m.s("m_T"))


def ring_wait(m, eng, slot, held):
    eng.wait_ge(m.free[slot], held + 1)


def sync_first(m, sp, l):
    d = m.d

    def load(i, dst, src):
        g = PLAN1[i]
        ring_wait(m, sp, g.slot, l * HELD1_LAYER[g.slot] + g.held)
        sp.dma_start(dst, src).then_inc(m.landed[g.slot], 16)

    def layer(w):
        return w[bass.ds(l, 1)].rearrange("l (k p) n -> p (l k) n", p=P)

    def whole(i, w, c0, n):
        load(i, slab(m, PLAN1[i].slot, KD, n), layer(w)[:, :, c0:c0 + n])

    def half(i, w, nh, kh):
        load(i, slab(m, PLAN1[i].slot, 4, BANK), layer(w)[:, 4 * kh:4 * kh + 4, nh * BANK:(nh + 1) * BANK])

    for j in range(4):
        whole(W_IN1 + j, d["w_in"], j * BANK, min(BANK, 1792 - j * BANK))
    for j in range(4):
        half(W_OUT1 + j, d["w_out"], j // 2, j % 2)
    for j in range(2):
        whole(W_XQ + j, d["xattn_w_q"], j * BANK, BANK)
    for j in range(4):
        whole(W_XK + j, d["xattn_w_kv"], j * BANK, BANK)
    for j in range(4):
        half(W_XO + j, d["xattn_w_o"], j // 2, j % 2)
    with sp.Fori(0, E) as e:
        for s, (name, n) in enumerate((("w_gate", 0), ("w_gate", 1), ("w_up", 0), ("w_up", 1), ("w_down", 0), ("w_down", 1))):
            ring_wait(m, sp, s, l * HELD1_LAYER[s] + e + HELD1[s])
            w = d[name].rearrange("l e (k p) n -> (l e) p k n", p=P)[bass.ds(l * E + e, 1)]
            sp.dma_start(slab(m, s, KD, BANK), w[:, :, :, n * BANK:(n + 1) * BANK].rearrange("o p k n -> p (o k) n"))\
              .then_inc(m.landed[s], 16)


def landed1(m, pe, l, i):
    g = PLAN1[i]
    pe.wait_ge(m.landed[g.slot], l * LANDED1_LAYER[g.slot] + g.landed)


def tensor_first(m, pe, l):
    nc, ps, at = m.nc, m.ps, m.at
    mm = nc.tensor.matmul

    def weights(i, k=KD, n=BANK):
        landed1(m, pe, l, i)
        return slab(m, PLAN1[i].slot, k, n)

    def used(i):
        return m.free[PLAN1[i].slot]

    def columns_of(src, ready, T_full, a, dcols):
        pe.wait_ge(*at(ready, l))
        pe_columns(m, src, m.s(T_full))
        pe.wait_ge(*at(a, l))
        pe.wait_ge(*at(dcols, l))

    def into_residual(first, full):
        for j in range(4):
            w = weights(first + j, 4)
            nh, kh = j // 2, j % 2
            for t in range(NT):
                for k in range(4):
                    ins = mm(ps[:, 4 + 2 * nh + t, :], m.hT[:, 4 * kh + k, t * P:(t + 1) * P], w[:, k, :],
                             start=kh == 0 and k == 0, stop=kh == 1 and k == 3)
                if kh == 1 and t == 0:
                    ins.then_inc(m.s(full), 1)
                if kh == 0 and t == NT - 1:
                    ins.then_inc(used(first + j), 1)
            if kh == 1:
                ins.then_inc(m.s(full), 1)
                release.append(first + j)

    release = []

    def free_released(ins):
        ins.then_inc(used(release.pop()), 1)

    columns_of(m.xn, "h1_xn", "h1_T", "h1_cols_a", "h1_cols_d")
    for j in range(4):
        n = 256 if j == 3 else BANK
        w = weights(W_IN1 + j, KD, n)
        for t in range(NT):
            b = (4, 6, 0, 2)[j] + t
            for k in range(KD):
                ins = mm(ps[:, b, 0:n], m.hT[:, k, t * P:(t + 1) * P], w[:, k, :], start=k == 0, stop=k == KD - 1)
                if t == 0 and k == 0 and release:
                    free_released(ins)
            ins.then_inc(m.s("uv_full" if j < 2 else "qkv_full"), 1)
        release.append(W_IN1 + j)
    pe.wait_ge(*at("v_norm", l))
    pe.wait_ge(*at("uv_gelu", l))
    w_s = m.par1("w_s")
    for t in range(NT):
        for g in range(GM_G):
            ins = mm(ps[:, 4 + t, g * P:(g + 1) * P], w_s[:, g * P:(g + 1) * P], m.vg[:, t, g * P:(g + 1) * P],
                     start=True, stop=True)
            if release:
                free_released(ins)
        ins.then_inc(m.s("mix_full"), 1)
    pe.wait_ge(*at("qk_rot", l))
    for b in range(3):
        for i in range(2):
            for t in range(NT):
                if b < 2:
                    h = 2 * (2 * b + i)
                    src = m.rot[:, t, h:h + 2, :].rearrange("p a b -> p (a b)")
                else:
                    src = m.kd[:, t, i].rearrange("p a b -> p (a b)")
                ins = nc.tensor.transpose(ps[:, (6, 7, 0)[b], i * T + t * P:i * T + (t + 1) * P], src, m.ident)
        ins.then_inc(m.s("qk_T"), 1)
    pe.wait_ge(*at("q_cols", l))
    pe.wait_ge(*at("k_cols", l))
    for t in range(NT):
        if t == 1:
            pe.wait_ge(*at("gm_rows", l))
        for h in range(NQ):
            r = (h % 2) * HD
            ins = mm(ps[:, 4 * t + 2 * (h % 2) + h // 4, (h // 2 % 2) * T:(h // 2 % 2 + 1) * T],
                     m.qT[r:r + HD, h // 2, t * P:(t + 1) * P], m.kT[r:r + HD, h // 4, :], start=True, stop=True)
        ins.then_inc(m.s("sc_full"), 1)
    for t in range(NT):
        pe.wait_ge(*at("sc_exp", l, NQ * (t + 1)))
        for b in range(4):
            for j in (2 * b, 2 * b + 1):
                for kt in range(2):
                    ins = nc.tensor.transpose(ps[:, 4 * t + b, (j % 2) * T + kt * P:(j % 2) * T + (kt + 1) * P],
                                              m.p[:, j, kt * P:(kt + 1) * P], m.ident)
            ins.then_inc(m.s("pT_full"), 1)
        pe.wait_ge(*at("pT_a", l, 2 * (t + 1)))
        pe.wait_ge(*at("pT_d", l, 2 * (t + 1)))
        for j in range(NQ):
            h = 4 * (j // 2 % 2) + 2 * (j % 2) + j // 4
            for kt in range(2):
                c = NQ * HD + NKV * HD + (h // 4) * HD
                ins = mm(ps[:, 4 * t, h * HD:(h + 1) * HD], m.pT[:, j, kt, :], m.raw[:, kt, c:c + HD],
                         start=kt == 0, stop=kt == 1)
        ins.then_inc(m.s("at_full"), 1)
    columns_of(m.xn, "br_xn", "br_T", "br_cols_a", "br_cols_d")
    into_residual(W_OUT1, "out1_full")

    pe.wait_ge(*at("h2_xn", l))
    pe_columns(m, m.xn, m.s("h2_T"))
    pe.wait_ge(*at("h2_cols_a", l))
    pe.wait_ge(*at("h2_cols_d", l))
    for first, rhs, b0, full in ((W_XQ, m.hT, 4, "xq_full"), (W_XK, m.memT, 0, "xk_full")):
        for j in range(2):
            w = weights(first + j)
            for c in range(4):
                out = ps[:, b0 + 2 * j + c // 2, (c % 2) * T:(c % 2 + 1) * T]
                for k in range(KD):
                    ins = mm(out, w[:, k, c * P:(c + 1) * P], rhs[:, k, :], start=k == 0, stop=k == KD - 1)
                    if k == 0 and release:
                        free_released(ins)
                if c % 2:
                    ins.then_inc(m.s(full), 1)
            release.append(first + j)
    pe.wait_ge(*at("xq_cols", l))
    for j in range(2):
        w = weights(W_XV + j)
        for t in range(NT):
            for k in range(KD):
                ins = mm(ps[:, 4 + 2 * j + t, :], m.memT[:, k, t * P:(t + 1) * P], w[:, k, :], start=k == 0, stop=k == KD - 1)
                if k == 0 and release:
                    free_released(ins)
            ins.then_inc(m.s("xv_full"), 1)
        release.append(W_XV + j)
    pe.wait_ge(*at("xk_cols", l))
    for t in range(NT):
        for h in range(XH):
            for k in range(2):
                ins = mm(ps[:, 2 * t + h // 2, (h % 2) * T:(h % 2 + 1) * T], m.xqT[:, 2 * h + k, t * P:(t + 1) * P],
                         m.xkT[:, 2 * h + k, :], start=k == 0, stop=k == 1)
                if release:
                    free_released(ins)
        ins.then_inc(m.s("xs_full"), 1)
    pe.wait_ge(*at("xv_rows", l))
    pe.wait_ge(*at("xp_rows", l))
    for b in range(4):
        mt = b // 2
        for i in range(2):
            for t in range(NT):
                ins = nc.tensor.transpose(ps[:, 4 + b, i * T + t * P:i * T + (t + 1) * P],
                                          m.xp[:, t, 2 * (b % 2) + i, mt * P:(mt + 1) * P], m.ident)
        ins.then_inc(m.s("xpT_full"), 1)
    pe.wait_ge(*at("xpT_a", l))
    pe.wait_ge(*at("xpT_d", l))
    for c in range(KD):
        h = c // 2
        for mt in range(2):
            ins = mm(ps[:, c // 2, (c % 2) * T:(c % 2 + 1) * T], m.xv[:, mt, c * P:(c + 1) * P], m.xpT[:, mt, h, :],
                     start=mt == 0, stop=mt == 1)
        if c % 2:
            ins.then_inc(m.s("xo_full"), 1)
    pe.wait_ge(*at("xo_cols_a", l))
    pe.wait_ge(*at("xo_cols_d", l))
    into_residual(W_XO, "out2_full")
    tensor_experts(m, pe, l, release, free_released, columns_of)


def tensor_experts(m, pe, l, release, free_released, columns_of):
    nc, ps, at = m.nc, m.ps, m.at
    mm = nc.tensor.matmul
    columns_of(m.xn, "h3_xn", "h3_T", "h3_cols_a", "h3_cols_d")
    router = m.par1("router").rearrange("p (k e) -> p k e", e=E)
    for t in range(NT):
        for k in range(KD):
            ins = mm(ps[:, 4 + t, 0:E], m.hT[:, k, t * P:(t + 1) * P], router[:, k, :], start=k == 0, stop=k == KD - 1)
            if release:
                free_released(ins)
        ins.then_inc(m.s("router_full"), 1)
    pe.wait_ge(*at("aff_rows", l))
    for t in range(NT):
        ins = nc.tensor.transpose(ps[0:E, 6, t * P:(t + 1) * P], m.aff[:, t, :], m.ident)
    ins.then_inc(m.s("aff_T"), 1)
    pe.wait_ge(*at("top_found", l))
    mm(ps[:, 7, 0:E * CAP], m.const("ones")[0:E, :], m.diag[0:E].rearrange("p e c -> p (e c)"), start=True, stop=True)
    for i in range(2):
        ins = nc.tensor.transpose(ps[:, 6, i * E:(i + 1) * E], m.rep[0:E, i].rearrange("p g c -> p (g c)"), m.ident[0:E, 0:E])
    ins.then_inc(m.s("top_T"), 1)
    pe.wait_ge(*at("onehot", l))
    pe.wait_ge(*at("router_exp", l))
    for nh in range(2):
        for t in range(NT):
            mm(ps[:, 4 + 2 * nh + t, :], m.ident, m.x[:, t, nh * BANK:(nh + 1) * BANK], start=True, stop=False,
               skip_group_check=True)
    w = [slab(m, s, KD, BANK) for s in range(SLOTS)]
    with pe.Fori(0, E) as e:
        n = e + l * E + 1

        def slab_landed(s):
            pe.wait_ge(m.landed[s], l * LANDED1_LAYER[s] + LANDED1[s] + 16 + e * 16)

        for k in range(KD):
            for t in range(NT):
                ins = mm(ps[:, 0, k * CAP:(k + 1) * CAP], m.xn[:, t, k * P:(k + 1) * P], m.onehot[:, t, bass.ds(e * CAP, CAP)],
                         start=t == 0, stop=t == NT - 1)
        ins.then_inc(m.s("tok_full"), 1)
        pe.wait_ge(m.s("tok_cols"), n)
        for k in range(KD):
            for g in range(4):
                if k == 0:
                    slab_landed(g)
                ins = mm(ps[32 * g:32 * g + CAP, 1, :], m.tokT[:, k, :], w[g][:, k, :], start=k == 0, stop=k == KD - 1)
                if k == KD - 1:
                    ins.then_inc(m.free[g] if g < 3 else m.s("gu_full"), 1)
        pe.wait_ge(m.s("gu_rows"), n)
        for c in range(4):
            ins = nc.tensor.transpose(ps[:, 0, c * P:(c + 1) * P], m.gu[:, c * P:(c + 1) * P], m.ident)
            if c == 0:
                ins.then_inc(m.free[3], 1)
        ins.then_inc(m.s("gu_T"), 1)
        pe.wait_ge(m.s("hid_cols"), n)
        for nh in range(2):
            slab_landed(4 + nh)
            for k in range(KD):
                c, half = k % 4, k // 4
                ins = mm(ps[32 * c:32 * c + CAP, 2 + nh, :], m.hid[:, c, half, :], w[4 + nh][:, k, :],
                         start=half == 0, stop=half == 1)
                if nh == 1 and k == 0:
                    ins.then_inc(m.free[4], 1)
            ins.then_inc(m.s("dn_full"), 1)
        pe.wait_ge(m.s("pick"), n)
        for nh in range(2):
            pe.wait_ge(m.s("dn_rows_a" if nh == 0 else "dn_rows_d"), n)
            for t in range(NT):
                ins = mm(ps[:, 4 + 2 * nh + t, :], m.pick[:, t * P:(t + 1) * P], m.dn[:, nh, :], start=False, stop=True,
                         skip_group_check=True)
                if nh == 0 and t == 0:
                    ins.then_inc(m.free[5], 1)
        ins.then_inc(m.s("acc_full"), 1)


def norm_squares(m, act, x_ready, done):
    act.wait_ge(*x_ready)
    act_squares(m, act, [m.x[:, t, :] for t in range(NT)], [m.xn[:, t, :] for t in range(NT)],
                [m.stat[:, t:t + 1] for t in range(NT)], D ** -0.5, done)


def two(bank):
    return bank.rearrange("p (a b) -> p a b", b=T)


S_MAX, S_SUM, S_INV = 128, 144, 160
S_XMAX, S_XSUM, S_XINV = 176, 184, 192
S_RMAX, S_RSUM, S_RINV = 200, 202, 204


def scalar_first(m, act, l):
    nc, ps, at, s = m.nc, m.ps, m.at, m.s
    go = nc.scalar.activation
    col = lambda c: m.stat[:, c:c + 1]
    norm_squares(m, act, m.prev("x_routed", l), s("h1_sq"))
    act.wait_ge(*at("par1_loaded", l))
    act_columns(m, act, m.hT, m.par1("mix_g"), *at("h1_T", l, 0), s("h1_cols_a"))
    for i in range(4):
        act.wait_ge(*at("uv_full", l, i + 1))
        go((m.ug, m.vg)[i // 2][:, i % 2, :], ps[:, 4 + i, :], ACT.Gelu_apprx_tanh).then_inc(s("uv_gelu"), 1)
    act.wait_ge(*at("uv_gelu", l))
    act_squares(m, act, [m.vg[:, t, :] for t in range(NT)], [m.xn[:, t, 0:GM_W] for t in range(NT)],
                [col(4 + t) for t in range(NT)], GM_W ** -0.5, s("v_sq"))
    for b in range(2):
        act.wait_ge(*at("qk_T", l, b + 1))
        go(m.qT[:, 2 * b:2 * b + 2, :], two(ps[:, 6 + b, :]), ACT.Copy).then_inc(s("q_cols"), 1)
    for t in range(NT):
        act.wait_ge(*at("sc_max", l, t + 1))
        if t:
            act.wait_ge(*at("pT_full", l, 4 * t))
        for j in range(NQ):
            h = 4 * (j // 2 % 2) + 2 * (j % 2) + j // 4
            go(m.p[:, j, :], two(ps[:, 4 * t + j // 2, :])[:, j % 2, :], ACT.Exp, bias=col(S_MAX + NQ * t + j),
               scale=HD ** 0.5, accum_out=col(S_SUM + NQ * t + h)).then_inc(s("sc_exp"), 1)
        if t:
            act.wait_ge(*at("at_full", l, t))
        for b in range(2):
            act.wait_ge(*at("pT_full", l, 4 * t + b + 1))
            go(m.pT[:, 2 * b:2 * b + 2], ps[:, 4 * t + b, :].rearrange("p (a k b) -> p a k b", a=2, b=P), ACT.Copy)\
                .then_inc(s("pT_a"), 1)
    for t in range(NT):
        act.wait_ge(*at("at_rows", l, t + 1))
        for br in range(2):
            part = slice(br * GM_W, (br + 1) * GM_W)
            go(m.xn[:, t, part], m.merged[:, t, part], ACT.Square, scale=GM_W ** -0.5,
               accum_out=col(6 + 2 * t + br)).then_inc(s("br_sq"), 1)
    act_columns(m, act, m.hT, m.par1("branch_g"), *at("br_T", l, 0), s("br_cols_a"))
    norm_squares(m, act, at("x_mixed", l), s("h2_sq"))
    act_columns(m, act, m.hT, m.par1("x_g"), *at("h2_T", l, 0), s("h2_cols_a"))
    for b in range(4):
        act.wait_ge(*at("xq_full", l, b + 1))
        go(m.xqT[:, 2 * b:2 * b + 2, :], two(ps[:, 4 + b, :]), ACT.Copy).then_inc(s("xq_cols"), 1)
    for i in range(4):
        act.wait_ge(*at("xv_full", l, i + 1))
        go(m.xv[:, i % 2, (i // 2) * BANK:(i // 2 + 1) * BANK], ps[:, 4 + i, :], ACT.Copy).then_inc(s("xv_rows"), 1)
    for t in range(NT):
        act.wait_ge(*at("xs_max", l, t + 1))
        for h in range(XH):
            go(m.xp[:, t, h, :], two(ps[:, 2 * t + h // 2, :])[:, h % 2, :], ACT.Exp, bias=col(S_XMAX + XH * t + h),
               scale=XD ** -0.5, accum_out=col(S_XSUM + XH * t + h)).then_inc(s("xs_exp"), 1)
    for b in range(2):
        act.wait_ge(*at("xpT_full", l, b + 1))
        go(m.xpT[:, 0, 2 * b:2 * b + 2, :], two(ps[:, 4 + b, :]), ACT.Copy).then_inc(s("xpT_a"), 1)
    for b in range(2):
        act.wait_ge(*at("xo_full", l, b + 1))
        go(m.hT[:, 2 * b:2 * b + 2, :], two(ps[:, b, :]), ACT.Copy).then_inc(s("xo_cols_a"), 1)
    norm_squares(m, act, at("x_attended", l), s("h3_sq"))
    act_columns(m, act, m.hT, m.par1("ffn_g"), *at("h3_T", l, 0), s("h3_cols_a"))
    act.wait_ge(*at("router_max", l))
    for t in range(NT):
        go(m.aff[:, t, :], ps[:, 4 + t, 0:E], ACT.Exp, bias=col(S_RMAX + t), accum_out=col(S_RSUM + t)).then_inc(s("router_exp"), 1)
    gate = ps[:, 0, :].rearrange("p (c n) -> p c n", n=P)[:, :, 0:2 * CAP]
    with act.Fori(0, E) as e:
        n = e + l * E + 1
        act.wait_ge(s("gu_full"), n)
        go(m.gu, ps[:, 1, :], ACT.Copy).then_inc(s("gu_rows"), 1)
        act.wait_ge(s("gu_T"), n)
        go(m.sil, gate, ACT.Silu).then_inc(s("gate_silu"), 1)
        act.wait_ge(s("dn_full"), 2 * n - 1)
        go(m.dn[:, 0, :], ps[:, 2, :], ACT.Copy).then_inc(s("dn_rows_a"), 1)


def gpsimd_first(m, pool, l):
    at, s = m.at, m.s
    pool.wait_ge(*m.prev("x_routed", l))
    pool.dma_start(m.par[:, 0:NPAR1], m.d["par1"][bass.ds(l, 1)].rearrange("l p n -> p (l n)")).then_inc(s("par1_loaded"), 16)
    gpsimd_rstd(m, pool, at("h1_sq", l), 0, 2, 0, s("h1_rstd"))
    gpsimd_rstd(m, pool, at("v_sq", l), 4, 2, 0, s("v_rstd"))
    gpsimd_rstd(m, pool, at("qk_ss", l), 32, NT * HEADS_QK, 32, s("qk_rstd"))
    gpsimd_rstd(m, pool, at("br_sq", l), 6, 4, 0, s("br_rstd"))
    gpsimd_rstd(m, pool, at("h2_sq", l), 0, 2, 0, s("h2_rstd"))
    gpsimd_rstd(m, pool, at("h3_sq", l), 0, 2, 0, s("h3_rstd"))
    pool.dma_start(m.fin, m.d["fix"][:, KD:KD + D]).then_inc(s("fin1_loaded"), 16)


def add_into_x(m, dve, full, base, done):
    for i in range(4):
        nh, t = i // 2, i % 2
        dve.wait_ge(full, base + i + 1)
        xs = m.x[:, t, nh * BANK:(nh + 1) * BANK]
        m.nc.vector.tensor_tensor(xs, xs, m.ps[:, 4 + i, :], ALU.add).then_inc(done, 1)


def bc(ap, n):
    return ap.unsqueeze(len(ap.shape)).to_broadcast([*ap.shape, n])


def vector_norm(m, dve, l, name, gain):
    dve.wait_ge(*m.at(name + "_rstd", l))
    dve_scale_rows(m, m.xn, m.x, m.stat[:, 64:66], m.s(name + "_xn"))
    dve_columns(m, dve, m.hT, gain, *m.at(name + "_T", l, 0), m.s(name + "_cols_d"))


def vector_first(m, dve, l):
    vector_mix(m, dve, l)
    vector_memory(m, dve, l)
    vector_route(m, dve, l)
    vector_experts(m, dve, l)


def vector_mix(m, dve, l):
    v, ps, at, s = m.nc.vector, m.ps, m.at, m.s
    dve.wait_ge(*at("par1_loaded", l))
    vector_norm(m, dve, l, "h1", m.par1("mix_g"))
    dve.wait_ge(*at("v_rstd", l))
    for t in range(NT):
        v.scalar_tensor_tensor(m.vg[:, t, :], m.vg[:, t, :], m.stat[:, 68 + t:69 + t], m.par1("v_g"), ALU.mult, ALU.mult)\
            .then_inc(s("v_norm"), 1)
    for i in range(4):
        dve.wait_ge(*at("qkv_full", l, i + 1))
        if i < 2:
            v.tensor_copy(m.raw[:, i, 0:BANK], ps[:, i, :]).then_inc(s("qkv_rows"), 1)
        else:
            v.tensor_copy(m.raw[:, i - 2, BANK:768], ps[:, i, 0:256]).then_inc(s("qkv_rows"), 1)
    qk = m.raw[:, :, 0:HEADS_QK * HD]
    heads = m.raw.rearrange("p t (h d) -> p t h d", d=HD)[:, :, 0:HEADS_QK, :]
    dve.wait_ge(*at("qkv_rows", l))
    v.tensor_tensor(m.rot.rearrange("p t h d -> p t (h d)"), qk, qk, ALU.mult)
    dve.drain()
    ss = m.stat[:, 32:32 + NT * HEADS_QK].rearrange("p (t h) -> p t h", t=NT)
    v.tensor_reduce(ss, m.rot, axis=AX.X, op=ALU.add).then_inc(s("qk_ss"), 1)
    dve.wait_ge(*at("qk_rstd", l))
    rstd = m.stat[:, 96:96 + NT * HEADS_QK].rearrange("p (t h) -> p t h", t=NT)
    v.tensor_tensor(heads, heads, bc(rstd, HD), ALU.mult)
    dve.drain()
    v.tensor_tensor(qk, qk, m.par1("qk_g").unsqueeze(1).to_broadcast([P, NT, HEADS_QK * HD]), ALU.mult)
    dve.drain()
    pairs = m.raw.rearrange("p t (h i two) -> p t h i two", i=HD // 2, two=2)[:, :, 0:HEADS_QK]
    rot = m.rot.rearrange("p t h (i two) -> p t h i two", two=2)
    cos, sin = (m.const(n).rearrange("p (t i) -> p t i", t=NT) for n in ("cos1", "sin1"))
    t0, t1 = (m.tmp[:, i].rearrange("p (t h i) -> p t h i", t=NT, h=HEADS_QK) for i in range(2))
    for t in range(NT):
        c, sn = (a[:, t].unsqueeze(1).to_broadcast([P, HEADS_QK, HD // 2]) for a in (cos, sin))
        v.tensor_tensor(rot[:, t, :, :, 0], pairs[:, t, :, :, 0], c, ALU.mult)
        v.tensor_tensor(rot[:, t, :, :, 1], pairs[:, t, :, :, 0], sn, ALU.mult)
        v.tensor_tensor(t0[:, t], pairs[:, t, :, :, 1], sn, ALU.mult)
        v.tensor_tensor(t1[:, t], pairs[:, t, :, :, 1], c, ALU.mult)
    dve.drain()
    for t in range(NT):
        v.tensor_tensor(rot[:, t, :, :, 0], rot[:, t, :, :, 0], t0[:, t], ALU.subtract)
        v.tensor_tensor(rot[:, t, :, :, 1], rot[:, t, :, :, 1], t1[:, t], ALU.add)
    dve.drain()
    for t in range(NT):
        ins = v.tensor_copy(m.kd[:, t], m.rot[:, t, NQ:, :].unsqueeze(2).to_broadcast([P, NKV, 2, HD]))
    ins.then_inc(s("qk_rot"), 1)
    dve.wait_ge(*at("qk_T", l))
    v.tensor_copy(m.kT, two(ps[:, 0, :])).then_inc(s("k_cols"), 1)
    for t in range(NT):
        dve.wait_ge(*at("mix_full", l, t + 1))
        for g in range(GM_G):
            part = slice(g * P, (g + 1) * P)
            v.scalar_tensor_tensor(m.merged[:, t, part], ps[:, 4 + t, part], m.par1("b_s")[:, g:g + 1], m.ug[:, t, part],
                                   ALU.add, ALU.mult).then_inc(s("gm_rows"), 1)
    for t in range(NT):
        dve.wait_ge(*at("sc_full", l, t + 1))
        mx = m.stat[:, S_MAX + NQ * t:S_MAX + NQ * (t + 1)]
        v.tensor_reduce(mx, ps[:, 4 * t:4 * t + 4, :].rearrange("p b (j n) -> p (b j) n", n=T), axis=AX.X, op=ALU.max)
        dve.drain()
        v.tensor_scalar(mx, mx, -HD ** 0.5, None, ALU.mult).then_inc(s("sc_max"), 1)
    for t in range(NT):
        if t:
            dve.wait_ge(*at("at_full", l, t))
        for b in (2, 3):
            dve.wait_ge(*at("pT_full", l, 4 * t + b + 1))
            v.tensor_copy(m.pT[:, 2 * b:2 * b + 2], ps[:, 4 * t + b, :].rearrange("p (a k b) -> p a k b", a=2, b=P))\
                .then_inc(s("pT_d"), 1)
        inv = m.stat[:, S_INV + NQ * t:S_INV + NQ * (t + 1)]
        dve.wait_ge(*at("sc_exp", l, NQ * (t + 1)))
        v.reciprocal(inv, m.stat[:, S_SUM + NQ * t:S_SUM + NQ * (t + 1)])
        dve.drain()
        dve.wait_ge(*at("at_full", l, t + 1))
        v.tensor_tensor(m.merged[:, t, GM_W:].rearrange("p (h d) -> p h d", d=HD),
                        ps[:, 4 * t, :].rearrange("p (h d) -> p h d", d=HD), bc(inv, HD), ALU.mult).then_inc(s("at_rows"), 1)
    dve.wait_ge(*at("br_rstd", l))
    for t in range(NT):
        for br in range(2):
            part = slice(br * GM_W, (br + 1) * GM_W)
            c = 70 + 2 * t + br
            v.tensor_scalar(m.xn[:, t, part], m.merged[:, t, part], m.stat[:, c:c + 1], None, ALU.mult).then_inc(s("br_xn"), 1)
    dve_columns(m, dve, m.hT, m.par1("branch_g"), *at("br_T", l, 0), s("br_cols_d"))
    add_into_x(m, dve, *at("out1_full", l, 0), s("x_mixed"))


def vector_memory(m, dve, l):
    v, ps, at, s = m.nc.vector, m.ps, m.at, m.s
    vector_norm(m, dve, l, "h2", m.par1("x_g"))
    for b in range(4):
        dve.wait_ge(*at("xk_full", l, b + 1))
        v.tensor_copy(m.xkT[:, 2 * b:2 * b + 2, :], two(ps[:, b, :])).then_inc(s("xk_cols"), 1)
    for t in range(NT):
        dve.wait_ge(*at("xs_full", l, t + 1))
        mx = m.stat[:, S_XMAX + XH * t:S_XMAX + XH * (t + 1)]
        v.tensor_reduce(mx, ps[:, 2 * t:2 * t + 2, :].rearrange("p b (j n) -> p (b j) n", n=T), axis=AX.X, op=ALU.max)
        dve.drain()
        v.tensor_scalar(mx, mx, -XD ** -0.5, None, ALU.mult).then_inc(s("xs_max"), 1)
    for t in range(NT):
        dve.wait_ge(*at("xs_exp", l, XH * (t + 1)))
        inv = m.stat[:, S_XINV + XH * t:S_XINV + XH * (t + 1)]
        v.reciprocal(inv, m.stat[:, S_XSUM + XH * t:S_XSUM + XH * (t + 1)])
        dve.drain()
        v.tensor_tensor(m.xp[:, t], m.xp[:, t], bc(inv, T), ALU.mult).then_inc(s("xp_rows"), 1)
    for b in range(2):
        dve.wait_ge(*at("xpT_full", l, b + 3))
        v.tensor_copy(m.xpT[:, 1, 2 * b:2 * b + 2, :], two(ps[:, 6 + b, :])).then_inc(s("xpT_d"), 1)
    for b in (2, 3):
        dve.wait_ge(*at("xo_full", l, b + 1))
        v.tensor_copy(m.hT[:, 2 * b:2 * b + 2, :], two(ps[:, b, :])).then_inc(s("xo_cols_d"), 1)
    add_into_x(m, dve, *at("out2_full", l, 0), s("x_attended"))


def vector_route(m, dve, l):
    v, ps, at, s = m.nc.vector, m.ps, m.at, m.s
    vector_norm(m, dve, l, "h3", m.par1("ffn_g"))
    dve.wait_ge(*at("router_full", l))
    mx = m.stat[:, S_RMAX:S_RMAX + NT]
    v.tensor_reduce(mx, ps[:, 4:6, 0:E], axis=AX.X, op=ALU.max)
    dve.drain()
    v.tensor_scalar(mx, mx, -1.0, None, ALU.mult).then_inc(s("router_max"), 1)
    dve.wait_ge(*at("router_exp", l))
    inv = m.stat[:, S_RINV:S_RINV + NT]
    v.reciprocal(inv, m.stat[:, S_RSUM:S_RSUM + NT])
    dve.drain()
    v.tensor_tensor(m.aff, m.aff, bc(inv, E), ALU.mult).then_inc(s("aff_rows"), 1)
    dve.wait_ge(*at("aff_T", l))
    v.tensor_copy(m.work[0:E, 0, :], ps[0:E, 6, 0:T])
    dve.drain()
    for r in range(CAP // 8):
        best, work = m.gates[0:E, 8 * r:8 * r + 8], m.work[0:E, r % 2, :]
        v.max(best, work)
        dve.drain()
        v.max_index(m.top_i[0:E, 8 * r:8 * r + 8], best, work)
        v.match_replace(m.work[0:E, 1 - r % 2, :], best, work, -1.0)
        dve.drain()
    slots, gates = m.slots[0:E], m.gates[0:E]
    v.tensor_copy(slots, m.top_i[0:E, :])
    dve.drain()
    v.tensor_copy(m.rep[0:E, 0], slots.unsqueeze(1).to_broadcast([E, 4, CAP]))
    v.tensor_copy(m.rep[0:E, 1], gates.unsqueeze(1).to_broadcast([E, 4, CAP]))
    v.tensor_tensor(m.diag[0:E], slots.unsqueeze(1).to_broadcast([E, E, CAP]), bc(m.const("expert_diag")[0:E, :], CAP),
                    ALU.mult).then_inc(s("top_found"), 1)
    dve.wait_ge(*at("top_T", l))
    v.tensor_copy(m.topc, ps[:, 6, 0:2 * E].rearrange("p (i e) -> p i e", e=E)).then_inc(s("onehot"), 1)
    for t in range(NT):
        v.tensor_scalar(m.onehot[:, t, :], ps[:, 7, :], m.const("iota_col")[:, t:t + 1], None, ALU.is_equal)\
            .then_inc(s("onehot"), 1)
    dve.drain()


def vector_experts(m, dve, l):
    v, ps, at, s = m.nc.vector, m.ps, m.at, m.s
    up = ps[:, 0, :].rearrange("p (c n) -> p c n", n=P)[:, :, 2 * CAP:]
    with dve.Fori(0, E) as e:
        n = e + l * E + 1
        dve.wait_ge(s("tok_full"), n)
        v.tensor_tensor(m.tokT, ps[:, 0, 0:KD * CAP].rearrange("p (k c) -> p k c", c=CAP), bc(m.par1("ffn_g"), CAP), ALU.mult)\
            .then_inc(s("tok_cols"), 1)
        v.tensor_scalar(m.pick, m.const("iota_row"), m.topc[:, 0, bass.ds(e, 1)], m.topc[:, 1, bass.ds(e, 1)],
                        ALU.is_equal, ALU.mult).then_inc(s("pick"), 1)
        dve.wait_ge(s("gate_silu"), n)
        v.tensor_tensor(m.hid.rearrange("p c h n -> p c (h n)"), m.sil, up, ALU.mult).then_inc(s("hid_cols"), 1)
        dve.wait_ge(s("dn_full"), 2 * n)
        v.tensor_copy(m.dn[:, 1, :], ps[:, 3, :]).then_inc(s("dn_rows_d"), 1)
    dve.wait_ge(*at("acc_full", l))
    for i in range(4):
        nh, t = i // 2, i % 2
        v.tensor_copy(m.x[:, t, nh * BANK:(nh + 1) * BANK], ps[:, 4 + i, :]).then_inc(s("x_routed"), 1)


def vector_between(m, dve):
    dve.wait_ge(*m.at("fin1_loaded", L - 1))
    dve.wait_ge(*m.at("f1_rstd", 0))
    for t in range(NT):
        m.nc.vector.scalar_tensor_tensor(m.x[:, t, :], m.x[:, t, :], m.stat[:, 64 + t:65 + t], m.fin, ALU.mult, ALU.mult)\
            .then_inc(m.s("x_first"), 1)


def scalar_between(m, act):
    norm_squares(m, act, m.prev("x_routed", L), m.s("f1_sq"))


def gpsimd_between(m, pool):
    gpsimd_rstd(m, pool, m.at("f1_sq", 0), 0, 2, 0, m.s("f1_rstd"))


def sync_second(m, sp, l):
    d = m.d
    after_first = [L * n for n in HELD1_LAYER]

    def free(i):
        g = PLAN2[i]
        ring_wait(m, sp, g.slot, l * HELD2[g.slot] + (after_first[g.slot] + g.held))

    def load(i, dst, src):
        sp.dma_start(dst, src).then_inc(m.landed[PLAN2[i].slot], 16)

    def layer(name):
        return d[name][bass.ds(l, 1)].rearrange("l (k p) n -> p (l k) n", p=P)

    def whole(i, name, c0, k=KD, n=BANK, k0=0):
        free(i)
        load(i, slab(m, PLAN2[i].slot, k, n), layer(name)[:, k0:k0 + k, c0:c0 + n])

    lat0 = SHIFT_TILES * P + QL
    for j in range(4):
        whole(W_IN2 + j, "w_in_2", j * BANK)
    free(W_LAT)
    keys, kv_up, q_up = lat_slab(m)
    load(W_LAT, keys, layer("w_in_2")[:, :, lat0:lat0 + KVL + PE_D])
    load(W_LAT, kv_up, layer("w_kv_up_2"))
    load(W_LAT, q_up, layer("w_q_up_2"))
    for j in range(4):
        whole(W_GATES + j, "w_in_2", SHIFT_TILES * P + LAT + j * BANK)
    whole(W_ORW, "w_out_rwkv_2", 0, k=4, n=D)
    whole(W_OMLA, "w_out_mla_2", 0, k=4, n=D)
    for j in range(2):
        whole(W_OUT2 + j, "w_out_2", j * BANK)
    for j in range(NUP):
        i = W_UP + j
        free(i)
        w = layer("w_ffn_up_2")
        for part in range(2):
            load(i, up_slab(m, i)[:, part], w[:, :, part * FFN + j * T:part * FFN + (j + 1) * T])
    for j in range(6):
        whole(W_DN + j, "w_ffn_down_2", 0, k=min(4, NF - 4 * j), n=D, k0=4 * j)


def lat_slab(m):
    r = m.ring[:, PLAN2[W_LAT].slot]
    a = KD * (KVL + PE_D)
    b = a + MH * 2 * NOPE
    return (r[:, 0:a].rearrange("p (k n) -> p k n", k=KD), r[:, a:b].unsqueeze(1),
            r[:, b:b + 2 * MH * QKD].rearrange("p (k n) -> p k n", k=2))


def up_slab(m, i):
    return m.ring[:, PLAN2[i].slot].rearrange("p (g k n) -> p g k n", g=2, k=KD)


def tensor_second(m, pe, l):
    nc, ps, at, s = m.nc, m.ps, m.at, m.s
    mm = nc.tensor.matmul
    release = []

    def landed(i):
        g = PLAN2[i]
        pe.wait_ge(m.landed[g.slot], l * LANDED2[g.slot] + (L * LANDED1_LAYER[g.slot] + g.landed))

    def weights(i, k=KD, n=BANK):
        landed(i)
        return slab(m, PLAN2[i].slot, k, n)

    def used(i):
        return m.free[PLAN2[i].slot]

    def free_released(ins):
        if release:
            ins.then_inc(used(release.pop()), 1)

    def tile_products(out, w, c, rhs, ks):
        for i, k in enumerate(ks):
            ins = mm(out, w[:, k, c:c + P], rhs[:, k, :], start=i == 0, stop=i == len(ks) - 1)
            if i == 0:
                free_released(ins)
        return ins

    def norm_columns(name):
        pe.wait_ge(*at(name + "_xn", l))
        pe_columns(m, m.xn, s(name + "_T"))
        pe.wait_ge(*at(name + "_cols_a", l))
        pe.wait_ge(*at(name + "_cols_d", l))

    norm_columns("n1")
    for j in range(4):
        w = weights(W_IN2 + j)
        for c in range(4 if j < 3 else 2):
            i = 4 * j + c
            ins = tile_products(half_bank(m, (4, 5, 6, 7, 0, 1, 2)[i // 2], i % 2), w, c * P, m.hT, range(KD))
            if i % 2:
                ins.then_inc(s("rw_full"), 1)
        if j < 3:
            release.append(W_IN2 + j)
    keys = lat_slab(m)[0]
    landed(W_LAT)
    pe.wait_ge(*at("rw_cols", l, 2))
    for t in range(NT):
        for part, w_part, c0 in ((slice(0, QL), w, QL), (slice(QL, LAT), keys, 0)):
            for k in range(KD):
                ins = mm(ps[:, 3 + t, part], m.hT[:, k, t * P:(t + 1) * P], w_part[:, k, c0:c0 + part.stop - part.start],
                         start=k == 0, stop=k == KD - 1)
                if k == 0 and t == 0:
                    free_released(ins)
        ins.then_inc(s("lat_full"), 1)
    release.append(W_IN2 + 3)
    pe.wait_ge(*at("lora_in", l))
    pe.wait_ge(*at("rw_cols", l))
    up = m.par2("lora_up")
    for b in range(4):
        rows = slice(64 * (b // 2), 64 * (b // 2) + 64)
        for i in range(2):
            tile = 2 * (b % 2) + i
            ins = mm(half_bank(m, (5, 6, 7, 0)[b], i), up[rows, tile * P:(tile + 1) * P], m.wa[rows, :], start=True, stop=True)
            if i == 0:
                free_released(ins)
        ins.then_inc(s("lora_full"), 1)
    pe.wait_ge(*at("kk_sq", l))
    for b in range(2):
        mm(ps[:, 1 + b, :], m.const("head_sum"), m.sq[:, 2 * b:2 * b + 2, :], start=True, stop=True).then_inc(s("kk_full"), 1)
    with pe.Fori(0, PAIRS) as p:
        tensor_pair(m, pe, l, p)
    tensor_rwkv_out(m, pe, l)
    tensor_mla(m, pe, l, used)
    for j in range(4):
        w = weights(W_GATES + j)
        if j == 0:
            pe.wait_ge(*at("o2_cols", l))
        for c in range(4):
            ins = tile_products(half_bank(m, 2 * j + c // 2, c % 2), w, c * P, m.hT, range(KD))
            if c % 2:
                ins.then_inc(s("gates_full"), 1)
        release.append(W_GATES + j)
    pe.wait_ge(*at("ya_cols", l))
    for j, src in ((0, m.yaT), (1, m.o2T)):
        w = weights((W_ORW, W_OMLA)[j], 4, D)
        for i in range(KD):
            if i % 2 == 0:
                pe.wait_ge(*at("gates_sig", l, 4 * j + i // 2 + 1))
            ins = tile_products(half_bank(m, 4 * j + i // 2, i % 2), w, i * P, src, range(4))
            if i % 2:
                ins.then_inc(s("br2_full"), 1)
        release.append((W_ORW, W_OMLA)[j])
    pe.wait_ge(*at("merged", l))
    for nh in range(2):
        w = weights(W_OUT2 + nh)
        for t in range(NT):
            for k in range(KD):
                ins = mm(ps[:, 4 + 2 * nh + t, :], m.mT[:, k, t * P:(t + 1) * P], w[:, k, :], start=k == 0, stop=k == KD - 1)
                if k == 0:
                    free_released(ins)
            ins.then_inc(s("out3_full"), 1)
        release.append(W_OUT2 + nh)
    norm_columns("n2")
    for j in range(NUP):
        landed(W_UP + j)
        w = up_slab(m, W_UP + j)
        if j >= 4:
            pe.wait_ge(*at("up_act", l, j - 3))
        for part in range(2):
            for c in range(2):
                ins = tile_products(half_bank(m, (2 * j + part) % 8, c), w[:, part], c * P, m.hT, range(KD))
            ins.then_inc(s("up_full"), 1)
        release.append(W_UP + j)
    pe.wait_ge(*at("up_act", l))
    for j in range(6):
        n = min(4, NF - 4 * j)
        w = weights(W_DN + j, n, D)
        for b in range(4):
            nh, t = b // 2, b % 2
            for i in range(n):
                k = 4 * j + i
                ins = mm(ps[:, 4 + b, :], m.act[:, k, t * P:(t + 1) * P], w[:, i, nh * BANK:(nh + 1) * BANK],
                         start=k == 0, stop=k == NF - 1)
                if i == 0:
                    free_released(ins)
            if j == 5:
                ins.then_inc(s("down_full"), 1)
        if j < 5:
            ins.then_inc(used(W_DN + j), 1)
    mm(ps[:, 0, 0:32], m.ident, m.ident[:, 0:32], start=True, stop=True).then_inc(used(W_DN + 5), 1)


def half_bank(m, b, i):
    return m.ps[:, b, i * T:(i + 1) * T]


def tensor_pair(m, pe, l, p):
    nc, ps, s = m.nc, m.ps, m.s
    mm = nc.tensor.matmul
    M = m.mat
    count = pair_counter(m, l, p)
    units = [(h, t) for h in range(2) for t in range(NT)]

    def unit(b, h, t):
        return ps[:, b, (2 * h + t) * P:(2 * h + t + 1) * P]

    def products(b, lhs, rhs):
        for h, t in units:
            ins = mm(unit(b, h, t), lhs[:, h, t, :], rhs[:, h, t, :], start=True, stop=True)
        ins.then_inc(s("inv_full"), 1)

    pe.wait_ge(*count("pair_in", 5))
    for b, pair in ((0, (m.arp[:, :, 0, :], m.btp)), (1, (m.ktp, m.vtp))):
        for i, src in enumerate(pair):
            for t in range(NT):
                ins = nc.tensor.transpose(ps[:, b, i * T + t * P:i * T + (t + 1) * P], src[:, t, :], m.ident)
        ins.then_inc(s("tok_T"), 1)
    for b, lhs in ((6, None), (2, m.btp), (4, m.ktp)):
        for t in range(NT):
            for h in range(2):
                r = slice(h * HD, (h + 1) * HD)
                if lhs is None:
                    ins = mm(ps[:, b + h, t * P:(t + 1) * P], m.arp[r, t, 0, :], m.btp[r, t, :], start=True, stop=True)
                else:
                    ins = mm(ps[:, b + h, t * T:(t + 1) * T], lhs[r, t, :], m.arp[r, t].rearrange("p a b -> p (a b)"),
                             start=True, stop=True)
        ins.then_inc(s("prod_full"), 1)
    pe.wait_ge(*count("prod_masked", 2))
    pe.wait_ge(*count("tok_a", 1))
    pe.wait_ge(*count("tok_d", 2))
    products(0, M["DT"], M["D"])
    products(1, M["D"], M["DT"])
    pe.wait_ge(*count("inv_a", 1))
    pe.wait_ge(*count("inv_d", 1))
    products(0, M["D2T"], M["D2"])
    products(1, M["D2"], M["D2T"])
    pe.wait_ge(*count("prod_masked", 4))
    products(6, M["D2T"], M["ID"])
    pe.wait_ge(*count("inv_a", 2))
    pe.wait_ge(*count("inv_d", 2))
    products(7, M["D"], M["DT"])
    pe.wait_ge(*count("prod_masked", 7))
    for h, t in units:
        ins = mm(ps[:, 4, (2 * h + t) * HD:(2 * h + t + 1) * HD], M["Aak"][:, h, t, :], m.kvtok[:, 1, t, h * HD:(h + 1) * HD],
                 start=True, stop=True)
    ins.then_inc(s("u_full"), 1)
    pe.wait_ge(*count("inv_d", 4))
    products(0, M["D"], M["D2"])
    pe.wait_ge(*count("inv_d", 5))
    products(1, M["ID"], M["D2T"])
    products(6, M["D2T"], M["ID"])
    pe.wait_ge(*count("inv_d", 6))
    products(7, M["X"], M["D"])
    pe.wait_ge(*count("inv_a", 4))
    products(0, M["DT"], M["D2"])
    pe.wait_ge(*count("inv_d", 7))
    pe.wait_ge(*count("u_rows", 1))
    for h, t in units:
        ins = mm(unit(5, h, t), M["D"][:, h, t, :], m.rb[:, h, t, :], start=True, stop=True)
    ins.then_inc(s("wu_full"), 1)
    pe.wait_ge(*count("wu_rows", 1))
    for t in range(NT):
        for part in range(3):
            for c in range(CT):
                r = slice(c * CH, (c + 1) * CH)
                lhs, rhs = ((m.WU[r, t, 0], m.btok[r, t, :]), (m.btok[r, t, :], m.WU[r, t, 1]),
                            (m.kvtok[r, 0, t, :], m.kvtok[r, 1, t, :]))[part]
                flat = lambda a: a.rearrange("p h b -> p (h b)") if len(a.shape) == 3 else a
                at = t * T + (0 if part == 0 else P)
                ins = mm(ps[:, c, at:at + P], flat(lhs), flat(rhs), start=part != 2, stop=part != 1)
    ins.then_inc(s("gh_full"), 1)
    for h, t in units:
        ins = mm(ps[h * HD:(h + 1) * HD, 6, t * P:(t + 1) * P], m.WU[:, t, 0, h, :], M["Arb"][:, h, t, :], start=True, stop=True)
    ins.then_inc(s("q_full"), 1)
    for part in range(2):
        for h, t in units:
            lhs = m.WU[:, t, 1, h, :] if part == 0 else m.kvtok[:, 1, t, h * HD:(h + 1) * HD]
            mm(ps[h * HD:(h + 1) * HD, (4, 7)[t], 0:P], lhs, M["Arb" if part == 0 else "Ark"][:, h, t, :],
               start=part == 0, stop=False, skip_group_check=True)
    pe.wait_ge(*count("gh_set", 4))
    pe.wait_ge(*count("q_set", 1))
    for c in range(1, NCH):
        state = m.H[:, 0, :] if c == 1 else m.S[:, c - 2, :]
        if c > 1:
            pe.wait_ge(*count("state_set", c - 1))
        if c < NCH - 1:
            mm(ps[:, 5, (c % 4) * P:(c % 4 + 1) * P], m.G[:, c, :], state, start=True, stop=True).then_inc(s("state_full"), 1)
        t, r = c // CT, slice((c % CT) * CH, (c % CT + 1) * CH)
        ins = mm(ps[:, (4, 7)[t], r], state, m.QT[:, t, r], start=False, stop=True, skip_group_check=True)
    ins.then_inc(s("y_full"), 1)


def pair_counter(m, l, p):
    def count(signal, k):
        per = m.s.of[signal][4] // PAIRS
        return m.at(signal, l, p * per + k)
    return count


def tensor_rwkv_out(m, pe, l):
    ps, at, s = m.ps, m.at, m.s
    mm = m.nc.tensor.matmul
    head_sum = m.const("head_sum")

    def head_sums(b0, src, signal):
        for b in range(2):
            mm(ps[:, b0 + b, :], head_sum, src[:, 2 * b:2 * b + 2, :], start=True, stop=True).then_inc(s(signal), 1)

    pe.wait_ge(*at("y_cols", l))
    head_sums(0, m.y, "gn_full")
    pe.wait_ge(*at("bonus_in", l))
    head_sums(4, m.A, "bonus_full")
    pe.wait_ge(*at("gateup_in", l))
    up = m.par2("gate_up")
    for b in range(2):
        for i in range(2):
            tile = 2 * b + i
            ins = mm(half_bank(m, 6 + b, i), up[:, tile * P:(tile + 1) * P], m.gg, start=True, stop=True)
        ins.then_inc(s("gateup_full"), 1)
    pe.wait_ge(*at("gn_sq", l))
    head_sums(2, m.LW, "var_full")


def tensor_mla(m, pe, l, used):
    nc, ps, at, s = m.nc, m.ps, m.at, m.s
    mm = nc.tensor.matmul
    _, kv_up, q_up = lat_slab(m)
    pe.wait_ge(*at("l_norm", l))
    for b, tiles in ((0, (0, 1)), (1, (2,))):
        for i, c in enumerate(tiles):
            for t in range(NT):
                ins = nc.tensor.transpose(ps[:, b, i * T + t * P:i * T + (t + 1) * P], m.lat[:, t, c * P:(c + 1) * P], m.ident)
        ins.then_inc(s("l_T"), 1)
    pe.wait_ge(*at("l_cols", l))
    pe.wait_ge(*at("ya_cols", l))
    for t in range(NT):
        for b, c0, c1 in ((2, 0, BANK), (3, BANK, MH * QKD)):
            for k in range(2):
                ins = mm(ps[:, b + 2 * t, 0:c1 - c0], m.latT[:, k, t * P:(t + 1) * P], q_up[:, k, c0:c1], start=k == 0, stop=k == 1)
            ins.then_inc(s("q2_full"), 1)
    for t in range(NT):
        for i in range(2):
            mm(ps[:, (6, 0)[t] + i, :], m.latT[:, 2, t * P:(t + 1) * P], kv_up[:, 0, i * BANK:(i + 1) * BANK], start=True, stop=True)\
                .then_inc(s("kv2_full"), 1)
    pe.wait_ge(*at("qk2_rot", l))
    pe.wait_ge(*at("kv2_rows", l))
    for b in range(8):
        for i in range(2):
            h = 2 * (b % 4) + i
            for t in range(NT):
                src = (m.qm if b < 4 else m.km)[:, t, h, :]
                ins = nc.tensor.transpose(ps[0:QKD, b, i * T + t * P:i * T + (t + 1) * P], src, m.ident)
                if b == 0 and i == 0 and t == 0:
                    ins.then_inc(used(W_LAT), 1)
        ins.then_inc(s("qk2_T"), 1)
    pe.wait_ge(*at("qk2_cols_a", l))
    pe.wait_ge(*at("qk2_cols_d", l))
    causal = m.const("causal")
    for t in range(NT):
        n = (t + 1) * P
        for h in range(MH):
            out = mla_scores(m, t)[:, h, :]
            mm(out, m.qmT[0:QKD, h, t * P:(t + 1) * P], m.kmT[0:QKD, h, 0:n], start=True, stop=False)
            ins = mm(out, m.ident, causal[:, 2 * P - n:], start=False, stop=True)
        ins.then_inc(s("s2_full"), 1)
    done = 0
    for t in range(NT):
        pe.wait_ge(*at("p2_rows", l, t + 1))
        banks = (2, 3) if t == 0 else (4, 5, 6, 7)
        n = MH // len(banks)
        for j, b in enumerate(banks):
            for i in range(n):
                for kt in range(t + 1):
                    at0 = (i * (t + 1) + kt) * P
                    ins = nc.tensor.transpose(ps[:, b, at0:at0 + P], m.pm[:, n * j + i, kt * P:(kt + 1) * P], m.ident)
            ins.then_inc(s("p2_T"), 1)
        pe.wait_ge(*at("p2_cols_a", l, (1, 3)[t]))
        pe.wait_ge(*at("p2_cols_d", l, (1, 3)[t]))
        for h in range(MH):
            r = (h % 2) * HD
            for kt in range(t + 1):
                ins = mm(ps[r:r + HD, t, (h // 2) * P:(h // 2 + 1) * P], m.vm[:, kt, h * HD:(h + 1) * HD], m.pmT[:, h, kt, :],
                         start=kt == 0, stop=kt == t)
        ins.then_inc(s("o2_full"), 1)


def mla_scores(m, t):
    if t == 0:
        return m.ps[:, 0:2, :].rearrange("p b (h n) -> p (b h) n", n=P)
    return m.ps[:, 4:8, :].rearrange("p b (h n) -> p (b h) n", n=T)


def scalar_rope(m, act):
    act.wait_ge(*m.at("rope_ang", 0))
    for i in range(2):
        m.nc.scalar.activation(m.cs2[:, i].rearrange("p t i -> p (t i)"), m.rope_tmp[:, i], ACT.Sin).then_inc(m.s("rope_set"), 1)


def shift_tile(m, i):
    return (m.R, m.K, m.V)[i // 4][:, i % 4, :] if i < 12 else (m.wa, m.gg)[i - 12]


S_MU = 208


def scalar_second(m, act, l):
    nc, ps, at, s = m.nc, m.ps, m.at, m.s
    go = nc.scalar.activation
    col = lambda c: m.stat[:, c:c + 1]
    norm_squares(m, act, m.prev("h_ffn", l), s("n1_sq"))
    act.wait_ge(*at("par2_loaded", l))
    act_columns(m, act, m.hT, m.par2("attn_g"), *at("n1_T", l, 0), s("n1_cols_a"))
    act.wait_ge(*at("mu_set", l))
    for i in range(SHIFT_TILES):
        if i % 2 == 0:
            act.wait_ge(*at("rw_full", l, i // 2 + 1))
        go(shift_tile(m, i), half_bank(m, (4, 5, 6, 7, 0, 1, 2)[i // 2], i % 2), ACT.Copy, scale=col(S_MU + i))\
            .then_inc(s("rw_scaled"), 1)
    act.wait_ge(*at("rw_cols", l, 13))
    go(m.wa[0:64, :], m.wa[0:64, :], ACT.Tanh).then_inc(s("lora_in"), 1)
    act.wait_ge(*at("rw_cols", l))
    go(m.gg, m.gg, ACT.Sigmoid).then_inc(s("gateup_in"), 1)
    for b in range(4):
        act.wait_ge(*at("lora_full", l, b + 1))
        for i in range(2):
            tile = 2 * (b % 2) + i
            go((m.LW, m.A)[b // 2][:, tile, :], half_bank(m, (5, 6, 7, 0)[b], i), ACT.Sigmoid,
               bias=m.par2(("decay_base", "iclr_base")[b // 2])[:, tile:tile + 1]).then_inc(s("lora_sig"), 1)
    for b in range(2):
        act.wait_ge(*at("kk_full", l, b + 1))
        go(m.rs[:, 2 * b:2 * b + 2, :], two(ps[:, 1 + b, :]), ACT.Sqrt, bias=m.const("kk_eps")).then_inc(s("kk_root"), 1)
    act.wait_ge(*at("c_less", l))
    go(m.LW, m.LW, ACT.Exp).then_inc(s("decays"), 1)
    go(m.E1, m.C, ACT.Exp).then_inc(s("decays"), 1)
    act.wait_ge(*at("decays", l, 2))
    go(m.C, m.C, ACT.Exp, scale=-1.0).then_inc(s("decays"), 1)
    with act.Fori(0, PAIRS) as p:
        scalar_pair(m, act, l, p)
    for b in range(2):
        act.wait_ge(*at("y_mid", l, b + 1))
        go(m.LW[:, 2 * b:2 * b + 2, :], m.y[:, 2 * b:2 * b + 2, :], ACT.Square, scale=HD ** -0.5).then_inc(s("gn_sq"), 1)
    for b in range(2):
        act.wait_ge(*at("var_full", l, b + 1))
        go(m.C[:, 2 * b:2 * b + 2, :], two(ps[:, 2 + b, :]), ACT.Sqrt, bias=m.const("lnx_eps")).then_inc(s("gn_root"), 1)
    act.wait_ge(*at("lat_rows", l))
    junk = m.S.rearrange("p n b -> p (n b)")
    for t in range(NT):
        for i, part in enumerate((slice(0, QL), slice(QL, QL + KVL))):
            n = part.stop - part.start
            go(junk[:, t * (QL + KVL) + part.start:t * (QL + KVL) + part.stop], m.lat[:, t, part], ACT.Square,
               scale=n ** -0.5, accum_out=col(10 + 2 * t + i)).then_inc(s("l_sq"), 1)
    for c in range(3):
        if c != 1:
            act.wait_ge(*at("l_T", l, c // 2 + 1))
        gain = m.par2("q_g")[:, c:c + 1] if c < 2 else m.par2("kv_g")
        go(m.latT[:, c, :], half_bank(m, c // 2, c % 2), ACT.Copy, scale=gain).then_inc(s("l_cols"), 1)
    for i in range(4):
        act.wait_ge(*at("kv2_full", l, i + 1))
        heads = ps[:, (6, 7, 0, 1)[i], :].rearrange("p (h d) -> p h d", d=2 * NOPE)
        half = slice(4 * (i % 2), 4 * (i % 2) + 4)
        go(m.km[:, i // 2, half, 0:NOPE], heads[:, :, 0:NOPE], ACT.Copy).then_inc(s("kv2_rows"), 1)
        go(m.vm[:, i // 2, (i % 2) * 256:(i % 2 + 1) * 256].rearrange("p (h d) -> p h d", d=NOPE), heads[:, :, NOPE:], ACT.Copy)\
            .then_inc(s("kv2_rows"), 1)
    for b in range(4):
        act.wait_ge(*at("qk2_T", l, b + 1))
        go(m.qmT[0:QKD, 2 * b:2 * b + 2, :], two(ps[0:QKD, b, :]), ACT.Copy).then_inc(s("qk2_cols_a"), 1)
    for t in range(NT):
        act.wait_ge(*at("s2_max", l, t + 1))
        if t:
            act.wait_ge(*at("p2_T", l, 2))
        for h in range(MH):
            go(m.pm[:, h, 0:(t + 1) * P], mla_scores(m, t)[:, h, :], ACT.Exp, bias=col(S_MAX + MH * t + h), scale=QKD ** -0.5,
               accum_out=col(S_SUM + MH * t + h)).then_inc(s("s2_exp"), 1)
        if t:
            act.wait_ge(*at("o2_full", l, 1))
        for j in range(t + 1):
            act.wait_ge(*at("p2_T", l, (1, 3 + j)[t]))
            mla_prob_columns(m, go, t, j, ACT.Copy).then_inc(s("p2_cols_a"), 1)
    for b in range(8):
        act.wait_ge(*at("gates_full", l, b + 1))
        go(m.sg[:, b // 4, 2 * (b % 4):2 * (b % 4) + 2, :], two(ps[:, b, :]), ACT.Sigmoid).then_inc(s("gates_sig"), 1)
    norm_squares(m, act, at("h_mixed", l), s("n2_sq"))
    act_columns(m, act, m.hT, m.par2("ffn_g"), *at("n2_T", l, 0), s("n2_cols_a"))
    for j in range(NUP):
        act.wait_ge(*at("up_full", l, 2 * j + 1))
        if j >= 2:
            act.wait_ge(*at("up_act", l, j - 1))
        for c in range(2):
            f = 2 * j + c
            go(m.cb[:, j % 2, c, :], half_bank(m, 2 * j % 8, c), ACT.Identity, bias=m.par2("conv_b")[:, f:f + 1],
               scale=m.par2("conv_w")[:, 2 * NF + f:2 * NF + f + 1]).then_inc(s("up_base"), 1)
        act.wait_ge(*at("up_conv", l, j + 1))
        go(m.cb[:, j % 2], m.cb[:, j % 2], ACT.Gelu).then_inc(s("up_gelu"), 1)


def mla_prob_columns(m, op, t, j, *args):
    n = (4, 2)[t]
    src = m.ps[:, (2, 4)[t] + j, :].rearrange("p (h k b) -> p h k b", h=n, b=P)
    return op(m.pmT[:, n * j:n * j + n, 0:t + 1, :], src, *args)


def scalar_pair(m, act, l, p):
    ps, s, M = m.ps, m.s, m.mat
    count = pair_counter(m, l, p)

    def copy(wait, dst, src, done):
        act.wait_ge(*count(*wait))
        return m.nc.scalar.activation(dst, src, ACT.Copy).then_inc(s(done), 1)

    def units(b):
        return ps[:, b, :].rearrange("p (h t b) -> p h t b", h=2, t=NT)

    copy(("tok_T", 2), m.kvtok, ps[:, 1, :].rearrange("p (a t b) -> p a t b", a=2, t=NT), "tok_a")
    copy(("inv_full", 1), M["D2"], units(0), "inv_a")
    copy(("inv_full", 3), M["D"], units(0), "inv_a")
    copy(("u_full", 1), m.rb[:, :, :, HD:], ps[:, 4, 0:4 * HD].rearrange("p (h t b) -> p h t b", h=2, t=NT), "u_rows")
    copy(("inv_full", 9), M["DT"], units(6), "inv_a")
    copy(("inv_full", 10), M["D2"], units(7), "inv_a")
    act.wait_ge(*count("wu_full", 1))
    for h in range(2):
        ins = m.nc.scalar.activation(m.WU[:, :, :, h, :], units(5)[:, h].rearrange("p t (w b) -> p t w b", w=2), ACT.Copy)
    ins.then_inc(s("wu_rows"), 1)


def gpsimd_second(m, pool, l):
    at, s = m.at, m.s
    pool.wait_ge(*m.prev("h_ffn", l))
    pool.dma_start(m.par[:, 0:NPAR2], m.d["par2"][bass.ds(l, 1)].rearrange("l p n -> p (l n)")).then_inc(s("par2_loaded"), 16)
    gpsimd_rstd(m, pool, at("n1_sq", l), 0, 2, 0, s("n1_rstd"))
    gpsimd_rstd(m, pool, at("l_sq", l), 10, 4, 0, s("l_rstd"))
    gpsimd_rstd(m, pool, at("n2_sq", l), 0, 2, 0, s("n2_rstd"))
    pool.dma_start(m.fin, m.d["fix"][:, KD + D:KD + 2 * D]).then_inc(s("fin2_loaded"), 16)


def vector_rope(m, dve):
    v = m.nc.vector
    cos, sin, turns, pos = (m.rope_tmp[:, i] for i in range(4))
    dve.wait_ge(*m.at("x_first", 0))
    v.tensor_copy(pos[:, 0:NT], m.pos_i[:, :])
    dve.drain()
    for t in range(NT):
        v.tensor_scalar(sin[:, t * PE_D // 2:(t + 1) * PE_D // 2], m.const("freq"), pos[:, t:t + 1], None, ALU.mult)
    dve.drain()
    magic = 1.5 * 2.0 ** 23
    v.tensor_scalar(turns, sin, 1.0 / (2 * math.pi), None, ALU.mult)
    for step in (magic, -magic):
        dve.drain()
        v.tensor_scalar(turns, turns, step, None, ALU.add)
    c1 = 6.28125
    c2 = float(np.float32(round((2 * math.pi - c1) * 2 ** 20) / 2 ** 20))
    for part in (c1, c2, 2 * math.pi - c1 - c2):
        dve.drain()
        v.scalar_tensor_tensor(sin, turns, -part, sin, ALU.mult, ALU.add)
    dve.drain()
    limit = float(np.nextafter(np.float32(math.pi), np.float32(0)))
    v.tensor_scalar(sin, sin, limit, -limit, ALU.min, ALU.max)
    dve.drain()
    v.tensor_scalar(cos, sin, -1.0, None, ALU.mult)
    dve.drain()
    v.tensor_tensor(cos, cos, sin, ALU.max)
    dve.drain()
    v.tensor_scalar(cos, cos, -1.0, math.pi / 2, ALU.mult, ALU.add).then_inc(m.s("rope_ang"), 1)


def tiles_bc(par):
    return bc(par, T)


def vector_second(m, dve, l):
    v, ps, at, s = m.nc.vector, m.ps, m.at, m.s
    stt = v.scalar_tensor_tensor
    dve.wait_ge(*at("par2_loaded", l))
    v.tensor_scalar(m.stat[:, S_MU:S_MU + SHIFT_TILES], m.par2("mu"), -1.0, 1.0, ALU.mult, ALU.add).then_inc(s("mu_set"), 1)
    vector_norm(m, dve, l, "n1", m.par2("attn_g"))
    for i in range(SHIFT_TILES):
        dve.wait_ge(*at("rw_scaled", l, i // 2 * 2 + 2))
        dst = shift_tile(m, i)
        stt(dst[:, 1:], half_bank(m, (4, 5, 6, 7, 0, 1, 2)[i // 2], i % 2)[:, 0:T - 1], m.par2("mu")[:, i:i + 1], dst[:, 1:],
            ALU.mult, ALU.add).then_inc(s("rw_cols"), 1)
    for t in range(NT):
        dve.wait_ge(*at("lat_full", l, t + 1))
        v.tensor_copy(m.lat[:, t, :], ps[:, 3 + t, 0:LAT]).then_inc(s("lat_rows"), 1)
    dve.wait_ge(*at("rw_cols", l))
    v.tensor_tensor(m.KK, m.K, tiles_bc(m.par2("k_k")), ALU.mult)
    dve.drain()
    v.tensor_tensor(m.sq, m.KK, m.KK, ALU.mult).then_inc(s("kk_sq"), 1)
    dve.wait_ge(*at("lora_sig", l, 4))
    v.tensor_scalar(m.LW, m.LW, -math.exp(-0.5), None, ALU.mult).then_inc(s("log_w"), 1)
    dve.wait_ge(*at("log_w", l))
    for i in range(PAIRS):
        v.tensor_tensor_scan(m.C[:, i, :], m.const("scan"), m.LW[:, i, :], 0.0, ALU.mult, ALU.add).then_inc(s("log_c"), 1)
    dve.wait_ge(*at("log_c", l))
    v.tensor_tensor(m.LW, m.C, m.LW, ALU.subtract).then_inc(s("c_less"), 1)
    dve.wait_ge(*at("kk_root", l))
    v.reciprocal(m.rs, m.rs)
    dve.drain()
    v.tensor_tensor(m.KK, m.KK, m.rs, ALU.mult)
    dve.wait_ge(*at("lora_sig", l))
    stt(m.sq, m.A, 1.0, tiles_bc(m.par2("k_a")), ALU.subtract, ALU.mult)
    dve.drain()
    stt(m.K, m.sq, 1.0, m.K, ALU.add, ALU.mult)
    v.tensor_tensor(m.A, m.KK, m.A, ALU.mult)
    for zero in (m.G, m.H):
        v.memset(zero, 0.0)
    dve.drain()
    dve.wait_ge(*at("decays", l))
    v.memset(m.stat[:, 254:255], 0.0)
    with dve.Fori(0, PAIRS) as p:
        vector_pair(m, dve, l, p)
    vector_rwkv_out(m, dve, l)
    vector_mla(m, dve, l)
    dve.wait_ge(*at("gates_sig", l))
    for b in range(4):
        dve.wait_ge(*at("br2_full", l, 4 + b + 1))
        for j in range(2):
            v.tensor_tensor(two(m.m1[:, j, :]), m.sg[:, j, 2 * b:2 * b + 2, :], two(ps[:, 4 * j + b, :]), ALU.mult)
        dve.drain()
        v.tensor_tensor(m.mT[:, 2 * b:2 * b + 2, :], two(m.m1[:, 0, :]), two(m.m1[:, 1, :]), ALU.add).then_inc(s("merged"), 1)
        dve.drain()
    add_into_x(m, dve, *at("out3_full", l, 0), s("h_mixed"))
    vector_norm(m, dve, l, "n2", m.par2("ffn_g"))
    for j in range(NUP):
        dve.wait_ge(*at("up_base", l, 2 * j + 2))
        for back in (1, 2):
            for c in range(2):
                f = (2 - back) * NF + 2 * j + c
                dst = m.cb[:, j % 2, c, back:]
                ins = stt(dst, half_bank(m, 2 * j % 8, c)[:, 0:T - back], m.par2("conv_w")[:, f:f + 1], dst, ALU.mult, ALU.add)
            if back == 1:
                dve.drain()
        ins.then_inc(s("up_conv"), 1)
        dve.wait_ge(*at("up_gelu", l, j + 1))
        dve.wait_ge(*at("up_full", l, 2 * j + 2))
        v.tensor_tensor(m.act[:, 2 * j:2 * j + 2, :], m.cb[:, j % 2], two(ps[:, (2 * j + 1) % 8, :]), ALU.mult)\
            .then_inc(s("up_act"), 1)
    add_into_x(m, dve, *at("down_full", l, 0), s("h_ffn"))


def vector_pair(m, dve, l, p):
    v, ps, s, M = m.nc.vector, m.ps, m.s, m.mat
    tt = v.tensor_tensor
    count = pair_counter(m, l, p)

    def wait(signal, k):
        dve.wait_ge(*count(signal, k))

    def mine(a):
        return a[:, bass.ds(p, 1), :].rearrange("p o (t b) -> p (o t) b", b=P)

    def units(b):
        return ps[:, b, :].rearrange("p (h t b) -> p h t b", h=2, t=NT)

    def masked(name, b, part, mask):
        src = ps[:, b:b + 2, 0:NT * P].rearrange("p h (t b) -> p h t b", t=NT) if part is None else \
            ps[:, b:b + 2, :].rearrange("p h (t w b) -> p h t w b", t=NT, w=2)[:, :, :, part, :]
        for h in range(2):
            ins = tt(M[name][:, h], src[:, h], m.const(mask).unsqueeze(1).to_broadcast([P, NT, P]), ALU.mult)
        ins.then_inc(s("prod_masked"), 1)

    v.scalar_tensor_tensor(m.arp[:, :, 0, :], mine(m.KK), -1.0, mine(m.LW), ALU.mult, ALU.mult).then_inc(s("pair_in"), 1)
    tt(m.btp, mine(m.A), mine(m.C), ALU.mult).then_inc(s("pair_in"), 1)
    tt(m.ktp, mine(m.K), mine(m.C), ALU.mult).then_inc(s("pair_in"), 1)
    v.tensor_copy(m.vtp, mine(m.V)).then_inc(s("pair_in"), 1)
    tt(m.arp[:, :, 1, :], mine(m.R), mine(m.E1), ALU.mult).then_inc(s("pair_in"), 1)
    wait("tok_T", 1)
    v.tensor_copy(m.rb.rearrange("p h t b -> p t h b")[:, :, :, 0:HD], ps[:, 0, 0:T].rearrange("p (t h b) -> p t h b", t=NT, h=2))\
        .then_inc(s("tok_d"), 1)
    v.tensor_copy(m.btok, ps[:, 0, T:].rearrange("p (t b) -> p t b", t=NT)).then_inc(s("tok_d"), 1)
    wait("prod_full", 1)
    masked("D", 6, None, "low16")
    wait("prod_full", 2)
    masked("DT", 2, 0, "up16")
    wait("prod_masked", 1)
    tt(M["ID"].rearrange("p h t b -> p (h t) b"), M["D"].rearrange("p h t b -> p (h t) b"),
       m.ident.unsqueeze(1).to_broadcast([P, 2 * NT, P]), ALU.add).then_inc(s("prod_masked"), 1)
    masked("X", 6, None, "low32x")
    wait("inv_full", 2)
    v.tensor_copy(M["D2T"], units(1)).then_inc(s("inv_d"), 1)
    wait("prod_full", 3)
    masked("Aak", 4, 0, "up32")
    wait("inv_full", 4)
    v.tensor_copy(M["DT"], units(1)).then_inc(s("inv_d"), 1)
    wait("inv_full", 5)
    tt(M["ID"], units(6), M["ID"], ALU.add).then_inc(s("inv_d"), 1)
    masked("Arb", 2, 1, "up32d")
    masked("Ark", 4, 1, "up32d")
    wait("inv_full", 6)
    tt(M["D2"].rearrange("p h t b -> p (h t) b"), ps[:, 7, :].rearrange("p (u b) -> p u b", b=P),
       m.ident.unsqueeze(1).to_broadcast([P, 2 * NT, P]), ALU.add).then_inc(s("inv_d"), 1)
    wait("inv_d", 4)
    wait("inv_full", 7)
    tt(M["D2T"], units(0), M["D2"], ALU.add).then_inc(s("inv_d"), 1)
    wait("inv_full", 8)
    v.tensor_copy(M["D"], units(1)).then_inc(s("inv_d"), 1)
    wait("inv_full", 11)
    wait("inv_d", 6)
    tt(M["D"], units(0), M["D"], ALU.add).then_inc(s("inv_d"), 1)
    wait("gh_full", 1)
    ends = m.E1[:, bass.ds(p, 1), CH - 1::CH].rearrange("p o (t c) -> p (o t) c", t=NT)
    for w, dst in ((0, m.G), (1, m.H)):
        for h in range(2):
            r = slice(h * HD, (h + 1) * HD)
            for t in range(NT):
                out = dst[r, t * CT:(t + 1) * CT, r]
                src = ps[r, 0:CT, t * T + w * P + h * HD:t * T + w * P + (h + 1) * HD]
                other = m.ident[r, r].unsqueeze(1).to_broadcast([HD, CT, HD]) if w == 0 else bc(ends[r, t], HD)
                ins = tt(out, src, other, ALU.add if w == 0 else ALU.mult)
            ins.then_inc(s("gh_set"), 1)
    wait("q_full", 1)
    tt(m.QT, ps[:, 6, 0:T].rearrange("p (t b) -> p t b", t=NT), m.arp[:, :, 1, :], ALU.add).then_inc(s("q_set"), 1)
    wait("gh_set", 4)
    for c in range(1, NCH - 1):
        wait("state_full", c)
        end = m.E1[:, bass.ds(p, 1), (c + 1) * CH - 1]
        v.scalar_tensor_tensor(m.S[:, c - 1, :], ps[:, 5, (c % 4) * P:(c % 4 + 1) * P], end, m.H[:, c, :], ALU.mult, ALU.add)\
            .then_inc(s("state_set"), 1)
    wait("y_full", 1)
    v.tensor_scalar(mine(m.y), ps[:, 4:8:3, 0:P], 1.0, None, ALU.mult).then_inc(s("y_cols"), 1)


def vector_rwkv_out(m, dve, l):
    v, ps, at, s = m.nc.vector, m.ps, m.at, m.s
    tt = v.tensor_tensor

    def banks(b):
        return ps[:, b:b + 2, :].rearrange("p b (a n) -> p (b a) n", n=T)

    tt(m.A, m.R, m.K, ALU.mult)
    dve.drain()
    tt(m.A, m.A, tiles_bc(m.par2("r_k")), ALU.mult).then_inc(s("bonus_in"), 1)
    for b in range(2):
        dve.wait_ge(*at("gn_full", l, b + 1))
        yb = m.y[:, 2 * b:2 * b + 2, :]
        v.scalar_tensor_tensor(yb, two(ps[:, b, :]), -1.0 / HD, yb, ALU.mult, ALU.add).then_inc(s("y_mid"), 1)
    dve.wait_ge(*at("bonus_full", l))
    tt(m.E1, banks(4), m.V, ALU.mult)
    dve.wait_ge(*at("gn_root", l))
    v.reciprocal(m.C, m.C)
    dve.drain()
    tt(m.y, m.y, m.C, ALU.mult)
    dve.drain()
    for i in range(PAIRS):
        v.tensor_scalar(m.y[:, i, :], m.y[:, i, :], m.par2("lnx_w")[:, i:i + 1], m.par2("lnx_b")[:, i:i + 1], ALU.mult, ALU.add)
    dve.drain()
    tt(m.y, m.y, m.E1, ALU.add)
    dve.drain()
    for b in range(2):
        dve.wait_ge(*at("gateup_full", l, b + 1))
        tt(m.yaT[:, 2 * b:2 * b + 2, :], m.y[:, 2 * b:2 * b + 2, :], two(ps[:, 6 + b, :]), ALU.mult).then_inc(s("ya_cols"), 1)


def vector_mla(m, dve, l):
    v, ps, at, s = m.nc.vector, m.ps, m.at, m.s
    tt = v.tensor_tensor
    dve.wait_ge(*at("l_rstd", l))
    for t in range(NT):
        for i, part in enumerate((slice(0, QL), slice(QL, QL + KVL))):
            c = 74 + 2 * t + i
            v.tensor_scalar(m.lat[:, t, part], m.lat[:, t, part], m.stat[:, c:c + 1], None, ALU.mult).then_inc(s("l_norm"), 1)
    pe_part = slice(NOPE, QKD)
    dve.wait_ge(*at("ya_cols", l))
    v.tensor_copy(m.qm[:, :, MH, pe_part], m.lat[:, :, QL + KVL:])
    for i in range(4):
        t, c0, c1 = i // 2, (0, BANK)[i % 2], (BANK, MH * QKD)[i % 2]
        dve.wait_ge(*at("q2_full", l, i + 1))
        v.tensor_copy(m.qm[:, t].rearrange("p h d -> p (h d)")[:, c0:c1], ps[:, 2 + i, 0:c1 - c0]).then_inc(s("q2_rows"), 1)
    dve.wait_ge(*at("q2_rows", l))
    dve.wait_ge(*at("rope_set", 0))
    x1, x2 = m.qm[:, :, :, NOPE:NOPE + PE_D // 2], m.qm[:, :, :, NOPE + PE_D // 2:]
    tmp = [m.pe_tmp[:, i].rearrange("p (t h i) -> p t h i", t=NT, h=MH + 1) for i in range(4)]
    cos, sin = (m.cs2[:, i].unsqueeze(2).to_broadcast([P, NT, MH + 1, PE_D // 2]) for i in range(2))
    for out, x, c in zip(tmp, (x1, x2, x1, x2), (cos, sin, sin, cos)):
        tt(out, x, c, ALU.mult)
    dve.drain()
    tt(x1, tmp[0], tmp[1], ALU.subtract)
    tt(x2, tmp[2], tmp[3], ALU.add)
    dve.drain()
    v.tensor_copy(m.km[:, :, :, pe_part], m.qm[:, :, MH, pe_part].unsqueeze(2).to_broadcast([P, NT, MH, PE_D]))\
        .then_inc(s("qk2_rot"), 1)
    for b in range(4):
        dve.wait_ge(*at("qk2_T", l, 4 + b + 1))
        v.tensor_copy(m.kmT[0:QKD, 2 * b:2 * b + 2, :], two(ps[0:QKD, 4 + b, :])).then_inc(s("qk2_cols_d"), 1)
    for t in range(NT):
        dve.wait_ge(*at("s2_full", l, t + 1))
        mx = m.stat[:, S_MAX + MH * t:S_MAX + MH * (t + 1)]
        v.tensor_reduce(mx, mla_scores(m, t), axis=AX.X, op=ALU.max)
        dve.drain()
        v.tensor_scalar(mx, mx, -QKD ** -0.5, None, ALU.mult).then_inc(s("s2_max"), 1)
    for t in range(NT):
        dve.wait_ge(*at("s2_exp", l, MH * (t + 1)))
        inv = m.stat[:, S_INV + MH * t:S_INV + MH * (t + 1)]
        v.reciprocal(inv, m.stat[:, S_SUM + MH * t:S_SUM + MH * (t + 1)])
        dve.drain()
        rows = m.pm[:, :, 0:(t + 1) * P]
        tt(rows, rows, bc(inv, (t + 1) * P), ALU.mult).then_inc(s("p2_rows"), 1)
        if t:
            dve.wait_ge(*at("o2_full", l, 1))
        for j in range(t + 1):
            dve.wait_ge(*at("p2_T", l, (2, 5 + j)[t]))
            mla_prob_columns(m, v.tensor_copy, t, t + 1 + j).then_inc(s("p2_cols_d"), 1)
    for t in range(NT):
        dve.wait_ge(*at("o2_full", l, t + 1))
        v.tensor_copy(m.o2T[:, :, t * P:(t + 1) * P], ps[:, t, :].rearrange("p (i b) -> p i b", b=P)).then_inc(s("o2_cols"), 1)


def scalar_end(m, act):
    norm_squares(m, act, m.prev("h_ffn", L), m.s("f2_sq"))


def gpsimd_end(m, pool):
    gpsimd_rstd(m, pool, m.at("f2_sq", 0), 0, 2, 0, m.s("f2_rstd"))


def vector_end(m, dve):
    dve.wait_ge(*m.at("fin2_loaded", L - 1))
    dve.wait_ge(*m.at("f2_rstd", 0))
    for t in range(NT):
        m.nc.vector.scalar_tensor_tensor(m.xn[:, t, :], m.x[:, t, :], m.stat[:, 64 + t:65 + t], m.fin, ALU.mult, ALU.mult)\
            .then_inc(m.s("y_final"), 1)


def sync_end(m, sp, out):
    for t in range(NT):
        sp.wait_ge(*m.at("y_final", 0, t + 1))
        sp.dma_start(out[0, t * P:(t + 1) * P, :], m.xn[:, t, :]).then_inc(m.s("out_stored"), 16)
    sp.wait_ge(*m.at("out_stored", 0))


BIG = ("x", "mem", "w_in", "w_out", "xattn_w_q", "xattn_w_kv", "xattn_w_o", "w_gate", "w_up", "w_down", "w_in_2",
       "w_q_up_2", "w_kv_up_2", "w_out_rwkv_2", "w_out_mla_2", "w_out_2", "w_ffn_up_2", "w_ffn_down_2")


def build(nc, d, out):
    from contextlib import ExitStack
    with ExitStack() as ctx:
        m = allocate(nc, ctx)
        m.d = d
        block = ctx.enter_context(nc.Block())

        @block.sync
        def _(sp):
            sync_start(m, sp)
            with sp.Fori(0, L) as l:
                sync_first(m, sp, l)
            with sp.Fori(0, L) as l:
                sync_second(m, sp, l)
            sync_end(m, sp, out)

        @block.gpsimd
        def _(pool):
            gpsimd_start(m, pool)
            with pool.Fori(0, L) as l:
                gpsimd_first(m, pool, l)
            gpsimd_between(m, pool)
            with pool.Fori(0, L) as l:
                gpsimd_second(m, pool, l)
            gpsimd_end(m, pool)

        @block.scalar
        def _(act):
            scalar_start(m, act)
            with act.Fori(0, L) as l:
                scalar_first(m, act, l)
            scalar_between(m, act)
            scalar_rope(m, act)
            with act.Fori(0, L) as l:
                scalar_second(m, act, l)
            scalar_end(m, act)

        @block.vector
        def _(dve):
            vector_start(m, dve)
            with dve.Fori(0, L) as l:
                vector_first(m, dve, l)
            vector_between(m, dve)
            vector_rope(m, dve)
            with dve.Fori(0, L) as l:
                vector_second(m, dve, l)
            vector_end(m, dve)

        @block.tensor
        def _(pe):
            tensor_start(m, pe)
            with pe.Fori(0, L) as l:
                tensor_first(m, pe, l)
            with pe.Fori(0, L) as l:
                tensor_second(m, pe, l)


def kernel(**inputs):
    from concourse import bacc
    from concourse.bass_utils import run_bass_kernel_spmd as run
    nc = bacc.Bacc("TRN2", target_bir_lowering=False, num_devices=1)
    arrays = {n: np.asarray(inputs[n]) for n in BIG}
    arrays.update(lay_out(inputs))
    d = {n: nc.dram_tensor("in_" + n, a.shape, I32 if n == "positions" else F32, kind="ExternalInput").ap()
         for n, a in arrays.items()}
    out = nc.dram_tensor("out_0", (1, T, D), F32, kind="ExternalOutput").ap()
    build(nc, d, out)
    r = run(nc, [{"in_" + n: a for n, a in arrays.items()}], core_ids=[0])
    return r.results[0]["out_0"]
```

```python
import math

import numpy as np

import concourse.bass as bass
from concourse import mybir
from concourse.alu_op_type import AluOpType as ALU

F32 = mybir.dt.float32
F32R = mybir.dt.float32r
I32 = mybir.dt.int32
U32 = mybir.dt.uint32
ACT = mybir.ActivationFunctionType
AX = mybir.AxisListType

P = 128
D = 1024
KD = D // P
T = 256
NT = T // P
L = 2
EPS = 1e-6
BANK = 512

GM_W, GM_G = 512, 4
NQ, NKV, HD = 8, 2, 64
HEADS_QK = NQ + NKV
XH, XD = 4, 256
E, CAP, FF = 16, 32, 1024

RW = 512
PAIRS = RW // P
CH = 32
NCH = T // CH
CT = P // CH
SHIFT_TILES = 14
QL, KVL, PE_D, NOPE = 256, 128, 32, 64
MH = 8
QKD = NOPE + PE_D
LAT = QL + KVL + PE_D
FFN = 2816
NF = FFN // P
NUP = NF // 2
LNX_EPS = 64e-5

SLOTS = 6
SLAB = 4096


class Slab:
    def __init__(self, slot, landed, held):
        self.slot, self.landed, self.held = slot, landed, held


def ring_plan(slabs):
    landed, held = [0] * SLOTS, [0] * SLOTS
    plan = []
    for s, n in slabs:
        landed[s] += 16 * n
        plan.append(Slab(s, landed[s], held[s]))
        held[s] += 1
    return plan, landed, held


PLAN1, LANDED1, HELD1 = ring_plan([(i % SLOTS, 1) for i in range(18)])
W_IN1, W_XK, W_OUT1, W_XQ, W_XV, W_XO = 0, 4, 6, 10, 12, 14
LANDED1_LAYER = [n + 16 * E for n in LANDED1]
HELD1_LAYER = [n + E for n in HELD1]
SG_SLOT = SLOTS - 1
NDN = -(-NF // 4)
PLAN2, LANDED2, HELD2 = ring_plan(
    [(s, 1) for s in (0, 1, 2, 3)] + [(4, 3)] + [(s, 1) for s in (0, 1, 2, 3, 0, 1, 2, 3)] +
    [((4 + i) % SLOTS, 2) for i in range(NUP)] + [((4 + NUP + i) % SLOTS, 1) for i in range(NDN)])
W_IN2, W_LAT, W_GATES, W_ORW, W_OMLA, W_OUT2, W_UP, W_DN = 0, 4, 5, 9, 10, 11, 13, 13 + NUP

CONST_COLS = {}


def _const_layout():
    at = 0
    for name, width in (("ident", P), ("head_sum", P), ("ones", P), ("cos1", NT * HD // 2), ("sin1", NT * HD // 2),
                        ("iota_row", T), ("iota_col", NT), ("expert_diag", E), ("causal", P),
                        ("low16", P), ("up16", P), ("low32x", P), ("up32", P), ("up32d", P),
                        ("scan", T), ("freq", PE_D // 2), ("eps", 64), ("neg_half", 1), ("kk_eps", 1),
                        ("lnx_eps", 1)):
        CONST_COLS[name] = (at, width)
        at += width
    return at


NCONST = _const_layout()


def constants():
    c = np.zeros((P, NCONST), np.float32)

    def put(name, value):
        at, width = CONST_COLS[name]
        c[:, at:at + width] = np.asarray(value, np.float32).reshape(-1, width)

    i = np.arange(P)
    put("ident", np.eye(P))
    put("head_sum", i[:, None] // 64 == i[None, :] // 64)
    put("ones", np.ones((P, P)))
    n = HD // 4
    freqs = np.exp(-math.log(10000.0) * np.arange(n, dtype=np.float32) / n).astype(np.float32)
    t = np.arange(T)
    ang = np.concatenate([(t // 64).astype(np.float32)[:, None] * freqs, (t % 64).astype(np.float32)[:, None] * freqs], 1)
    put("cos1", np.cos(ang).reshape(NT, P, HD // 2).transpose(1, 0, 2).reshape(P, -1))
    put("sin1", np.sin(ang).reshape(NT, P, HD // 2).transpose(1, 0, 2).reshape(P, -1))
    put("iota_row", np.broadcast_to(np.arange(T), (P, T)))
    put("iota_col", i[:, None] + P * np.arange(NT)[None, :])
    put("expert_diag", np.eye(P)[:, :E])
    put("causal", np.where(i[None, :] <= i[:, None], 0.0, -1e30))
    r, s = i[:, None], i[None, :]
    put("low16", (s < r) & (r // 16 == s // 16))
    put("up16", (r < s) & (r // 16 == s // 16))
    put("low32x", (r // CH == s // CH) & (r // 16 == s // 16 + 1))
    put("up32", (r < s) & (r // CH == s // CH))
    put("up32d", (r <= s) & (r // CH == s // CH))
    put("scan", np.broadcast_to((t % CH != 0), (P, T)))
    put("freq", np.broadcast_to(np.power(np.float32(10000.0), -np.arange(0, PE_D, 2, dtype=np.float32) / PE_D), (P, PE_D // 2)))
    eps = np.full(64, EPS)
    eps[32:52] = 64 * EPS
    put("neg_half", np.full((P, 1), -0.5))
    put("kk_eps", np.full((P, 1), 1e-12))
    put("lnx_eps", np.full((P, 1), LNX_EPS))
    put("eps", np.broadcast_to(eps, (P, 64)))
    return c


def _layout(items):
    cols, at = {}, 0
    for name, width in items:
        cols[name] = (at, width)
        at += width
    return cols, at


PAR1, SOON1 = _layout((("mix_g", 8), ("x_g", 8), ("ffn_g", 8), ("branch_g", 8), ("b_s", GM_G), ("router", KD * E)))
PAR2, SOON2 = _layout((("attn_g", 8), ("ffn_g", 8), ("mu", 14), ("decay_base", 4), ("iclr_base", 4), ("k_k", 4),
                       ("k_a", 4), ("r_k", 4), ("lnx_w", 4), ("lnx_b", 4), ("q_g", 2), ("kv_g", 1), ("conv_w", 3 * NF),
                       ("conv_b", NF)))
SOON = max(SOON1, SOON2)
LATE1, NLATE1 = _layout((("w_s", GM_G * P), ("v_g", GM_W), ("qk_g", 2 * HD)))
LATE2, NLATE2 = _layout((("lora_up", RW), ("gate_up", RW)))
for late, cols in ((LATE1, PAR1), (LATE2, PAR2)):
    cols.update((name, (SOON + at, width)) for name, (at, width) in late.items())
NPAR = SOON + max(NLATE1, NLATE2)


def columns(v):
    v = np.asarray(v)
    return np.swapaxes(v.reshape(*v.shape[:-1], -1, P), -1, -2)


def rows(v):
    v = np.asarray(v)
    return np.broadcast_to(v[:, None, :], (v.shape[0], P, v.shape[1]))


def lay_out(a):
    soon1 = np.concatenate([
        columns(a["mix_norm_g"]), columns(a["xattn_norm_g"]), columns(a["ffn_norm_g"]),
        columns(np.reshape(a["branch_norm_g"], (L, 2 * GM_W))), np.swapaxes(a["gm_b_s"], 1, 2),
        np.reshape(a["w_router"], (L, KD, P, E)).transpose(0, 2, 1, 3).reshape(L, P, KD * E)], axis=2)
    late1 = np.concatenate([
        np.asarray(a["gm_w_s"]).transpose(0, 3, 1, 2).reshape(L, P, GM_G * P),
        rows(a["gm_v_norm_g"]), rows(a["q_norm_g"]), rows(a["k_norm_g"])], axis=2)
    soon2 = np.concatenate([
        columns(a["attn_norm_2"]), columns(a["ffn_norm_2"]), columns(a["mu_shift_2"]), columns(a["decay_base_2"]),
        columns(a["iclr_base_2"]), columns(a["k_k_2"]), columns(a["k_a_2"]), columns(np.reshape(a["r_k_2"], (L, RW))),
        columns(a["lnx_w_2"]), columns(a["lnx_b_2"]), columns(a["q_norm_2"]), columns(a["kv_norm_2"]),
        columns(np.reshape(a["conv_w_2"], (L, 3 * FFN))), columns(a["conv_b_2"])], axis=2)
    late2 = np.concatenate([
        np.concatenate([a["w_decay_up_2"], a["w_iclr_up_2"]], axis=1), np.asarray(a["w_gate_up_2"])], axis=2)
    soon = np.zeros((2 * L + 1, P, SOON), np.float32)
    soon[0:L, :, 0:SOON1], soon[L:2 * L, :, 0:SOON2] = soon1, soon2
    fix = np.concatenate([columns(a["mem_norm_g"]), rows(np.asarray(a["final_norm_g"])[None])[0],
                          rows(np.asarray(a["final_norm_2"])[None])[0]], axis=1)
    return {"soon": soon, "late1": np.ascontiguousarray(late1), "late2": np.ascontiguousarray(late2), "fix": np.ascontiguousarray(fix),
            "consts": constants(),
            "positions": np.ascontiguousarray(np.reshape(a["positions_2"], (NT, P)).T)}


AREA = 18432

GROUPS = {}


def group(name, pre=(), first=(), mid=(), second=(), post=()):
    GROUPS[name] = (pre, first, mid, second, post)


group("inputs", pre=[("inputs_loaded", 80)])
group("soon", pre=[("soon0_loaded", 16)], first=[("soon1_loaded", 16)], second=[("soon2_loaded", 16)])
group("soon_set", first=[("par1_set", 1)], second=[("par2_set", 1)])
group("late", first=[("late1_loaded", 16)], second=[("late2_loaded", 16)])
group("fin", mid=[("fin1_loaded", 16)], post=[("fin2_loaded", 16)])
group("store", post=[("out_stored", 32)])
group("norm_sq", pre=[("m_sq", 2)], first=[("h1_sq", 2), ("v_sq", 2), ("br_sq", 4), ("h2_sq", 2), ("h3_sq", 2)],
      mid=[("f1_sq", 2)], second=[("n1_sq", 2), ("l_sq", 4), ("n2_sq", 2)], post=[("f2_sq", 2)])
group("norm_rstd", pre=[("m_rstd", 1)],
      first=[("h1_rstd", 1), ("v_rstd", 1), ("qk_rstd", 1), ("br_rstd", 1), ("h2_rstd", 1), ("h3_rstd", 1)],
      mid=[("f1_rstd", 1)], second=[("n1_rstd", 1), ("l_rstd", 1), ("n2_rstd", 1)],
      post=[("f2_rstd", 1)])
group("norm_mean", pre=[("m_mean", 1)],
      first=[("h1_mean", 1), ("v_mean", 1), ("qk_mean", 1), ("br_mean", 1), ("h2_mean", 1), ("h3_mean", 1)],
      mid=[("f1_mean", 1)], second=[("n1_mean", 1), ("l_mean", 1), ("n2_mean", 1)],
      post=[("f2_mean", 1)])
group("norm_xn", pre=[("m_xn", 2)], first=[("h1_xn", 2), ("v_norm", 2), ("br_xn", 4), ("h2_xn", 2), ("h3_xn", 2)],
      second=[("n1_xn", 2), ("l_norm", 4), ("n2_xn", 2)])
group("norm_T", pre=[("m_T", 4)], first=[("h1_T", 4), ("br_T", 4), ("h2_T", 4), ("h3_T", 4)],
      second=[("n1_T", 4), ("l_T", 2), ("n2_T", 4)])
group("norm_cols_a", pre=[("m_cols_a", 4)], first=[("h1_cols_a", 4), ("br_cols_a", 4), ("h2_cols_a", 4), ("h3_cols_a", 4)],
      second=[("n1_cols_a", 4), ("l_cols", 3), ("n2_cols_a", KD)])
group("norm_cols_d", pre=[("m_cols_d", 4)], first=[("h1_cols_d", 4), ("br_cols_d", 4), ("h2_cols_d", 4), ("h3_cols_d", 4)],
      second=[("n1_cols_d", 4), ("n2_cols_d", KD)])
group("mix_pe", first=[("uv_full", 4), ("qkv_full", 4), ("mix_full", 2), ("qk_T", 3)])
group("mix_act", first=[("uv_gelu", 4), ("q_cols", 2)])
group("mix_dve", first=[("qkv_rows", 4), ("qk_ss", 1), ("qk_rot", 1), ("k_cols", 1), ("gm_rows", 2 * GM_G)])
group("gqa_pe_scores", first=[("sc_full", 2)], second=[("s2_full", 2)])
group("gqa_pe_turn", first=[("pT_full", 8)], second=[("p2_T", 6)])
group("gqa_pe_out", first=[("at_full", 2)], second=[("o2_full", 2)])
group("gqa_act_exp", first=[("sc_exp", 2 * NQ)], second=[("s2_exp", 2 * MH)])
group("gqa_act_cols", first=[("pT_a", 4)], second=[("p2_cols_a", 3)])
group("gqa_dve_max", first=[("sc_max", 2)], second=[("s2_max", 2)])
group("gqa_dve_cols", first=[("pT_d", 4)], second=[("p2_cols_d", 3)])
group("mla_dve_rows", second=[("p2_rows", 2)])
group("gqa_dve_out", first=[("at_rows", 2)], second=[("o2_cols", 2)])
group("res_pe", first=[("out1_full", 4), ("out2_full", 4)], second=[("out3_full", 4), ("down_full", 4)])
group("res_dve", pre=[("x_start", 1)], first=[("x_mixed", 4), ("x_attended", 4), ("x_routed", 4)],
      mid=[("x_first", 2)], second=[("h_mixed", 4), ("h_ffn", 4)], post=[("y_final", 2)])
group("mem_pe", first=[("xq_full", 4), ("xv_full", 4), ("xs_full", 2), ("xpT_full", 4), ("xo_full", 4)])
group("mem_act", first=[("xq_cols", 4), ("xv_rows", 4), ("xs_exp", NT * XH), ("xpT_a", 2), ("xo_cols_a", 2)])
group("memk_pe", first=[("xk_full", 4)])
group("memk_act", first=[("xk_cols", 4)])
group("mem_dve", first=[("xs_max", 2), ("xp_rows", 2), ("xpT_d", 2), ("xo_cols_d", 2)])
group("route_pe", first=[("router_full", 2), ("aff_T", 1), ("top_T", 1)])
group("route_act", first=[("router_exp", 2)])
group("route_dve", first=[("router_max", 1), ("aff_rows", 1), ("top_found", 1), ("onehot", 3)])
for n in ("tok_full", "gu_full", "gu_T", "acc_full", "tok_cols", "hid_cols", "pick", "gu_rows", "gate_silu",
          "dn_rows_a", "dn_rows_d"):
    group(n, first=[(n, E)])
group("dn_full", first=[("dn_full", 2 * E)])
group("rope_dve", mid=[("rope_ang", 1)])
group("rope_act", mid=[("rope_set", 2)])
for n, c in (("rw_full", 7), ("kk_full", 2), ("lat_full", 2), ("lora_full", 4), ("kk_root", 2), ("kk_sq", 1), ("lat_rows", 2)):
    group(n, second=[(n, c)])
group("rw_act", second=[("rw_scaled", 14), ("lora_in", 1), ("lora_sig", 8), ("decays", 3)])
group("rw_dve", second=[("mu_set", 1), ("rw_cols", 14), ("log_w", 1), ("log_c", 4), ("c_less", 1)])
for n, c in (("pair_in", 5), ("tok_T", 2), ("tok_d", 2), ("tok_a", 1), ("prod_full", 3), ("prod_masked", 7), ("inv_full", 11),
             ("inv_a", 4), ("inv_d", 7), ("u_full", 1), ("u_rows", 1), ("wu_full", 1), ("wu_rows", 1), ("gh_full", 1),
             ("gh_set", 4), ("q_full", 1), ("q_set", 1), ("state_full", NCH - 2), ("state_set", NCH - 2), ("y_full", 1),
             ("y_cols", 1), ("gates_full", 2), ("gates_sig", 2)):
    group(n, second=[(n, c * PAIRS)])
group("gn_pe", second=[("gn_full", 2), ("bonus_full", 2), ("gateup_full", 2), ("var_full", 2)])
group("gn_act", second=[("gateup_in", 1), ("gn_sq", 2), ("gn_root", 2)])
group("gn_dve", second=[("y_mid", 2), ("bonus_in", 1), ("ya_cols", 2)])
group("mla_pe", second=[("q2_full", 4), ("kv2_full", 4), ("qk2_T", 8), ("br2_full", 8), ("merged_T", 4), ("up_full", 2 * NUP), ("dn_half", NF // 2 - 1)])
group("ffn_hi", second=[("w_hi", 2 * NUP + NF // 2)])
group("ffn_lo", second=[("w_lo", 2 * NUP + NF // 2)])
group("mla_act", second=[("q2_rows", 4), ("kv2_rows", 8), ("qk2_cols_a", 4), ("merged_cols_a", 2)])
group("mla_dve", second=[("qk2_rot", 1), ("qk2_cols_d", 4), ("merged", 4), ("merged_cols_d", 2)])
group("ffn_base", second=[("up_base", 2 * NUP)])
group("ffn_gelu", second=[("up_gelu", NUP)])
group("ffn_conv", second=[("up_conv", NUP)])
group("ffn_act", second=[("up_act", NUP)])


class Signals:

    def __init__(self, nc, ctx):
        self.of = {}
        for name, phases in GROUPS.items():
            sem = ctx.enter_context(nc.semaphore(name))
            base = 0
            for i, phase in enumerate(phases):
                per, at = sum(n for _, n in phase), 0
                for signal, n in phase:
                    assert signal not in self.of, signal
                    self.of[signal] = (sem, base, per, at, n)
                    at += n
                base += per * (L if i in (1, 3) else 1)

    def __call__(self, signal):
        return self.of[signal][0]

    def at(self, signal, l, k=None):
        sem, base, per, at, n = self.of[signal]
        k = n if k is None else k
        return sem, l * per + (base + at) + k

    def prev(self, signal, l):
        sem, base, per, at, n = self.of[signal]
        assert at + n == per and base > 0
        return sem, l * per + base


class Memory:

    def __init__(self, nc):
        self.nc = nc


def allocate(nc, ctx):
    m = Memory(nc)

    def sb(name, *shape, dt=F32):
        return ctx.enter_context(nc.sbuf_tensor(name, [P, *shape], dt))

    ring_at = -(-nc.sbuf_base // 32) * 32
    m.ring = sb("ring", SLOTS, SLAB)
    m.x = sb("x", NT, D)
    m.xn = sb("xn", NT, D)
    hT_at = -(-nc.sbuf_base // 32) * 32
    m.hT = sb("hT", KD, T)
    m.con = sb("con", NCONST)
    m.par = sb("par", NPAR)
    m.soon = sb("soon", SOON)
    m.mem_g = sb("mem_g", KD)
    m.stat = sb("stat", 256)
    m.cs2 = sb("cs2", 2, NT, PE_D // 2)
    area_at = -(-nc.sbuf_base // 32) * 32
    m.area = sb("area", AREA)
    m.top_i = sb("top_i", CAP, dt=U32)
    m.pos_i = sb("pos_i", NT, dt=I32)
    m.ps = ctx.enter_context(nc.psum_tensor("ps", [P, 8, BANK], F32))
    m.landed = [ctx.enter_context(nc.semaphore(f"slab_landed{s}")) for s in range(SLOTS)]
    m.free = [ctx.enter_context(nc.semaphore(f"slab_free{s}")) for s in range(SLOTS)]
    m.s = Signals(nc, ctx)
    m.at, m.prev = m.s.at, m.s.prev

    def const(name):
        at, width = CONST_COLS[name]
        return m.con[:, at:at + width]

    m.const = const
    m.ident = const("ident")

    def par(cols, name):
        at, width = cols[name]
        return m.par[:, at:at + width]

    m.par1 = lambda name: par(PAR1, name)
    m.par2 = lambda name: par(PAR2, name)
    used = [0]

    def view(*shape, at=None):
        n = int(np.prod(shape))
        if at is not None:
            used[0] = at
        a = m.area[:, used[0]:used[0] + n]
        used[0] += n
        assert used[0] <= AREA, used[0]
        if len(shape) == 1:
            return a
        names = "abcd"[:len(shape)]
        return a.rearrange(f"p ({' '.join(names)}) -> p {' '.join(names)}", **dict(zip(names[1:], shape[1:])))

    m.memT = view(KD, T, at=0)
    base = used[0]
    m.ug, m.vg = view(NT, GM_W), view(NT, GM_W)
    m.raw = view(NT, 768)
    m.rot, m.kd = view(NT, HEADS_QK, HD), view(NT, NKV, 2, HD)
    m.tmp = view(2, NT * HEADS_QK * HD // 2)
    m.qT, m.kT = view(NQ // 2, T), view(NKV, T)
    m.p, m.pT = view(NQ, T), view(NQ, 2, P)
    m.merged = view(NT, 2 * GM_W)
    m.xkT = view(KD, T, at=16384)
    m.xqT, m.xv = view(KD, T, at=base), view(NT, D)
    m.xp, m.xpT = view(NT, XH, T), view(NT, XH, T)
    m.mem_rows = view(NT, D, at=base)
    m.aff = view(NT, E, at=base)
    m.work = view(2, T)
    m.gates, m.slots = view(CAP), view(CAP)
    m.rep = view(2, 4, CAP)
    m.diag = view(E, CAP)
    m.topc = view(2, E)
    m.onehot = view(NT, E * CAP)
    m.tokT, m.gu, m.sil, m.hid = view(KD, CAP), view(BANK), view(4, 64), view(4, 2, CAP)
    m.pick, m.dn = view(T), view(2, BANK)
    m.R, m.K, m.V = view(PAIRS, T, at=0), view(PAIRS, T), view(PAIRS, T)
    m.wa, m.gg = view(T), view(T)
    m.lat = view(NT, LAT)
    after_lat = used[0]
    m.KK, m.A, m.LW, m.C, m.E1 = (view(PAIRS, T) for _ in range(5))
    m.y = m.KK
    flat = m.xn[:, :, :].rearrange("p t d -> p (t d)")
    m.sq, m.rs = (flat[:, i * D:(i + 1) * D].rearrange("p (a b) -> p a b", b=T) for i in (0, 1))
    m.arp, m.btp, m.ktp, m.vtp = view(NT, 2, P), view(NT, P), view(NT, P), view(NT, P)
    m.rb = flat[:, 0:512].rearrange("p (a t b) -> p a t b", a=2, t=NT)
    m.WU = flat[:, 512:1024].rearrange("p (t w h b) -> p t w h b", t=NT, w=2, h=2)
    m.H = flat[:, 1024:2048].rearrange("p (n b) -> p n b", b=P)
    m.btok, m.kvtok = view(NT, P), view(2, NT, P)
    m.mat = {n: view(2, NT, P) for n in ("D", "DT", "D2", "D2T", "ID", "X", "Arb", "Aak", "Ark")}
    assert used[0] == 16192
    m.G, m.S = view(NCH, P), view(NCH - 2, P)
    m.QT = m.mat["Aak"][:, 0]
    m.yaT = m.V
    mats = 16192 - 9 * 2 * NT * P
    m.qm, m.km, m.vm = view(NT, MH + 1, QKD, at=mats), view(NT, MH, QKD), view(NT, RW)
    m.latT = view(3, T, at=16384)
    m.pm = view(MH, T, at=after_lat)
    m.qmT, m.kmT = view(MH, T), view(MH, T)
    m.pe_tmp = view(4, NT * (MH + 1) * PE_D // 2, at=after_lat + 5 * PAIRS * T)
    m.pmT = m.xn[:, :, :].rearrange("p t (h k b) -> p (t h) k b", k=2, b=P)
    m.o2T = m.K
    m.sg = m.ring[:, SG_SLOT].rearrange("p (t n) -> p t n", t=NT)
    m.m1 = view(2, BANK, at=after_lat)
    m.rope_tmp = view(4, NT * PE_D // 2, at=0)
    m.cb = view(2, 2, T, at=2 * NF * T)
    def over(name, base, at, *shape):
        return nc.alloc_sbuf_tensor_at(name, [P, *shape], F32R, offset=base + 4 * at)

    m.act_hi, m.act_lo = over("act_hi", area_at, 0, NF, T), over("act_lo", area_at, NF * T, NF, T)
    m.hi = over("slab_hi", area_at, 12288, 2, SLAB // 2)
    m.hT_hi = over("hT_hi", area_at, 16384, KD, T)
    m.hT_lo = over("hT_lo", hT_at, 0, KD, T)
    m.ring_lo = over("ring_lo", ring_at, 0, SLOTS, SLAB)
    m.fin1 = view(D, at=12288)
    m.fin2 = m.hT[:, 0:4, :].rearrange("p k n -> p (k n)")
    return m


def slab(m, slot, k, n):
    return m.ring[:, slot, 0:k * n].rearrange("p (k n) -> p k n", n=n)


def high(m, act, q, src):
    return m.nc.scalar.activation(m.hi[:, q % 2, 0:src.shape[1]], src, ACT.Copy)


def low(m, dve, q, dst, src):
    return m.nc.vector.tensor_tensor(dst, src, m.hi[:, q % 2, 0:src.shape[1]], ALU.subtract)


def exact(m, out, lhs, rhs, start, stop):
    for i, (a, b) in enumerate(((0, 0), (0, 1), (1, 0))):
        ins = m.nc.tensor.matmul(out, lhs[a], rhs[b], start=start and i == 0, stop=stop and i == 2)
        if i == 0:
            first = ins
    return first, ins


def act_squares(m, act, src, junk, sums, scale, done):
    for s, j, c in zip(src, junk, sums):
        m.nc.scalar.activation(j, s, ACT.Square, scale=scale, accum_out=c).then_inc(done, 1)


def pe_columns(m, src, full):
    for b in range(4):
        for k in range(2):
            for t in range(NT):
                ins = m.nc.tensor.transpose(m.ps[:, b, k * T + t * P:k * T + (t + 1) * P],
                                            src[:, t, (2 * b + k) * P:(2 * b + k + 1) * P], m.ident)
        ins.then_inc(full, 1)


def act_columns(m, act, dst, gain, full, base, done):
    for b in (0, 1):
        act.wait_ge(full, base + b + 1)
        for k in (2 * b, 2 * b + 1):
            m.nc.scalar.activation(dst[:, k, :], m.ps[:, b, (k % 2) * T:(k % 2 + 1) * T], ACT.Copy,
                                   scale=gain[:, k:k + 1]).then_inc(done, 1)


def dve_columns(m, dve, dst, gain, full, base, done):
    for b in (2, 3):
        dve.wait_ge(full, base + b + 1)
        for k in (2 * b, 2 * b + 1):
            m.nc.vector.tensor_scalar(dst[:, k, :], m.ps[:, b, (k % 2) * T:(k % 2 + 1) * T], gain[:, k:k + 1], None,
                                      ALU.mult).then_inc(done, 1)


def dve_scale_rows(m, dst, src, rstd, done):
    for t in range(NT):
        m.nc.vector.tensor_scalar(dst[:, t, :], src[:, t, :], rstd[:, t:t + 1], None, ALU.mult).then_inc(done, 1)


def pe_rows(m, pe, out, lhs, w, ks, k0, start, stop):
    ins = None
    for t in range(NT):
        for i, k in enumerate(ks):
            ins = m.nc.tensor.matmul(out[t], lhs[:, k, t * P:(t + 1) * P], w[:, k - k0, :],
                                     start=start and i == 0, stop=stop and i == len(ks) - 1)
    return ins


def pe_cols(m, out, w, c, rhs, ks):
    ins = None
    for i, k in enumerate(ks):
        ins = m.nc.tensor.matmul(out, w[:, k, c:c + P], rhs[:, k, :], start=i == 0, stop=i == len(ks) - 1)
    return ins


def sync_start(m, sp):
    done = m.s("inputs_loaded")
    sp.dma_start(m.con[:, :], m.d["consts"]).then_inc(done, 16)
    sp.dma_start(m.mem_g[:, :], m.d["fix"][:, 0:KD]).then_inc(done, 16)
    sp.dma_start(m.pos_i[:, :], m.d["positions"]).then_inc(done, 16)
    sp.dma_start(m.mem_rows, m.d["mem"].rearrange("b (t p) d -> p (b t) d", p=P)).then_inc(done, 16)
    sp.dma_start(m.x[:, :, :], m.d["x"].rearrange("b (t p) d -> p (b t) d", p=P)).then_inc(done, 16)
    for s in range(SLOTS):
        sp.sem_inc(m.free[s], 1)


def scalar_start(m, act):
    act.wait_ge(*m.at("inputs_loaded", 0))
    act_squares(m, act, [m.mem_rows[:, t, :] for t in range(NT)], [m.xn[:, t, :] for t in range(NT)],
                [m.stat[:, t:t + 1] for t in range(NT)], D ** -0.5, m.s("m_sq"))
    act_columns(m, act, m.memT, m.mem_g, *m.at("m_T", 0, 0), m.s("m_cols_a"))


def gpsimd_rstd(m, pool, l, name, squares, c, width, eps):
    at = CONST_COLS["eps"][0] + eps
    out = m.stat[:, 64 + c:64 + c + width]
    pool.wait_ge(*m.at(squares, l))
    m.nc.gpsimd.tensor_tensor(out, m.stat[:, c:c + width], m.con[:, at:at + width], ALU.add).then_inc(m.s(name + "_mean"), 1)
    pool.wait_ge(*m.at(name + "_mean", l))
    m.nc.gpsimd.tensor_tensor(out, out, m.const("neg_half").to_broadcast([P, width]), ALU.pow).then_inc(m.s(name + "_rstd"), 1)


def gpsimd_start(m, pool):
    pool.dma_start(m.soon[:, :], m.d["soon"][0]).then_inc(m.s("soon0_loaded"), 16)
    gpsimd_rstd(m, pool, 0, "m", "m_sq", 0, NT, 0)


def vector_start(m, dve):
    dve.wait_ge(*m.at("m_rstd", 0))
    dve_scale_rows(m, m.xn, m.mem_rows, m.stat[:, 64:66], m.s("m_xn"))
    dve_columns(m, dve, m.memT, m.mem_g, *m.at("m_T", 0, 0), m.s("m_cols_d"))
    m.nc.vector.memset(m.stat[:, 255:256], 0.0).then_inc(m.s("x_start"), 1)


def tensor_start(m, pe):
    pe.wait_ge(*m.at("m_xn", 0))
    pe_columns(m, m.xn, m.s("m_T"))


def ring_wait(m, eng, slot, held):
    eng.wait_ge(m.free[slot], held + 1)


def sync_first(m, sp, l):
    d = m.d

    def load(i, dst, src):
        g = PLAN1[i]
        ring_wait(m, sp, g.slot, l * HELD1_LAYER[g.slot] + g.held)
        sp.dma_start(dst, src).then_inc(m.landed[g.slot], 16)

    def layer(w):
        return w[bass.ds(l, 1)].rearrange("l (k p) n -> p (l k) n", p=P)

    def whole(i, w, c0, n):
        load(i, slab(m, PLAN1[i].slot, KD, n), layer(w)[:, :, c0:c0 + n])

    def half(i, w, nh, kh):
        load(i, slab(m, PLAN1[i].slot, 4, BANK), layer(w)[:, 4 * kh:4 * kh + 4, nh * BANK:(nh + 1) * BANK])

    for j in range(4):
        whole(W_IN1 + j, d["w_in"], j * BANK, min(BANK, 1792 - j * BANK))
    for j in range(2):
        whole(W_XK + j, d["xattn_w_kv"], j * BANK, BANK)
    for j in range(4):
        half(W_OUT1 + j, d["w_out"], j // 2, j % 2)
    for j in range(2):
        whole(W_XQ + j, d["xattn_w_q"], j * BANK, BANK)
    for j in range(2):
        whole(W_XV + j, d["xattn_w_kv"], D + j * BANK, BANK)
    for j in range(4):
        half(W_XO + j, d["xattn_w_o"], j // 2, j % 2)
    with sp.Fori(0, E) as e:
        for s, (name, n) in enumerate((("w_gate", 0), ("w_gate", 1), ("w_up", 0), ("w_up", 1), ("w_down", 0), ("w_down", 1))):
            ring_wait(m, sp, s, l * HELD1_LAYER[s] + e + HELD1[s])
            w = d[name].rearrange("l e (k p) n -> (l e) p k n", p=P)[bass.ds(l * E + e, 1)]
            sp.dma_start(slab(m, s, KD, BANK), w[:, :, :, n * BANK:(n + 1) * BANK].rearrange("o p k n -> p (o k) n"))\
              .then_inc(m.landed[s], 16)


def landed1(m, pe, l, i):
    g = PLAN1[i]
    pe.wait_ge(m.landed[g.slot], l * LANDED1_LAYER[g.slot] + g.landed)


def tensor_first(m, pe, l):
    nc, ps, at = m.nc, m.ps, m.at
    mm = nc.tensor.matmul

    def weights(i, k=KD, n=BANK):
        landed1(m, pe, l, i)
        return slab(m, PLAN1[i].slot, k, n)

    def used(i):
        return m.free[PLAN1[i].slot]

    def columns_of(src, ready, T_full, a, dcols):
        pe.wait_ge(*at(ready, l))
        pe_columns(m, src, m.s(T_full))
        pe.wait_ge(*at(a, l))
        pe.wait_ge(*at(dcols, l))

    def into_residual(first, full):
        for j in range(4):
            w = weights(first + j, 4)
            nh, kh = j // 2, j % 2
            for t in range(NT):
                for k in range(4):
                    ins = mm(ps[:, 4 + 2 * nh + t, :], m.hT[:, 4 * kh + k, t * P:(t + 1) * P], w[:, k, :],
                             start=kh == 0 and k == 0, stop=kh == 1 and k == 3)
                if kh == 1 and t == 0:
                    ins.then_inc(m.s(full), 1)
                if kh == 0 and t == NT - 1:
                    ins.then_inc(used(first + j), 1)
            if kh == 1:
                ins.then_inc(m.s(full), 1)
                release.append(first + j)

    release = []

    def free_released(ins):
        ins.then_inc(used(release.pop()), 1)

    def tile_columns(out, w, c, rhs):
        for k in range(KD):
            ins = mm(out, w[:, k, c * P:(c + 1) * P], rhs[:, k, :], start=k == 0, stop=k == KD - 1)
            if k == 0 and release:
                free_released(ins)
        return ins

    def memory_keys(b):
        w = weights(W_XK + b // 2)
        for i in range(2):
            ins = tile_columns(ps[:, (1, 2, 5, 3)[b], i * T:(i + 1) * T], w, 2 * (b % 2) + i, m.memT)
        ins.then_inc(m.s("xk_full"), 1)
        if b % 2:
            release.append(W_XK + b // 2)

    columns_of(m.xn, "h1_xn", "h1_T", "h1_cols_a", "h1_cols_d")
    for j in range(4):
        n = 256 if j == 3 else BANK
        w = weights(W_IN1 + j, KD, n)
        for t in range(NT):
            b = (4, 6, 0, 2)[j] + t
            for k in range(KD):
                ins = mm(ps[:, b, 0:n], m.hT[:, k, t * P:(t + 1) * P], w[:, k, :], start=k == 0, stop=k == KD - 1)
                if t == 0 and k == 0 and release:
                    free_released(ins)
            ins.then_inc(m.s("uv_full" if j < 2 else "qkv_full"), 1)
        release.append(W_IN1 + j)
    pe.wait_ge(*at("v_norm", l))
    pe.wait_ge(*at("uv_gelu", l))
    w_s = m.par1("w_s")
    for t in range(NT):
        for g in range(GM_G):
            ins = mm(ps[:, 4 + t, g * P:(g + 1) * P], w_s[:, g * P:(g + 1) * P], m.vg[:, t, g * P:(g + 1) * P],
                     start=True, stop=True)
            if release:
                free_released(ins)
        ins.then_inc(m.s("mix_full"), 1)
    pe.wait_ge(*at("qkv_rows", l))
    memory_keys(0)
    memory_keys(1)
    pe.wait_ge(*at("qk_rot", l))
    for b in range(3):
        for i in range(2):
            for t in range(NT):
                if b < 2:
                    h = 2 * (2 * b + i)
                    src = m.rot[:, t, h:h + 2, :].rearrange("p a b -> p (a b)")
                else:
                    src = m.kd[:, t, i].rearrange("p a b -> p (a b)")
                ins = nc.tensor.transpose(ps[:, (6, 7, 0)[b], i * T + t * P:i * T + (t + 1) * P], src, m.ident)
        ins.then_inc(m.s("qk_T"), 1)
    pe.wait_ge(*at("q_cols", l))
    pe.wait_ge(*at("k_cols", l))
    pe.wait_ge(*at("xk_cols", l, 2))
    for t in range(NT):
        if t == 1:
            pe.wait_ge(*at("gm_rows", l))
        for h in range(NQ):
            r = (h % 2) * HD
            ins = mm(ps[:, 4 * t + 2 * (h % 2) + h // 4, (h // 2 % 2) * T:(h // 2 % 2 + 1) * T],
                     m.qT[r:r + HD, h // 2, t * P:(t + 1) * P], m.kT[r:r + HD, h // 4, :], start=True, stop=True)
        ins.then_inc(m.s("sc_full"), 1)
    for t in range(NT):
        pe.wait_ge(*at("sc_exp", l, NQ * (t + 1)))
        for b in range(4):
            for j in (2 * b, 2 * b + 1):
                for kt in range(2):
                    ins = nc.tensor.transpose(ps[:, 4 * t + b, (j % 2) * T + kt * P:(j % 2) * T + (kt + 1) * P],
                                              m.p[:, j, kt * P:(kt + 1) * P], m.ident)
            ins.then_inc(m.s("pT_full"), 1)
        pe.wait_ge(*at("pT_a", l, 2 * (t + 1)))
        pe.wait_ge(*at("pT_d", l, 2 * (t + 1)))
        for j in range(NQ):
            h = 4 * (j // 2 % 2) + 2 * (j % 2) + j // 4
            for kt in range(2):
                c = NQ * HD + NKV * HD + (h // 4) * HD
                ins = mm(ps[:, 4 * t, h * HD:(h + 1) * HD], m.pT[:, j, kt, :], m.raw[:, kt, c:c + HD],
                         start=kt == 0, stop=kt == 1)
        ins.then_inc(m.s("at_full"), 1)
    memory_keys(2)
    columns_of(m.xn, "br_xn", "br_T", "br_cols_a", "br_cols_d")
    pe.wait_ge(*at("xk_cols", l, 3))
    into_residual(W_OUT1, "out1_full")

    memory_keys(3)
    pe.wait_ge(*at("xk_cols", l))
    columns_of(m.xn, "h2_xn", "h2_T", "h2_cols_a", "h2_cols_d")
    for j in range(2):
        w = weights(W_XQ + j)
        for c in range(4):
            ins = tile_columns(ps[:, 4 + 2 * j + c // 2, (c % 2) * T:(c % 2 + 1) * T], w, c, m.hT)
            if c % 2:
                ins.then_inc(m.s("xq_full"), 1)
        release.append(W_XQ + j)
    for j in range(2):
        w = weights(W_XV + j)
        for t in range(NT):
            for k in range(KD):
                ins = mm(ps[:, 2 * j + t, :], m.memT[:, k, t * P:(t + 1) * P], w[:, k, :], start=k == 0, stop=k == KD - 1)
                if k == 0 and release:
                    free_released(ins)
            ins.then_inc(m.s("xv_full"), 1)
        release.append(W_XV + j)
    pe.wait_ge(*at("xv_rows", l))
    pe.wait_ge(*at("xq_cols", l))
    for t in range(NT):
        for h in range(XH):
            for k in range(2):
                ins = mm(ps[:, 2 * t + h // 2, (h % 2) * T:(h % 2 + 1) * T], m.xqT[:, 2 * h + k, t * P:(t + 1) * P],
                         m.xkT[:, 2 * h + k, :], start=k == 0, stop=k == 1)
                if release:
                    free_released(ins)
        ins.then_inc(m.s("xs_full"), 1)
    pe.wait_ge(*at("xp_rows", l))
    for b in range(4):
        mt = b // 2
        for i in range(2):
            for t in range(NT):
                ins = nc.tensor.transpose(ps[:, 4 + b, i * T + t * P:i * T + (t + 1) * P],
                                          m.xp[:, t, 2 * (b % 2) + i, mt * P:(mt + 1) * P], m.ident)
        ins.then_inc(m.s("xpT_full"), 1)
    pe.wait_ge(*at("xpT_a", l))
    pe.wait_ge(*at("xpT_d", l))
    for c in range(KD):
        h = c // 2
        for mt in range(2):
            ins = mm(ps[:, c // 2, (c % 2) * T:(c % 2 + 1) * T], m.xv[:, mt, c * P:(c + 1) * P], m.xpT[:, mt, h, :],
                     start=mt == 0, stop=mt == 1)
        if c % 2:
            ins.then_inc(m.s("xo_full"), 1)
    pe.wait_ge(*at("xo_cols_a", l))
    pe.wait_ge(*at("xo_cols_d", l))
    into_residual(W_XO, "out2_full")
    tensor_experts(m, pe, l, release, free_released, columns_of)


def tensor_experts(m, pe, l, release, free_released, columns_of):
    nc, ps, at = m.nc, m.ps, m.at
    mm = nc.tensor.matmul
    columns_of(m.xn, "h3_xn", "h3_T", "h3_cols_a", "h3_cols_d")
    router = m.par1("router").rearrange("p (k e) -> p k e", e=E)
    for t in range(NT):
        for k in range(KD):
            ins = mm(ps[:, 4 + t, 0:E], m.hT[:, k, t * P:(t + 1) * P], router[:, k, :], start=k == 0, stop=k == KD - 1)
            if release:
                free_released(ins)
        ins.then_inc(m.s("router_full"), 1)
    pe.wait_ge(*at("aff_rows", l))
    for t in range(NT):
        ins = nc.tensor.transpose(ps[0:E, 6, t * P:(t + 1) * P], m.aff[:, t, :], m.ident)
    ins.then_inc(m.s("aff_T"), 1)
    pe.wait_ge(*at("top_found", l))
    mm(ps[:, 7, 0:E * CAP], m.const("ones")[0:E, :], m.diag[0:E].rearrange("p e c -> p (e c)"), start=True, stop=True)
    for i in range(2):
        ins = nc.tensor.transpose(ps[:, 6, i * E:(i + 1) * E], m.rep[0:E, i].rearrange("p g c -> p (g c)"), m.ident[0:E, 0:E])
    ins.then_inc(m.s("top_T"), 1)
    pe.wait_ge(*at("onehot", l))
    pe.wait_ge(*at("router_exp", l))
    for nh in range(2):
        for t in range(NT):
            mm(ps[:, 4 + 2 * nh + t, :], m.ident, m.x[:, t, nh * BANK:(nh + 1) * BANK], start=True, stop=False,
               skip_group_check=True)
    w = [slab(m, s, KD, BANK) for s in range(SLOTS)]
    with pe.Fori(0, E) as e:
        n = e + l * E + 1

        def slab_landed(s):
            pe.wait_ge(m.landed[s], l * LANDED1_LAYER[s] + LANDED1[s] + 16 + e * 16)

        for k in range(KD):
            for t in range(NT):
                ins = mm(ps[:, 0, k * CAP:(k + 1) * CAP], m.xn[:, t, k * P:(k + 1) * P], m.onehot[:, t, bass.ds(e * CAP, CAP)],
                         start=t == 0, stop=t == NT - 1)
        ins.then_inc(m.s("tok_full"), 1)
        pe.wait_ge(m.s("tok_cols"), n)
        for k in range(KD):
            for g in range(4):
                if k == 0:
                    slab_landed(g)
                ins = mm(ps[32 * g:32 * g + CAP, 1, :], m.tokT[:, k, :], w[g][:, k, :], start=k == 0, stop=k == KD - 1)
                if k == KD - 1:
                    ins.then_inc(m.free[g] if g < 3 else m.s("gu_full"), 1)
        pe.wait_ge(m.s("gu_rows"), n)
        for c in range(4):
            ins = nc.tensor.transpose(ps[:, 0, c * P:(c + 1) * P], m.gu[:, c * P:(c + 1) * P], m.ident)
            if c == 0:
                ins.then_inc(m.free[3], 1)
        ins.then_inc(m.s("gu_T"), 1)
        pe.wait_ge(m.s("hid_cols"), n)
        for nh in range(2):
            slab_landed(4 + nh)
            for k in range(KD):
                c, half = k % 4, k // 4
                ins = mm(ps[32 * c:32 * c + CAP, 2 + nh, :], m.hid[:, c, half, :], w[4 + nh][:, k, :],
                         start=half == 0, stop=half == 1)
                if nh == 1 and k == 0:
                    ins.then_inc(m.free[4], 1)
            ins.then_inc(m.s("dn_full"), 1)
        pe.wait_ge(m.s("pick"), n)
        for nh in range(2):
            pe.wait_ge(m.s("dn_rows_a" if nh == 0 else "dn_rows_d"), n)
            for t in range(NT):
                ins = mm(ps[:, 4 + 2 * nh + t, :], m.pick[:, t * P:(t + 1) * P], m.dn[:, nh, :], start=False, stop=True,
                         skip_group_check=True)
                if nh == 0 and t == 0:
                    ins.then_inc(m.free[5], 1)
        ins.then_inc(m.s("acc_full"), 1)


def norm_squares(m, act, x_ready, done):
    act.wait_ge(*x_ready)
    act_squares(m, act, [m.x[:, t, :] for t in range(NT)], [m.xn[:, t, :] for t in range(NT)],
                [m.stat[:, t:t + 1] for t in range(NT)], D ** -0.5, done)


def two(bank):
    return bank.rearrange("p (a b) -> p a b", b=T)


S_MAX, S_SUM, S_INV = 128, 144, 160
S_XMAX, S_XSUM, S_XINV = 176, 184, 192
S_RMAX, S_RSUM, S_RINV = 200, 202, 204


def scalar_first(m, act, l):
    nc, ps, at, s = m.nc, m.ps, m.at, m.s
    go = nc.scalar.activation
    col = lambda c: m.stat[:, c:c + 1]

    def memory_keys(b):
        act.wait_ge(*at("xk_full", l, b + 1))
        go(m.xkT[:, 2 * b:2 * b + 2, :], two(ps[:, (1, 2, 5, 3)[b], :]), ACT.Copy).then_inc(s("xk_cols"), 1)

    norm_squares(m, act, m.prev("x_routed", l), s("h1_sq"))
    act.wait_ge(*at("par1_set", l))
    act_columns(m, act, m.hT, m.par1("mix_g"), *at("h1_T", l, 0), s("h1_cols_a"))
    for i in range(4):
        act.wait_ge(*at("uv_full", l, i + 1))
        go((m.ug, m.vg)[i // 2][:, i % 2, :], ps[:, 4 + i, :], ACT.Gelu_apprx_tanh).then_inc(s("uv_gelu"), 1)
    act.wait_ge(*at("uv_gelu", l))
    act_squares(m, act, [m.vg[:, t, :] for t in range(NT)], [m.xn[:, t, 0:GM_W] for t in range(NT)],
                [col(4 + t) for t in range(NT)], GM_W ** -0.5, s("v_sq"))
    memory_keys(0)
    memory_keys(1)
    for b in range(2):
        act.wait_ge(*at("qk_T", l, b + 1))
        go(m.qT[:, 2 * b:2 * b + 2, :], two(ps[:, 6 + b, :]), ACT.Copy).then_inc(s("q_cols"), 1)
    for t in range(NT):
        act.wait_ge(*at("sc_max", l, t + 1))
        if t:
            act.wait_ge(*at("pT_full", l, 4 * t))
        for j in range(NQ):
            h = 4 * (j // 2 % 2) + 2 * (j % 2) + j // 4
            go(m.p[:, j, :], two(ps[:, 4 * t + j // 2, :])[:, j % 2, :], ACT.Exp, bias=col(S_MAX + NQ * t + j),
               scale=HD ** 0.5, accum_out=col(S_SUM + NQ * t + h)).then_inc(s("sc_exp"), 1)
        if t:
            act.wait_ge(*at("at_full", l, t))
        for b in range(2):
            act.wait_ge(*at("pT_full", l, 4 * t + b + 1))
            go(m.pT[:, 2 * b:2 * b + 2], ps[:, 4 * t + b, :].rearrange("p (a k b) -> p a k b", a=2, b=P), ACT.Copy)\
                .then_inc(s("pT_a"), 1)
    for t in range(NT):
        act.wait_ge(*at("at_rows", l, t + 1))
        for br in range(2):
            part = slice(br * GM_W, (br + 1) * GM_W)
            go(m.xn[:, t, part], m.merged[:, t, part], ACT.Square, scale=GM_W ** -0.5,
               accum_out=col(6 + 2 * t + br)).then_inc(s("br_sq"), 1)
    memory_keys(2)
    act_columns(m, act, m.hT, m.par1("branch_g"), *at("br_T", l, 0), s("br_cols_a"))
    norm_squares(m, act, at("x_mixed", l), s("h2_sq"))
    memory_keys(3)
    act_columns(m, act, m.hT, m.par1("x_g"), *at("h2_T", l, 0), s("h2_cols_a"))
    for b in range(4):
        act.wait_ge(*at("xq_full", l, b + 1))
        go(m.xqT[:, 2 * b:2 * b + 2, :], two(ps[:, 4 + b, :]), ACT.Copy).then_inc(s("xq_cols"), 1)
    for i in range(4):
        act.wait_ge(*at("xv_full", l, i + 1))
        go(m.xv[:, i % 2, (i // 2) * BANK:(i // 2 + 1) * BANK], ps[:, i, :], ACT.Copy).then_inc(s("xv_rows"), 1)
    for t in range(NT):
        act.wait_ge(*at("xs_max", l, t + 1))
        for h in range(XH):
            go(m.xp[:, t, h, :], two(ps[:, 2 * t + h // 2, :])[:, h % 2, :], ACT.Exp, bias=col(S_XMAX + XH * t + h),
               scale=XD ** -0.5, accum_out=col(S_XSUM + XH * t + h)).then_inc(s("xs_exp"), 1)
    for b in range(2):
        act.wait_ge(*at("xpT_full", l, b + 1))
        go(m.xpT[:, 0, 2 * b:2 * b + 2, :], two(ps[:, 4 + b, :]), ACT.Copy).then_inc(s("xpT_a"), 1)
    for b in range(2):
        act.wait_ge(*at("xo_full", l, b + 1))
        go(m.hT[:, 2 * b:2 * b + 2, :], two(ps[:, b, :]), ACT.Copy).then_inc(s("xo_cols_a"), 1)
    norm_squares(m, act, at("x_attended", l), s("h3_sq"))
    act_columns(m, act, m.hT, m.par1("ffn_g"), *at("h3_T", l, 0), s("h3_cols_a"))
    act.wait_ge(*at("router_max", l))
    for t in range(NT):
        go(m.aff[:, t, :], ps[:, 4 + t, 0:E], ACT.Exp, bias=col(S_RMAX + t), accum_out=col(S_RSUM + t)).then_inc(s("router_exp"), 1)
    gate = ps[:, 0, :].rearrange("p (c n) -> p c n", n=P)[:, :, 0:2 * CAP]
    with act.Fori(0, E) as e:
        n = e + l * E + 1
        act.wait_ge(s("gu_full"), n)
        go(m.gu, ps[:, 1, :], ACT.Copy).then_inc(s("gu_rows"), 1)
        act.wait_ge(s("gu_T"), n)
        go(m.sil, gate, ACT.Silu).then_inc(s("gate_silu"), 1)
        act.wait_ge(s("dn_full"), 2 * n - 1)
        go(m.dn[:, 0, :], ps[:, 2, :], ACT.Copy).then_inc(s("dn_rows_a"), 1)


def gpsimd_first(m, pool, l):
    at, s = m.at, m.s
    pool.wait_ge(*m.prev("x_routed", l))
    pool.dma_start(m.par[:, SOON:SOON + NLATE1], m.d["late1"][bass.ds(l, 1)].rearrange("l p n -> p (l n)"))\
        .then_inc(s("late1_loaded"), 16)
    gpsimd_rstd(m, pool, l, "h1", "h1_sq", 0, NT, 0)
    gpsimd_rstd(m, pool, l, "v", "v_sq", 4, NT, 0)
    gpsimd_rstd(m, pool, l, "qk", "qk_ss", 32, NT * HEADS_QK, 32)
    gpsimd_rstd(m, pool, l, "br", "br_sq", 6, 2 * NT, 0)
    gpsimd_rstd(m, pool, l, "h2", "h2_sq", 0, NT, 0)
    gpsimd_rstd(m, pool, l, "h3", "h3_sq", 0, NT, 0)
    pool.dma_start(m.soon[:, :], m.d["soon"][bass.ds(l + 1, 1)].rearrange("l p n -> p (l n)")).then_inc(s("soon1_loaded"), 16)


def add_into_x(m, dve, full, base, done):
    for i in range(4):
        nh, t = i // 2, i % 2
        dve.wait_ge(full, base + i + 1)
        xs = m.x[:, t, nh * BANK:(nh + 1) * BANK]
        m.nc.vector.tensor_tensor(xs, xs, m.ps[:, 4 + i, :], ALU.add).then_inc(done, 1)


def bc(ap, n):
    return ap.unsqueeze(len(ap.shape)).to_broadcast([*ap.shape, n])


def vector_norm(m, dve, l, name, gain):
    dve.wait_ge(*m.at(name + "_rstd", l))
    dve_scale_rows(m, m.xn, m.x, m.stat[:, 64:66], m.s(name + "_xn"))
    dve_columns(m, dve, m.hT, gain, *m.at(name + "_T", l, 0), m.s(name + "_cols_d"))


def vector_first(m, dve, l):
    vector_mix(m, dve, l)
    vector_memory(m, dve, l)
    vector_route(m, dve, l)
    vector_experts(m, dve, l)


def vector_set_par(m, dve, l, loaded, done):
    dve.wait_ge(*m.prev(loaded, l))
    m.nc.vector.tensor_copy(m.par[:, 0:SOON], m.soon[:, :]).then_inc(m.s(done), 1)
    dve.wait_ge(*m.at(done, l))


def vector_mix(m, dve, l):
    v, ps, at, s = m.nc.vector, m.ps, m.at, m.s
    vector_set_par(m, dve, l, "soon1_loaded", "par1_set")
    vector_norm(m, dve, l, "h1", m.par1("mix_g"))
    dve.wait_ge(*at("late1_loaded", l))
    dve.wait_ge(*at("v_rstd", l))
    for t in range(NT):
        v.scalar_tensor_tensor(m.vg[:, t, :], m.vg[:, t, :], m.stat[:, 68 + t:69 + t], m.par1("v_g"), ALU.mult, ALU.mult)\
            .then_inc(s("v_norm"), 1)
    for i in range(4):
        dve.wait_ge(*at("qkv_full", l, i + 1))
        if i < 2:
            v.tensor_copy(m.raw[:, i, 0:BANK], ps[:, i, :]).then_inc(s("qkv_rows"), 1)
        else:
            v.tensor_copy(m.raw[:, i - 2, BANK:768], ps[:, i, 0:256]).then_inc(s("qkv_rows"), 1)
    qk = m.raw[:, :, 0:HEADS_QK * HD]
    heads = m.raw.rearrange("p t (h d) -> p t h d", d=HD)[:, :, 0:HEADS_QK, :]
    dve.wait_ge(*at("qkv_rows", l))
    v.tensor_tensor(m.rot.rearrange("p t h d -> p t (h d)"), qk, qk, ALU.mult)
    dve.drain()
    ss = m.stat[:, 32:32 + NT * HEADS_QK].rearrange("p (t h) -> p t h", t=NT)
    v.tensor_reduce(ss, m.rot, axis=AX.X, op=ALU.add).then_inc(s("qk_ss"), 1)
    dve.wait_ge(*at("qk_rstd", l))
    rstd = m.stat[:, 96:96 + NT * HEADS_QK].rearrange("p (t h) -> p t h", t=NT)
    v.tensor_tensor(heads, heads, bc(rstd, HD), ALU.mult)
    dve.drain()
    for h0, h1, g in ((0, NQ, 0), (NQ, HEADS_QK, 1)):
        gain = m.par1("qk_g")[:, g * HD:(g + 1) * HD].unsqueeze(1).unsqueeze(1).to_broadcast([P, NT, h1 - h0, HD])
        v.tensor_tensor(heads[:, :, h0:h1], heads[:, :, h0:h1], gain, ALU.mult)
    dve.drain()
    pairs = m.raw.rearrange("p t (h i two) -> p t h i two", i=HD // 2, two=2)[:, :, 0:HEADS_QK]
    rot = m.rot.rearrange("p t h (i two) -> p t h i two", two=2)
    cos, sin = (m.const(n).rearrange("p (t i) -> p t i", t=NT) for n in ("cos1", "sin1"))
    t0, t1 = (m.tmp[:, i].rearrange("p (t h i) -> p t h i", t=NT, h=HEADS_QK) for i in range(2))
    for t in range(NT):
        c, sn = (a[:, t].unsqueeze(1).to_broadcast([P, HEADS_QK, HD // 2]) for a in (cos, sin))
        v.tensor_tensor(rot[:, t, :, :, 0], pairs[:, t, :, :, 0], c, ALU.mult)
        v.tensor_tensor(rot[:, t, :, :, 1], pairs[:, t, :, :, 0], sn, ALU.mult)
        v.tensor_tensor(t0[:, t], pairs[:, t, :, :, 1], sn, ALU.mult)
        v.tensor_tensor(t1[:, t], pairs[:, t, :, :, 1], c, ALU.mult)
    dve.drain()
    for t in range(NT):
        v.tensor_tensor(rot[:, t, :, :, 0], rot[:, t, :, :, 0], t0[:, t], ALU.subtract)
        v.tensor_tensor(rot[:, t, :, :, 1], rot[:, t, :, :, 1], t1[:, t], ALU.add)
    dve.drain()
    for t in range(NT):
        ins = v.tensor_copy(m.kd[:, t], m.rot[:, t, NQ:, :].unsqueeze(2).to_broadcast([P, NKV, 2, HD]))
    ins.then_inc(s("qk_rot"), 1)
    dve.wait_ge(*at("qk_T", l))
    v.tensor_copy(m.kT, two(ps[:, 0, :])).then_inc(s("k_cols"), 1)
    for t in range(NT):
        dve.wait_ge(*at("mix_full", l, t + 1))
        for g in range(GM_G):
            part = slice(g * P, (g + 1) * P)
            v.scalar_tensor_tensor(m.merged[:, t, part], ps[:, 4 + t, part], m.par1("b_s")[:, g:g + 1], m.ug[:, t, part],
                                   ALU.add, ALU.mult).then_inc(s("gm_rows"), 1)
    for t in range(NT):
        dve.wait_ge(*at("sc_full", l, t + 1))
        mx = m.stat[:, S_MAX + NQ * t:S_MAX + NQ * (t + 1)]
        v.tensor_reduce(mx, ps[:, 4 * t:4 * t + 4, :].rearrange("p b (j n) -> p (b j) n", n=T), axis=AX.X, op=ALU.max)
        dve.drain()
        v.tensor_scalar(mx, mx, -HD ** 0.5, None, ALU.mult).then_inc(s("sc_max"), 1)
    for t in range(NT):
        if t:
            dve.wait_ge(*at("at_full", l, t))
        for b in (2, 3):
            dve.wait_ge(*at("pT_full", l, 4 * t + b + 1))
            v.tensor_copy(m.pT[:, 2 * b:2 * b + 2], ps[:, 4 * t + b, :].rearrange("p (a k b) -> p a k b", a=2, b=P))\
                .then_inc(s("pT_d"), 1)
        inv = m.stat[:, S_INV + NQ * t:S_INV + NQ * (t + 1)]
        dve.wait_ge(*at("sc_exp", l, NQ * (t + 1)))
        v.reciprocal(inv, m.stat[:, S_SUM + NQ * t:S_SUM + NQ * (t + 1)])
        dve.drain()
        dve.wait_ge(*at("at_full", l, t + 1))
        v.tensor_tensor(m.merged[:, t, GM_W:].rearrange("p (h d) -> p h d", d=HD),
                        ps[:, 4 * t, :].rearrange("p (h d) -> p h d", d=HD), bc(inv, HD), ALU.mult).then_inc(s("at_rows"), 1)
    dve.wait_ge(*at("br_rstd", l))
    for t in range(NT):
        for br in range(2):
            part = slice(br * GM_W, (br + 1) * GM_W)
            c = 70 + 2 * t + br
            v.tensor_scalar(m.xn[:, t, part], m.merged[:, t, part], m.stat[:, c:c + 1], None, ALU.mult).then_inc(s("br_xn"), 1)
    dve_columns(m, dve, m.hT, m.par1("branch_g"), *at("br_T", l, 0), s("br_cols_d"))
    add_into_x(m, dve, *at("out1_full", l, 0), s("x_mixed"))


def vector_memory(m, dve, l):
    v, ps, at, s = m.nc.vector, m.ps, m.at, m.s
    vector_norm(m, dve, l, "h2", m.par1("x_g"))
    for t in range(NT):
        dve.wait_ge(*at("xs_full", l, t + 1))
        mx = m.stat[:, S_XMAX + XH * t:S_XMAX + XH * (t + 1)]
        v.tensor_reduce(mx, ps[:, 2 * t:2 * t + 2, :].rearrange("p b (j n) -> p (b j) n", n=T), axis=AX.X, op=ALU.max)
        dve.drain()
        v.tensor_scalar(mx, mx, -XD ** -0.5, None, ALU.mult).then_inc(s("xs_max"), 1)
    for t in range(NT):
        dve.wait_ge(*at("xs_exp", l, XH * (t + 1)))
        inv = m.stat[:, S_XINV + XH * t:S_XINV + XH * (t + 1)]
        v.reciprocal(inv, m.stat[:, S_XSUM + XH * t:S_XSUM + XH * (t + 1)])
        dve.drain()
        v.tensor_tensor(m.xp[:, t], m.xp[:, t], bc(inv, T), ALU.mult).then_inc(s("xp_rows"), 1)
    for b in range(2):
        dve.wait_ge(*at("xpT_full", l, b + 3))
        v.tensor_copy(m.xpT[:, 1, 2 * b:2 * b + 2, :], two(ps[:, 6 + b, :])).then_inc(s("xpT_d"), 1)
    for b in (2, 3):
        dve.wait_ge(*at("xo_full", l, b + 1))
        v.tensor_copy(m.hT[:, 2 * b:2 * b + 2, :], two(ps[:, b, :])).then_inc(s("xo_cols_d"), 1)
    add_into_x(m, dve, *at("out2_full", l, 0), s("x_attended"))


def vector_route(m, dve, l):
    v, ps, at, s = m.nc.vector, m.ps, m.at, m.s
    vector_norm(m, dve, l, "h3", m.par1("ffn_g"))
    dve.wait_ge(*at("router_full", l))
    mx = m.stat[:, S_RMAX:S_RMAX + NT]
    v.tensor_reduce(mx, ps[:, 4:6, 0:E], axis=AX.X, op=ALU.max)
    dve.drain()
    v.tensor_scalar(mx, mx, -1.0, None, ALU.mult).then_inc(s("router_max"), 1)
    dve.wait_ge(*at("router_exp", l))
    inv = m.stat[:, S_RINV:S_RINV + NT]
    v.reciprocal(inv, m.stat[:, S_RSUM:S_RSUM + NT])
    dve.drain()
    v.tensor_tensor(m.aff, m.aff, bc(inv, E), ALU.mult).then_inc(s("aff_rows"), 1)
    dve.wait_ge(*at("aff_T", l))
    v.tensor_copy(m.work[0:E, 0, :], ps[0:E, 6, 0:T])
    dve.drain()
    for r in range(CAP // 8):
        best, work = m.gates[0:E, 8 * r:8 * r + 8], m.work[0:E, r % 2, :]
        v.max(best, work)
        dve.drain()
        v.max_index(m.top_i[0:E, 8 * r:8 * r + 8], best, work)
        v.match_replace(m.work[0:E, 1 - r % 2, :], best, work, -1.0)
        dve.drain()
    slots, gates = m.slots[0:E], m.gates[0:E]
    v.tensor_copy(slots, m.top_i[0:E, :])
    dve.drain()
    v.tensor_copy(m.rep[0:E, 0], slots.unsqueeze(1).to_broadcast([E, 4, CAP]))
    v.tensor_copy(m.rep[0:E, 1], gates.unsqueeze(1).to_broadcast([E, 4, CAP]))
    v.tensor_tensor(m.diag[0:E], slots.unsqueeze(1).to_broadcast([E, E, CAP]), bc(m.const("expert_diag")[0:E, :], CAP),
                    ALU.mult).then_inc(s("top_found"), 1)
    dve.wait_ge(*at("top_T", l))
    v.tensor_copy(m.topc, ps[:, 6, 0:2 * E].rearrange("p (i e) -> p i e", e=E)).then_inc(s("onehot"), 1)
    for t in range(NT):
        v.tensor_scalar(m.onehot[:, t, :], ps[:, 7, :], m.const("iota_col")[:, t:t + 1], None, ALU.is_equal)\
            .then_inc(s("onehot"), 1)
    dve.drain()


def vector_experts(m, dve, l):
    v, ps, at, s = m.nc.vector, m.ps, m.at, m.s
    up = ps[:, 0, :].rearrange("p (c n) -> p c n", n=P)[:, :, 2 * CAP:]
    with dve.Fori(0, E) as e:
        n = e + l * E + 1
        dve.wait_ge(s("tok_full"), n)
        v.tensor_tensor(m.tokT, ps[:, 0, 0:KD * CAP].rearrange("p (k c) -> p k c", c=CAP), bc(m.par1("ffn_g"), CAP), ALU.mult)\
            .then_inc(s("tok_cols"), 1)
        v.tensor_scalar(m.pick, m.const("iota_row"), m.topc[:, 0, bass.ds(e, 1)], m.topc[:, 1, bass.ds(e, 1)],
                        ALU.is_equal, ALU.mult).then_inc(s("pick"), 1)
        dve.wait_ge(s("gate_silu"), n)
        v.tensor_tensor(m.hid.rearrange("p c h n -> p c (h n)"), m.sil, up, ALU.mult).then_inc(s("hid_cols"), 1)
        dve.wait_ge(s("dn_full"), 2 * n)
        v.tensor_copy(m.dn[:, 1, :], ps[:, 3, :]).then_inc(s("dn_rows_d"), 1)
    dve.wait_ge(*at("acc_full", l))
    for i in range(4):
        nh, t = i // 2, i % 2
        v.tensor_copy(m.x[:, t, nh * BANK:(nh + 1) * BANK], ps[:, 4 + i, :]).then_inc(s("x_routed"), 1)


def vector_between(m, dve):
    dve.wait_ge(*m.at("fin1_loaded", 0))
    dve.wait_ge(*m.at("f1_rstd", 0))
    for t in range(NT):
        m.nc.vector.scalar_tensor_tensor(m.x[:, t, :], m.x[:, t, :], m.stat[:, 64 + t:65 + t], m.fin1, ALU.mult, ALU.mult)\
            .then_inc(m.s("x_first"), 1)


def scalar_between(m, act):
    norm_squares(m, act, m.prev("x_routed", L), m.s("f1_sq"))


def gpsimd_between(m, pool):
    pool.wait_ge(*m.at("x_attended", L - 1))
    pool.dma_start(m.fin1, m.d["fix"][:, KD:KD + D]).then_inc(m.s("fin1_loaded"), 16)
    gpsimd_rstd(m, pool, 0, "f1", "f1_sq", 0, NT, 0)


def sync_second(m, sp, l):
    d = m.d
    after_first = [L * n for n in HELD1_LAYER]

    def free(i):
        g = PLAN2[i]
        ring_wait(m, sp, g.slot, l * HELD2[g.slot] + (after_first[g.slot] + g.held))

    def load(i, dst, src):
        sp.dma_start(dst, src).then_inc(m.landed[PLAN2[i].slot], 16)

    def layer(name):
        return d[name][bass.ds(l, 1)].rearrange("l (k p) n -> p (l k) n", p=P)

    def whole(i, name, c0, k=KD, n=BANK, k0=0):
        free(i)
        load(i, slab(m, PLAN2[i].slot, k, n), layer(name)[:, k0:k0 + k, c0:c0 + n])

    lat0 = SHIFT_TILES * P + QL
    for j in range(4):
        whole(W_IN2 + j, "w_in_2", j * BANK)
    free(W_LAT)
    keys, kv_up, q_up = lat_slab(m)
    load(W_LAT, keys, layer("w_in_2")[:, :, lat0:lat0 + KVL + PE_D])
    load(W_LAT, kv_up, layer("w_kv_up_2"))
    load(W_LAT, q_up, layer("w_q_up_2"))
    for j in range(4):
        whole(W_GATES + j, "w_in_2", SHIFT_TILES * P + LAT + j * BANK)
    whole(W_ORW, "w_out_rwkv_2", 0, k=4, n=D)
    whole(W_OMLA, "w_out_mla_2", 0, k=4, n=D)
    for j in range(2):
        whole(W_OUT2 + j, "w_out_2", j * BANK)
    for j in range(NUP):
        i = W_UP + j
        free(i)
        if j == 1:
            sp.wait_ge(*m.at("merged", l))
        w = layer("w_ffn_up_2")
        for part in range(2):
            load(i, up_slab(m, i)[:, part], w[:, :, part * FFN + j * T:part * FFN + (j + 1) * T])
    for j in range(NDN):
        whole(W_DN + j, "w_ffn_down_2", 0, k=min(4, NF - 4 * j), n=D, k0=4 * j)


def lat_slab(m):
    r = m.ring[:, PLAN2[W_LAT].slot]
    a = KD * (KVL + PE_D)
    b = a + MH * 2 * NOPE
    return (r[:, 0:a].rearrange("p (k n) -> p k n", k=KD), r[:, a:b].unsqueeze(1),
            r[:, b:b + 2 * MH * QKD].rearrange("p (k n) -> p k n", k=2))


def up_slab(m, i):
    return m.ring[:, PLAN2[i].slot].rearrange("p (g k n) -> p g k n", g=2, k=KD)


def landed2(m, eng, l, i):
    g = PLAN2[i]
    eng.wait_ge(m.landed[g.slot], l * LANDED2[g.slot] + (L * LANDED1_LAYER[g.slot] + g.landed))


def tensor_second(m, pe, l):
    nc, ps, at, s = m.nc, m.ps, m.at, m.s
    mm = nc.tensor.matmul
    release = []

    def landed(i):
        landed2(m, pe, l, i)

    def weights(i, k=KD, n=BANK):
        landed(i)
        return slab(m, PLAN2[i].slot, k, n)

    def used(i):
        return m.free[PLAN2[i].slot]

    def free_released(ins):
        if release:
            ins.then_inc(used(release.pop()), 1)

    def tile_products(out, w, c, rhs, ks):
        for i, k in enumerate(ks):
            ins = mm(out, w[:, k, c:c + P], rhs[:, k, :], start=i == 0, stop=i == len(ks) - 1)
            if i == 0:
                free_released(ins)
        return ins

    def norm_columns(name):
        pe.wait_ge(*at(name + "_xn", l))
        pe_columns(m, m.xn, s(name + "_T"))
        pe.wait_ge(*at(name + "_cols_a", l))
        pe.wait_ge(*at(name + "_cols_d", l))

    norm_columns("n1")
    for j in range(4):
        w = weights(W_IN2 + j)
        for c in range(4 if j < 3 else 2):
            i = 4 * j + c
            ins = tile_products(half_bank(m, (4, 5, 6, 7, 0, 1, 2)[i // 2], i % 2), w, c * P, m.hT, range(KD))
            if i % 2:
                ins.then_inc(s("rw_full"), 1)
        if j < 3:
            release.append(W_IN2 + j)
        if j == 2:
            pe.wait_ge(*at("kk_sq", l))
            for b in range(2):
                mm(ps[:, 6 + b, :], m.const("head_sum"), m.sq[:, 2 * b:2 * b + 2, :], start=True, stop=True)\
                    .then_inc(s("kk_full"), 1)
    keys = lat_slab(m)[0]
    landed(W_LAT)
    pe.wait_ge(*at("rw_cols", l, 2))
    for t in range(NT):
        for cols, w_part, c0 in ((slice(0, QL), w, QL), (slice(QL, LAT), keys, 0)):
            for k in range(KD):
                ins = mm(ps[:, 3 + t, cols], m.hT[:, k, t * P:(t + 1) * P], w_part[:, k, c0:c0 + cols.stop - cols.start],
                         start=k == 0, stop=k == KD - 1)
                if k == 0:
                    if t == NT - 1 and c0 == 0:
                        release.append(W_IN2 + 3)
                    free_released(ins)
        ins.then_inc(s("lat_full"), 1)
        if t == 0:
            pe.wait_ge(*at("late2_loaded", l))
            pe.wait_ge(*at("kk_root", l))
            pe.wait_ge(*at("lora_in", l))
            pe.wait_ge(*at("rw_cols", l, 13))
            up = m.par2("lora_up")
            for b in range(4):
                rows = slice(64 * (b // 2), 64 * (b // 2) + 64)
                for i in range(2):
                    tile = 2 * (b % 2) + i
                    ins = mm(half_bank(m, (5, 6, 7, 0)[b], i), up[rows, tile * P:(tile + 1) * P], m.wa[rows, :],
                             start=True, stop=True)
                ins.then_inc(s("lora_full"), 1)
    with pe.Fori(0, PAIRS) as p:
        tensor_pair(m, pe, l, p, landed)
    release += [W_GATES + j for j in range(4)]
    tensor_rwkv_out(m, pe, l, free_released)
    tensor_mla(m, pe, l, used)
    pe.wait_ge(*at("o2_cols", l))
    for j, src in ((0, m.yaT), (1, m.o2T)):
        w = weights((W_ORW, W_OMLA)[j], 4, D)
        for i in range(4):
            nh, t = i // 2, i % 2
            for k in range(4):
                ins = mm(ps[:, 4 * j + i, :], src[:, k, t * P:(t + 1) * P], w[:, k, nh * BANK:(nh + 1) * BANK],
                         start=k == 0, stop=k == 3)
                if k == 0:
                    free_released(ins)
            ins.then_inc(s("br2_full"), 1)
        release.append((W_ORW, W_OMLA)[j])
    pe.wait_ge(*at("merged", l))
    pe_columns(m, m.xn, s("merged_T"))
    pe.wait_ge(*at("merged_cols_a", l))
    pe.wait_ge(*at("merged_cols_d", l))
    for nh in range(2):
        w = weights(W_OUT2 + nh)
        for t in range(NT):
            for k in range(KD):
                ins = mm(ps[:, 4 + 2 * nh + t, :], m.hT[:, k, t * P:(t + 1) * P], w[:, k, :], start=k == 0, stop=k == KD - 1)
                if k == 0:
                    free_released(ins)
            ins.then_inc(s("out3_full"), 1)
        release.append(W_OUT2 + nh)
    norm_columns("n2")
    columns = (m.hT_hi, m.hT_lo)
    for j in range(NUP):
        if j >= 4:
            pe.wait_ge(*at("up_act", l, j - 3))
        for g in range(2):
            q = 2 * j + g
            pe.wait_ge(*at("w_lo", l, q + 1))
            w = [a.rearrange("p (k n) -> p k n", k=KD) for a in ffn_half(m, q)[:2]]
            for c in range(2):
                for k in range(KD):
                    first, ins = exact(m, half_bank(m, (2 * j + g) % 8, c), [a[:, k, c * P:(c + 1) * P] for a in w],
                                       [a[:, k, :] for a in columns], k == 0, k == KD - 1)
                    free_released(first)
            ins.then_inc(s("up_full"), 1)
        release.append(W_UP + j)
    pe.wait_ge(*at("up_act", l))
    for r in range(NF // 2):
        q = 2 * NUP + r
        pe.wait_ge(*at("w_lo", l, q + 1))
        w = [a.rearrange("p (k n) -> p k n", k=2) for a in ffn_half(m, q)[:2]]
        for b in range(4):
            nh, t = b // 2, b % 2
            for i in range(2):
                k = 2 * r + i
                first, ins = exact(m, ps[:, 4 + b, :], [a[:, k, t * P:(t + 1) * P] for a in (m.act_hi, m.act_lo)],
                                   [a[:, i, nh * BANK:(nh + 1) * BANK] for a in w], k == 0, k == NF - 1)
                free_released(first)
            if r == NF // 2 - 1:
                ins.then_inc(s("down_full"), 1)
        if r < NF // 2 - 1:
            ins.then_inc(s("dn_half"), 1)
            if r % 2:
                release.append(W_DN + r // 2)
    mm(ps[:, 0, 0:32], m.ident, m.ident[:, 0:32], start=True, stop=True).then_inc(used(W_DN + NDN - 1), 1)


def ffn_half(m, q):
    i = W_UP + q // 2
    half = slice(q % 2 * (SLAB // 2), (q % 2 + 1) * (SLAB // 2))
    slot = PLAN2[i].slot
    return m.hi[:, q % 2, :], m.ring_lo[:, slot, half], m.ring[:, slot, half]


def half_bank(m, b, i):
    return m.ps[:, b, i * T:(i + 1) * T]


def tensor_pair(m, pe, l, p, landed):
    nc, ps, s = m.nc, m.ps, m.s
    mm = nc.tensor.matmul
    M = m.mat
    count = pair_counter(m, l, p)
    units = [(h, t) for h in range(2) for t in range(NT)]

    def unit(b, h, t):
        return ps[:, b, (2 * h + t) * P:(2 * h + t + 1) * P]

    def products(b, lhs, rhs):
        for h, t in units:
            ins = mm(unit(b, h, t), lhs[:, h, t, :], rhs[:, h, t, :], start=True, stop=True)
        ins.then_inc(s("inv_full"), 1)

    gates = iter([(t, k) for t in range(NT) for k in range(KD)])

    def fill(n):
        for _ in range(n):
            t, k = next(gates)
            ins = mm(ps[:, 6 + t, :], m.hT[:, k, t * P:(t + 1) * P],
                     m.ring[:, bass.ds(p, 1), k * BANK:(k + 1) * BANK].rearrange("p o n -> p (o n)"),
                     start=k == 0, stop=k == KD - 1)
            if k == KD - 1:
                ins.then_inc(s("gates_full"), 1)

    pe.wait_ge(*count("pair_in", 5))
    for b, pair in ((0, (m.arp[:, :, 0, :], m.btp)), (1, (m.ktp, m.vtp))):
        for i, src in enumerate(pair):
            for t in range(NT):
                ins = nc.tensor.transpose(ps[:, b, i * T + t * P:i * T + (t + 1) * P], src[:, t, :], m.ident)
        ins.then_inc(s("tok_T"), 1)
    for b, lhs in ((2, m.btp), (4, m.ktp), (0, None)):
        if lhs is None:
            pe.wait_ge(*count("tok_a", 1))
            pe.wait_ge(*count("tok_d", 2))
        for t in range(NT):
            for h in range(2):
                r = slice(h * HD, (h + 1) * HD)
                if lhs is None:
                    ins = mm(ps[:, b + h, t * P:(t + 1) * P], m.arp[r, t, 0, :], m.btp[r, t, :], start=True, stop=True)
                else:
                    ins = mm(ps[:, b + h, t * T:(t + 1) * T], lhs[r, t, :], m.arp[r, t].rearrange("p a b -> p (a b)"),
                             start=True, stop=True)
        ins.then_inc(s("prod_full"), 1)
    for j in range(4):
        landed(W_GATES + j)
    fill(2)
    pe.wait_ge(*count("prod_masked", 4))
    products(0, M["DT"], M["D"])
    products(1, M["D"], M["DT"])
    fill(1)
    pe.wait_ge(*count("inv_a", 1))
    pe.wait_ge(*count("inv_d", 1))
    products(0, M["D2T"], M["D2"])
    products(1, M["D2"], M["D2T"])
    pe.wait_ge(*count("prod_masked", 5))
    products(2, M["D2T"], M["ID"])
    fill(1)
    pe.wait_ge(*count("inv_a", 2))
    pe.wait_ge(*count("inv_d", 2))
    products(3, M["D"], M["DT"])
    pe.wait_ge(*count("prod_masked", 7))
    for h, t in units:
        ins = mm(ps[:, 4, (2 * h + t) * HD:(2 * h + t + 1) * HD], M["Aak"][:, h, t, :], m.kvtok[:, 1, t, h * HD:(h + 1) * HD],
                 start=True, stop=True)
    ins.then_inc(s("u_full"), 1)
    fill(1)
    pe.wait_ge(*count("inv_d", 4))
    products(0, M["D"], M["D2"])
    fill(1)
    pe.wait_ge(*count("inv_d", 5))
    products(1, M["ID"], M["D2T"])
    products(2, M["D2T"], M["ID"])
    fill(1)
    pe.wait_ge(*count("inv_d", 6))
    products(3, M["X"], M["D"])
    fill(1)
    pe.wait_ge(*count("inv_a", 4))
    products(0, M["DT"], M["D2"])
    pe.wait_ge(*count("inv_d", 7))
    pe.wait_ge(*count("u_rows", 1))
    for h, t in units:
        ins = mm(unit(5, h, t), M["D"][:, h, t, :], m.rb[:, h, t, :], start=True, stop=True)
    ins.then_inc(s("wu_full"), 1)
    pe.wait_ge(*count("wu_rows", 1))
    for h, t in units:
        ins = mm(ps[h * HD:(h + 1) * HD, 4, t * P:(t + 1) * P], m.WU[:, t, 0, h, :], M["Arb"][:, h, t, :], start=True, stop=True)
    ins.then_inc(s("q_full"), 1)
    for t in range(NT):
        for part in range(3):
            for c in range(CT):
                r = slice(c * CH, (c + 1) * CH)
                lhs, rhs = ((m.WU[r, t, 0], m.btok[r, t, :]), (m.btok[r, t, :], m.WU[r, t, 1]),
                            (m.kvtok[r, 0, t, :], m.kvtok[r, 1, t, :]))[part]
                flat = lambda a: a.rearrange("p h b -> p (h b)") if len(a.shape) == 3 else a
                at = t * T + (0 if part == 0 else P)
                ins = mm(ps[:, c, at:at + P], flat(lhs), flat(rhs), start=part != 2, stop=part != 1)
    ins.then_inc(s("gh_full"), 1)
    pe.wait_ge(*count("q_set", 1))
    for part in range(2):
        for h, t in units:
            lhs = m.WU[:, t, 1, h, :] if part == 0 else m.kvtok[:, 1, t, h * HD:(h + 1) * HD]
            mm(ps[h * HD:(h + 1) * HD, 4 + t, 0:P], lhs, M["Arb" if part == 0 else "Ark"][:, h, t, :],
               start=part == 0, stop=False, skip_group_check=True)
    pe.wait_ge(*count("gates_sig", 1))
    fill(2)
    pe.wait_ge(*count("gh_set", 4))
    for c in range(1, NCH):
        state = m.H[:, 0, :] if c == 1 else m.S[:, c - 2, :]
        if c > 1:
            pe.wait_ge(*count("state_set", c - 1))
        if c < NCH - 1:
            mm(ps[:, 0, (c % 4) * P:(c % 4 + 1) * P], m.G[:, c, :], state, start=True, stop=True).then_inc(s("state_full"), 1)
        t, r = c // CT, slice((c % CT) * CH, (c % CT + 1) * CH)
        ins = mm(ps[:, 4 + t, r], state, m.QT[:, t, r], start=False, stop=True, skip_group_check=True)
        if c == NCH - 1:
            ins.then_inc(s("y_full"), 1)
        else:
            fill(1)


def pair_counter(m, l, p):
    def count(signal, k):
        per = m.s.of[signal][4] // PAIRS
        return m.at(signal, l, p * per + k)
    return count


def tensor_rwkv_out(m, pe, l, free_released):
    ps, at, s = m.ps, m.at, m.s
    mm = m.nc.tensor.matmul
    head_sum = m.const("head_sum")

    def head_sums(b0, src, signal):
        for b in range(2):
            mm(ps[:, b0 + b, :], head_sum, src[:, 2 * b:2 * b + 2, :], start=True, stop=True).then_inc(s(signal), 1)

    pe.wait_ge(*at("y_cols", l))
    head_sums(0, m.y, "gn_full")
    pe.wait_ge(*at("l_norm", l))
    for b, tiles in ((2, (0, 1)), (3, (2,))):
        for i, c in enumerate(tiles):
            for t in range(NT):
                ins = m.nc.tensor.transpose(ps[:, b, i * T + t * P:i * T + (t + 1) * P], m.lat[:, t, c * P:(c + 1) * P], m.ident)
                if t == 0:
                    free_released(ins)
        ins.then_inc(s("l_T"), 1)
    pe.wait_ge(*at("bonus_in", l))
    head_sums(4, m.A, "bonus_full")
    pe.wait_ge(*at("gateup_in", l))
    pe.wait_ge(*at("gates_sig", l))
    up = m.par2("gate_up")
    for b in range(2):
        for i in range(2):
            tile = 2 * b + i
            ins = mm(half_bank(m, 6 + b, i), up[:, tile * P:(tile + 1) * P], m.gg, start=True, stop=True)
            if i == 0:
                free_released(ins)
        ins.then_inc(s("gateup_full"), 1)
    pe.wait_ge(*at("gn_sq", l))
    head_sums(0, m.LW, "var_full")


def tensor_mla(m, pe, l, used):
    nc, ps, at, s = m.nc, m.ps, m.at, m.s
    mm = nc.tensor.matmul
    _, kv_up, q_up = lat_slab(m)
    pe.wait_ge(*at("l_cols", l))
    for i in range(8):
        t, out = i // 2 % 2, ps[:, 2 + i % 2, :]
        if 2 <= i < 6:
            pe.wait_ge(*at("q2_rows", l, i - 1))
        elif i >= 6:
            pe.wait_ge(*at("kv2_rows", l, 2 * (i - 5)))
        if i < 4:
            c0, c1 = (0, BANK)[i % 2], (BANK, MH * QKD)[i % 2]
            for k in range(2):
                ins = mm(out[:, 0:c1 - c0], m.latT[:, k, t * P:(t + 1) * P], q_up[:, k, c0:c1], start=k == 0, stop=k == 1)
            ins.then_inc(s("q2_full"), 1)
        else:
            c0 = (i % 2) * BANK
            mm(out, m.latT[:, 2, t * P:(t + 1) * P], kv_up[:, 0, c0:c0 + BANK], start=True, stop=True).then_inc(s("kv2_full"), 1)
    pe.wait_ge(*at("qk2_rot", l))
    pe.wait_ge(*at("kv2_rows", l))
    for b in range(8):
        for i in range(2):
            h = 2 * (b % 4) + i
            for t in range(NT):
                src = (m.qm if b < 4 else m.km)[:, t, h, :]
                ins = nc.tensor.transpose(ps[0:QKD, b, i * T + t * P:i * T + (t + 1) * P], src, m.ident)
                if b == 0 and i == 0 and t == 0:
                    ins.then_inc(used(W_LAT), 1)
        ins.then_inc(s("qk2_T"), 1)
    pe.wait_ge(*at("qk2_cols_a", l))
    pe.wait_ge(*at("qk2_cols_d", l))
    causal = m.const("causal")
    for t in range(NT):
        n = (t + 1) * P
        for h in range(MH):
            out = mla_scores(m, t)[:, h, :]
            mm(out, m.qmT[0:QKD, h, t * P:(t + 1) * P], m.kmT[0:QKD, h, 0:n], start=True, stop=False, skip_group_check=True)
            ins = mm(out[:, t * P:], m.ident, causal, start=False, stop=True, skip_group_check=True)
        ins.then_inc(s("s2_full"), 1)
    done = 0
    for t in range(NT):
        pe.wait_ge(*at("p2_rows", l, t + 1))
        banks = (2, 3) if t == 0 else (4, 5, 6, 7)
        n = MH // len(banks)
        for j, b in enumerate(banks):
            for i in range(n):
                for kt in range(t + 1):
                    at0 = (i * (t + 1) + kt) * P
                    ins = nc.tensor.transpose(ps[:, b, at0:at0 + P], m.pm[:, n * j + i, kt * P:(kt + 1) * P], m.ident)
            ins.then_inc(s("p2_T"), 1)
        pe.wait_ge(*at("p2_cols_a", l, (1, 3)[t]))
        pe.wait_ge(*at("p2_cols_d", l, (1, 3)[t]))
        for h in range(MH):
            r = (h % 2) * HD
            for kt in range(t + 1):
                ins = mm(ps[r:r + HD, t, (h // 2) * P:(h // 2 + 1) * P], m.vm[:, kt, h * HD:(h + 1) * HD], m.pmT[:, h, kt, :],
                         start=kt == 0, stop=kt == t)
        ins.then_inc(s("o2_full"), 1)


def mla_scores(m, t):
    if t == 0:
        return m.ps[:, 0:2, :].rearrange("p b (h n) -> p (b h) n", n=P)
    return m.ps[:, 4:8, :].rearrange("p b (h n) -> p (b h) n", n=T)


def scalar_rope(m, act):
    act.wait_ge(*m.at("rope_ang", 0))
    for i in range(2):
        m.nc.scalar.activation(m.cs2[:, i].rearrange("p t i -> p (t i)"), m.rope_tmp[:, i], ACT.Sin).then_inc(m.s("rope_set"), 1)


def shift_tile(m, i):
    return (m.R, m.K, m.V)[i // 4][:, i % 4, :] if i < 12 else (m.wa, m.gg)[i - 12]


S_MU = 208


def scalar_second(m, act, l):
    nc, ps, at, s = m.nc, m.ps, m.at, m.s
    go = nc.scalar.activation
    col = lambda c: m.stat[:, c:c + 1]
    norm_squares(m, act, m.prev("h_ffn", l), s("n1_sq"))
    act.wait_ge(*at("par2_set", l))
    act_columns(m, act, m.hT, m.par2("attn_g"), *at("n1_T", l, 0), s("n1_cols_a"))
    act.wait_ge(*at("mu_set", l))
    for i in range(SHIFT_TILES):
        if i % 2 == 0:
            act.wait_ge(*at("rw_full", l, i // 2 + 1))
        go(shift_tile(m, i), half_bank(m, (4, 5, 6, 7, 0, 1, 2)[i // 2], i % 2), ACT.Copy, scale=col(S_MU + i))\
            .then_inc(s("rw_scaled"), 1)
        if i == 11:
            for b in range(2):
                act.wait_ge(*at("kk_full", l, b + 1))
                go(m.rs[:, 2 * b:2 * b + 2, :], two(ps[:, 6 + b, :]), ACT.Sqrt, bias=m.const("kk_eps")).then_inc(s("kk_root"), 1)
    act.wait_ge(*at("rw_cols", l, 13))
    go(m.wa[0:64, :], m.wa[0:64, :], ACT.Tanh).then_inc(s("lora_in"), 1)
    act.wait_ge(*at("rw_cols", l))
    go(m.gg, m.gg, ACT.Sigmoid).then_inc(s("gateup_in"), 1)
    for b in range(4):
        act.wait_ge(*at("lora_full", l, b + 1))
        for i in range(2):
            tile = 2 * (b % 2) + i
            go((m.LW, m.A)[b // 2][:, tile, :], half_bank(m, (5, 6, 7, 0)[b], i), ACT.Sigmoid,
               bias=m.par2(("decay_base", "iclr_base")[b // 2])[:, tile:tile + 1]).then_inc(s("lora_sig"), 1)
    act.wait_ge(*at("c_less", l))
    go(m.LW, m.LW, ACT.Exp).then_inc(s("decays"), 1)
    go(m.E1, m.C, ACT.Exp).then_inc(s("decays"), 1)
    act.wait_ge(*at("decays", l, 2))
    go(m.C, m.C, ACT.Exp, scale=-1.0).then_inc(s("decays"), 1)
    act.wait_ge(*at("lat_rows", l))
    junk = m.S.rearrange("p n b -> p (n b)")
    for t in range(NT):
        for i, part in enumerate((slice(0, QL), slice(QL, QL + KVL))):
            n = part.stop - part.start
            go(junk[:, t * (QL + KVL) + part.start:t * (QL + KVL) + part.stop], m.lat[:, t, part], ACT.Square,
               scale=n ** -0.5, accum_out=col(10 + 2 * t + i)).then_inc(s("l_sq"), 1)
    with act.Fori(0, PAIRS) as p:
        scalar_pair(m, act, l, p)
    for c in range(3):
        if c != 1:
            act.wait_ge(*at("l_T", l, c // 2 + 1))
        gain = m.par2("q_g")[:, c:c + 1] if c < 2 else m.par2("kv_g")
        go(m.latT[:, c, :], half_bank(m, 2 + c // 2, c % 2), ACT.Copy, scale=gain).then_inc(s("l_cols"), 1)
    for b in range(2):
        act.wait_ge(*at("y_mid", l, b + 1))
        go(m.LW[:, 2 * b:2 * b + 2, :], m.y[:, 2 * b:2 * b + 2, :], ACT.Square, scale=HD ** -0.5).then_inc(s("gn_sq"), 1)
    for b in range(2):
        act.wait_ge(*at("var_full", l, b + 1))
        go(m.C[:, 2 * b:2 * b + 2, :], two(ps[:, b, :]), ACT.Sqrt, bias=m.const("lnx_eps")).then_inc(s("gn_root"), 1)
    for i in range(4):
        t, c0, c1 = i // 2, (0, BANK)[i % 2], (BANK, MH * QKD)[i % 2]
        act.wait_ge(*at("q2_full", l, i + 1))
        go(m.qm[:, t].rearrange("p h d -> p (h d)")[:, c0:c1], ps[:, 2 + i % 2, 0:c1 - c0], ACT.Copy).then_inc(s("q2_rows"), 1)
    for i in range(4):
        act.wait_ge(*at("kv2_full", l, i + 1))
        heads = ps[:, 2 + i % 2, :].rearrange("p (h d) -> p h d", d=2 * NOPE)
        half = slice(4 * (i % 2), 4 * (i % 2) + 4)
        go(m.km[:, i // 2, half, 0:NOPE], heads[:, :, 0:NOPE], ACT.Copy).then_inc(s("kv2_rows"), 1)
        go(m.vm[:, i // 2, (i % 2) * 256:(i % 2 + 1) * 256].rearrange("p (h d) -> p h d", d=NOPE), heads[:, :, NOPE:], ACT.Copy)\
            .then_inc(s("kv2_rows"), 1)
    for b in range(4):
        act.wait_ge(*at("qk2_T", l, b + 1))
        go(m.qmT[0:QKD, 2 * b:2 * b + 2, :], two(ps[0:QKD, b, :]), ACT.Copy).then_inc(s("qk2_cols_a"), 1)
    for t in range(NT):
        act.wait_ge(*at("s2_max", l, t + 1))
        if t:
            act.wait_ge(*at("p2_T", l, 2))
        for h in range(MH):
            go(m.pm[:, h, 0:(t + 1) * P], mla_scores(m, t)[:, h, :], ACT.Exp, bias=col(S_MAX + MH * t + h), scale=QKD ** -0.5,
               accum_out=col(S_SUM + MH * t + h)).then_inc(s("s2_exp"), 1)
        if t:
            act.wait_ge(*at("o2_full", l, 1))
        for j in range(t + 1):
            act.wait_ge(*at("p2_T", l, (1, 3 + j)[t]))
            mla_prob_columns(m, go, t, j, ACT.Copy).then_inc(s("p2_cols_a"), 1)
    for b in (0, 1):
        act.wait_ge(*at("merged_T", l, b + 1))
        go(m.hT[:, 2 * b:2 * b + 2, :], two(ps[:, b, :]), ACT.Copy).then_inc(s("merged_cols_a"), 1)
    norm_squares(m, act, at("h_mixed", l), s("n2_sq"))
    gain = m.par2("ffn_g")
    for b in range(4):
        act.wait_ge(*at("n2_T", l, b + 1))
        for k in (2 * b, 2 * b + 1):
            go(m.hT_hi[:, k, :], half_bank(m, b, k % 2), ACT.Copy, scale=gain[:, k:k + 1]).then_inc(s("n2_cols_a"), 1)

    def split(q):
        if q < 2 * NUP + NF // 2:
            r = q - 2 * NUP
            landed2(m, act, l, W_UP + q // 2)
            if r >= 2:
                act.wait_ge(*at("dn_half", l, r - 1))
            elif q >= 2:
                act.wait_ge(*at("up_full", l, q - 1))
            high(m, act, q, ffn_half(m, q)[2]).then_inc(s("w_hi"), 1)

    split(0)
    split(1)
    for j in range(NUP):
        split(2 * j + 2)
        act.wait_ge(*at("up_full", l, 2 * j + 1))
        if j >= 2:
            act.wait_ge(*at("up_act", l, j - 1))
        for c in range(2):
            f = 2 * j + c
            go(m.cb[:, j % 2, c, :], half_bank(m, 2 * j % 8, c), ACT.Identity, bias=m.par2("conv_b")[:, f:f + 1],
               scale=m.par2("conv_w")[:, 2 * NF + f:2 * NF + f + 1]).then_inc(s("up_base"), 1)
        act.wait_ge(*at("up_conv", l, j + 1))
        go(m.cb[:, j % 2], m.cb[:, j % 2], ACT.Gelu).then_inc(s("up_gelu"), 1)
        split(2 * j + 3)
    for q in range(2 * NUP + 2, 2 * NUP + NF // 2):
        split(q)


def mla_prob_columns(m, op, t, j, *args):
    n = (4, 2)[t]
    src = m.ps[:, (2, 4)[t] + j, :].rearrange("p (h k b) -> p h k b", h=n, b=P)
    return op(m.pmT[:, n * j:n * j + n, 0:t + 1, :], src, *args)


def scalar_pair(m, act, l, p):
    ps, s, M = m.ps, m.s, m.mat
    count = pair_counter(m, l, p)

    def copy(wait, dst, src, done):
        act.wait_ge(*count(*wait))
        return m.nc.scalar.activation(dst, src, ACT.Copy).then_inc(s(done), 1)

    def units(b):
        return ps[:, b, :].rearrange("p (h t b) -> p h t b", h=2, t=NT)

    copy(("tok_T", 2), m.kvtok, ps[:, 1, :].rearrange("p (a t b) -> p a t b", a=2, t=NT), "tok_a")
    copy(("inv_full", 1), M["D2"], units(0), "inv_a")
    copy(("inv_full", 3), M["D"], units(0), "inv_a")
    copy(("u_full", 1), m.rb[:, :, :, HD:], ps[:, 4, 0:4 * HD].rearrange("p (h t b) -> p h t b", h=2, t=NT), "u_rows")
    copy(("inv_full", 9), M["DT"], units(2), "inv_a")
    copy(("inv_full", 10), M["D2"], units(3), "inv_a")
    act.wait_ge(*count("wu_full", 1))
    for h in range(2):
        ins = m.nc.scalar.activation(m.WU[:, :, :, h, :], units(5)[:, h].rearrange("p t (w b) -> p t w b", w=2), ACT.Copy)
    ins.then_inc(s("wu_rows"), 1)
    for t in range(NT):
        act.wait_ge(*count("gates_full", t + 1))
        m.nc.scalar.activation(m.sg[:, t, bass.ds(p * BANK, BANK)], ps[:, 6 + t, :], ACT.Sigmoid).then_inc(s("gates_sig"), 1)


def gpsimd_second(m, pool, l):
    at, s = m.at, m.s
    pool.wait_ge(*m.prev("h_ffn", l))
    pool.dma_start(m.par[:, SOON:SOON + NLATE2], m.d["late2"][bass.ds(l, 1)].rearrange("l p n -> p (l n)"))\
        .then_inc(s("late2_loaded"), 16)
    gpsimd_rstd(m, pool, l, "n1", "n1_sq", 0, NT, 0)
    gpsimd_rstd(m, pool, l, "l", "l_sq", 10, 2 * NT, 0)
    gpsimd_rstd(m, pool, l, "n2", "n2_sq", 0, NT, 0)
    pool.dma_start(m.soon[:, :], m.d["soon"][bass.ds(l + (L + 1), 1)].rearrange("l p n -> p (l n)")).then_inc(s("soon2_loaded"), 16)


def vector_rope(m, dve):
    v = m.nc.vector
    cos, sin, turns, pos = (m.rope_tmp[:, i] for i in range(4))
    dve.wait_ge(*m.at("x_first", 0))
    v.tensor_copy(pos[:, 0:NT], m.pos_i[:, :])
    dve.drain()
    for t in range(NT):
        v.tensor_scalar(sin[:, t * PE_D // 2:(t + 1) * PE_D // 2], m.const("freq"), pos[:, t:t + 1], None, ALU.mult)
    dve.drain()
    magic = 1.5 * 2.0 ** 23
    v.tensor_scalar(turns, sin, 1.0 / (2 * math.pi), None, ALU.mult)
    for step in (magic, -magic):
        dve.drain()
        v.tensor_scalar(turns, turns, step, None, ALU.add)
    c1 = 6.28125
    c2 = float(np.float32(round((2 * math.pi - c1) * 2 ** 20) / 2 ** 20))
    for part in (c1, c2, 2 * math.pi - c1 - c2):
        dve.drain()
        v.scalar_tensor_tensor(sin, turns, -part, sin, ALU.mult, ALU.add)
    dve.drain()
    limit = float(np.nextafter(np.float32(math.pi), np.float32(0)))
    v.tensor_scalar(sin, sin, limit, -limit, ALU.min, ALU.max)
    dve.drain()
    v.tensor_scalar(cos, sin, -1.0, None, ALU.mult)
    dve.drain()
    v.tensor_tensor(cos, cos, sin, ALU.max)
    dve.drain()
    v.tensor_scalar(cos, cos, -1.0, math.pi / 2, ALU.mult, ALU.add).then_inc(m.s("rope_ang"), 1)


def tiles_bc(par):
    return bc(par, T)


def vector_second(m, dve, l):
    v, ps, at, s = m.nc.vector, m.ps, m.at, m.s
    stt = v.scalar_tensor_tensor
    vector_set_par(m, dve, l, "soon2_loaded", "par2_set")
    v.tensor_scalar(m.stat[:, S_MU:S_MU + SHIFT_TILES], m.par2("mu"), -1.0, 1.0, ALU.mult, ALU.add).then_inc(s("mu_set"), 1)
    vector_norm(m, dve, l, "n1", m.par2("attn_g"))
    for i in range(SHIFT_TILES):
        dve.wait_ge(*at("rw_scaled", l, i // 2 * 2 + 2))
        dst = shift_tile(m, i)
        stt(dst[:, 1:], half_bank(m, (4, 5, 6, 7, 0, 1, 2)[i // 2], i % 2)[:, 0:T - 1], m.par2("mu")[:, i:i + 1], dst[:, 1:],
            ALU.mult, ALU.add).then_inc(s("rw_cols"), 1)
        if i == 7:
            dve.wait_ge(*at("rw_cols", l, 8))
            v.tensor_tensor(m.KK, m.K, tiles_bc(m.par2("k_k")), ALU.mult)
            dve.drain()
            v.tensor_tensor(m.sq, m.KK, m.KK, ALU.mult).then_inc(s("kk_sq"), 1)
    dve.wait_ge(*at("kk_root", l))
    v.reciprocal(m.rs, m.rs)
    dve.drain()
    v.tensor_tensor(m.KK, m.KK, m.rs, ALU.mult)
    dve.drain()
    for zero in (m.G, m.H):
        v.memset(zero, 0.0)
    dve.wait_ge(*at("lat_full", l, 1))
    v.tensor_copy(m.lat[:, 0, :], ps[:, 3, 0:LAT]).then_inc(s("lat_rows"), 1)
    dve.wait_ge(*at("lora_sig", l, 4))
    v.tensor_scalar(m.LW, m.LW, -math.exp(-0.5), None, ALU.mult).then_inc(s("log_w"), 1)
    dve.wait_ge(*at("log_w", l))
    for i in range(PAIRS):
        v.tensor_tensor_scan(m.C[:, i, :], m.const("scan"), m.LW[:, i, :], 0.0, ALU.mult, ALU.add).then_inc(s("log_c"), 1)
    dve.wait_ge(*at("log_c", l))
    v.tensor_tensor(m.LW, m.C, m.LW, ALU.subtract).then_inc(s("c_less"), 1)
    dve.wait_ge(*at("lora_sig", l))
    stt(m.sq, m.A, 1.0, tiles_bc(m.par2("k_a")), ALU.subtract, ALU.mult)
    dve.drain()
    stt(m.K, m.sq, 1.0, m.K, ALU.add, ALU.mult)
    v.tensor_tensor(m.A, m.KK, m.A, ALU.mult)
    dve.wait_ge(*at("lat_full", l, 2))
    v.tensor_copy(m.lat[:, 1, :], ps[:, 4, 0:LAT]).then_inc(s("lat_rows"), 1)
    dve.drain()
    dve.wait_ge(*at("decays", l))
    v.memset(m.stat[:, 254:255], 0.0)
    with dve.Fori(0, PAIRS) as p:
        vector_pair(m, dve, l, p)
    vector_rwkv_out(m, dve, l)
    vector_mla(m, dve, l)
    dve.wait_ge(*at("gates_sig", l))
    for i in range(4):
        nh, t = i // 2, i % 2
        dve.wait_ge(*at("br2_full", l, 4 + i + 1))
        for j in range(2):
            v.tensor_tensor(m.m1[:, j, :], m.sg[:, t, j * D + nh * BANK:j * D + (nh + 1) * BANK], ps[:, 4 * j + i, :], ALU.mult)
        dve.drain()
        v.tensor_tensor(m.xn[:, t, nh * BANK:(nh + 1) * BANK], m.m1[:, 0, :], m.m1[:, 1, :], ALU.add).then_inc(s("merged"), 1)
        dve.drain()
    for b in (2, 3):
        dve.wait_ge(*at("merged_T", l, b + 1))
        v.tensor_copy(m.hT[:, 2 * b:2 * b + 2, :], two(ps[:, b, :])).then_inc(s("merged_cols_d"), 1)
    add_into_x(m, dve, *at("out3_full", l, 0), s("h_mixed"))
    dve.wait_ge(*at("n2_rstd", l))
    dve_scale_rows(m, m.xn, m.x, m.stat[:, 64:66], s("n2_xn"))
    gain = m.par2("ffn_g")
    for b in range(4):
        dve.wait_ge(*at("n2_cols_a", l, 2 * b + 2))
        for k in (2 * b, 2 * b + 1):
            stt(m.hT_lo[:, k, :], half_bank(m, b, k % 2), gain[:, k:k + 1], m.hT_hi[:, k, :], ALU.mult, ALU.subtract)\
                .then_inc(s("n2_cols_d"), 1)

    def split(q):
        if q < 2 * NUP + NF // 2:
            dve.wait_ge(*at("w_hi", l, q + 1))
            low(m, dve, q, *ffn_half(m, q)[1:]).then_inc(s("w_lo"), 1)

    split(0)
    split(1)
    for j in range(NUP):
        split(2 * j + 2)
        dve.wait_ge(*at("up_base", l, 2 * j + 2))
        for back in (1, 2):
            for c in range(2):
                f = (2 - back) * NF + 2 * j + c
                dst = m.cb[:, j % 2, c, back:]
                ins = stt(dst, half_bank(m, 2 * j % 8, c)[:, 0:T - back], m.par2("conv_w")[:, f:f + 1], dst, ALU.mult, ALU.add)
            if back == 1:
                dve.drain()
        ins.then_inc(s("up_conv"), 1)
        dve.wait_ge(*at("up_gelu", l, j + 1))
        dve.wait_ge(*at("up_full", l, 2 * j + 2))
        gated = m.cb[:, j % 2]
        v.tensor_tensor(gated, gated, two(ps[:, (2 * j + 1) % 8, :]), ALU.mult)
        split(2 * j + 3)
        dve.drain()
        v.tensor_copy(m.act_hi[:, 2 * j:2 * j + 2, :], gated)
        dve.drain()
        v.tensor_tensor(m.act_lo[:, 2 * j:2 * j + 2, :], gated, m.act_hi[:, 2 * j:2 * j + 2, :], ALU.subtract)\
            .then_inc(s("up_act"), 1)
    for q in range(2 * NUP + 2, 2 * NUP + NF // 2):
        split(q)
    add_into_x(m, dve, *at("down_full", l, 0), s("h_ffn"))


def vector_pair(m, dve, l, p):
    v, ps, s, M = m.nc.vector, m.ps, m.s, m.mat
    tt = v.tensor_tensor
    count = pair_counter(m, l, p)

    def wait(signal, k):
        dve.wait_ge(*count(signal, k))

    def mine(a):
        return a[:, bass.ds(p, 1), :].rearrange("p o (t b) -> p (o t) b", b=P)

    def units(b):
        return ps[:, b, :].rearrange("p (h t b) -> p h t b", h=2, t=NT)

    def masked(name, b, part, mask):
        src = ps[:, b:b + 2, 0:NT * P].rearrange("p h (t b) -> p h t b", t=NT) if part is None else \
            ps[:, b:b + 2, :].rearrange("p h (t w b) -> p h t w b", t=NT, w=2)[:, :, :, part, :]
        for h in range(2):
            ins = tt(M[name][:, h], src[:, h], m.const(mask).unsqueeze(1).to_broadcast([P, NT, P]), ALU.mult)
        ins.then_inc(s("prod_masked"), 1)

    v.scalar_tensor_tensor(m.arp[:, :, 0, :], mine(m.KK), -1.0, mine(m.LW), ALU.mult, ALU.mult).then_inc(s("pair_in"), 1)
    tt(m.btp, mine(m.A), mine(m.C), ALU.mult).then_inc(s("pair_in"), 1)
    tt(m.ktp, mine(m.K), mine(m.C), ALU.mult).then_inc(s("pair_in"), 1)
    v.tensor_copy(m.vtp, mine(m.V)).then_inc(s("pair_in"), 1)
    tt(m.arp[:, :, 1, :], mine(m.R), mine(m.E1), ALU.mult).then_inc(s("pair_in"), 1)
    wait("tok_T", 1)
    v.tensor_copy(m.rb.rearrange("p h t b -> p t h b")[:, :, :, 0:HD], ps[:, 0, 0:T].rearrange("p (t h b) -> p t h b", t=NT, h=2))\
        .then_inc(s("tok_d"), 1)
    v.tensor_copy(m.btok, ps[:, 0, T:].rearrange("p (t b) -> p t b", t=NT)).then_inc(s("tok_d"), 1)
    wait("prod_full", 1)
    masked("DT", 2, 0, "up16")
    wait("prod_full", 3)
    masked("D", 0, None, "low16")
    wait("prod_masked", 2)
    tt(M["ID"].rearrange("p h t b -> p (h t) b"), M["D"].rearrange("p h t b -> p (h t) b"),
       m.ident.unsqueeze(1).to_broadcast([P, 2 * NT, P]), ALU.add).then_inc(s("prod_masked"), 1)
    masked("X", 0, None, "low32x")
    wait("inv_full", 2)
    v.tensor_copy(M["D2T"], units(1)).then_inc(s("inv_d"), 1)
    masked("Arb", 2, 1, "up32d")
    wait("inv_full", 4)
    v.tensor_copy(M["DT"], units(1)).then_inc(s("inv_d"), 1)
    masked("Aak", 4, 0, "up32")
    masked("Ark", 4, 1, "up32d")
    wait("inv_full", 5)
    tt(M["ID"], units(2), M["ID"], ALU.add).then_inc(s("inv_d"), 1)
    wait("inv_full", 6)
    tt(M["D2"].rearrange("p h t b -> p (h t) b"), ps[:, 3, :].rearrange("p (u b) -> p u b", b=P),
       m.ident.unsqueeze(1).to_broadcast([P, 2 * NT, P]), ALU.add).then_inc(s("inv_d"), 1)
    wait("inv_d", 4)
    wait("inv_full", 7)
    tt(M["D2T"], units(0), M["D2"], ALU.add).then_inc(s("inv_d"), 1)
    wait("inv_full", 8)
    v.tensor_copy(M["D"], units(1)).then_inc(s("inv_d"), 1)
    wait("inv_full", 11)
    wait("inv_d", 6)
    tt(M["D"], units(0), M["D"], ALU.add).then_inc(s("inv_d"), 1)
    wait("q_full", 1)
    tt(m.QT, ps[:, 4, 0:T].rearrange("p (t b) -> p t b", t=NT), m.arp[:, :, 1, :], ALU.add).then_inc(s("q_set"), 1)
    wait("gh_full", 1)
    ends = m.E1[:, bass.ds(p, 1), CH - 1::CH].rearrange("p o (t c) -> p (o t) c", t=NT)
    for w, dst in ((0, m.G), (1, m.H)):
        for h in range(2):
            r = slice(h * HD, (h + 1) * HD)
            for t in range(NT):
                out = dst[r, t * CT:(t + 1) * CT, r]
                src = ps[r, 0:CT, t * T + w * P + h * HD:t * T + w * P + (h + 1) * HD]
                other = m.ident[r, r].unsqueeze(1).to_broadcast([HD, CT, HD]) if w == 0 else bc(ends[r, t], HD)
                ins = tt(out, src, other, ALU.add if w == 0 else ALU.mult)
            ins.then_inc(s("gh_set"), 1)
    wait("gh_set", 4)
    for c in range(1, NCH - 1):
        wait("state_full", c)
        end = m.E1[:, bass.ds(p, 1), (c + 1) * CH - 1]
        v.scalar_tensor_tensor(m.S[:, c - 1, :], ps[:, 0, (c % 4) * P:(c % 4 + 1) * P], end, m.H[:, c, :], ALU.mult, ALU.add)\
            .then_inc(s("state_set"), 1)
    wait("y_full", 1)
    v.tensor_scalar(mine(m.y), ps[:, 4:6, 0:P], 1.0, None, ALU.mult).then_inc(s("y_cols"), 1)


def vector_rwkv_out(m, dve, l):
    v, ps, at, s = m.nc.vector, m.ps, m.at, m.s
    tt = v.tensor_tensor

    def banks(b):
        return ps[:, b:b + 2, :].rearrange("p b (a n) -> p (b a) n", n=T)

    dve.wait_ge(*at("l_rstd", l))
    for t in range(NT):
        for i, part in enumerate((slice(0, QL), slice(QL, QL + KVL))):
            c = 74 + 2 * t + i
            v.tensor_scalar(m.lat[:, t, part], m.lat[:, t, part], m.stat[:, c:c + 1], None, ALU.mult).then_inc(s("l_norm"), 1)
    for b in range(2):
        dve.wait_ge(*at("gn_full", l, b + 1))
        yb = m.y[:, 2 * b:2 * b + 2, :]
        v.scalar_tensor_tensor(yb, two(ps[:, b, :]), -1.0 / HD, yb, ALU.mult, ALU.add).then_inc(s("y_mid"), 1)
    tt(m.A, m.R, m.K, ALU.mult)
    dve.drain()
    tt(m.A, m.A, tiles_bc(m.par2("r_k")), ALU.mult).then_inc(s("bonus_in"), 1)
    dve.wait_ge(*at("bonus_full", l))
    tt(m.E1, banks(4), m.V, ALU.mult)
    dve.wait_ge(*at("gn_root", l))
    v.reciprocal(m.C, m.C)
    dve.drain()
    tt(m.y, m.y, m.C, ALU.mult)
    dve.drain()
    for i in range(PAIRS):
        v.tensor_scalar(m.y[:, i, :], m.y[:, i, :], m.par2("lnx_w")[:, i:i + 1], m.par2("lnx_b")[:, i:i + 1], ALU.mult, ALU.add)
    dve.drain()
    tt(m.y, m.y, m.E1, ALU.add)
    dve.drain()
    for b in range(2):
        dve.wait_ge(*at("gateup_full", l, b + 1))
        tt(m.yaT[:, 2 * b:2 * b + 2, :], m.y[:, 2 * b:2 * b + 2, :], two(ps[:, 6 + b, :]), ALU.mult).then_inc(s("ya_cols"), 1)


def vector_mla(m, dve, l):
    v, ps, at, s = m.nc.vector, m.ps, m.at, m.s
    tt = v.tensor_tensor
    pe_part = slice(NOPE, QKD)
    dve.wait_ge(*at("ya_cols", l))
    v.tensor_copy(m.qm[:, :, MH, pe_part], m.lat[:, :, QL + KVL:])
    dve.drain()
    dve.wait_ge(*at("q2_rows", l))
    dve.wait_ge(*at("rope_set", 0))
    x1, x2 = m.qm[:, :, :, NOPE:NOPE + PE_D // 2], m.qm[:, :, :, NOPE + PE_D // 2:]
    tmp = [m.pe_tmp[:, i].rearrange("p (t h i) -> p t h i", t=NT, h=MH + 1) for i in range(4)]
    cos, sin = (m.cs2[:, i].unsqueeze(2).to_broadcast([P, NT, MH + 1, PE_D // 2]) for i in range(2))
    for out, x, c in zip(tmp, (x1, x2, x1, x2), (cos, sin, sin, cos)):
        tt(out, x, c, ALU.mult)
    dve.drain()
    tt(x1, tmp[0], tmp[1], ALU.subtract)
    tt(x2, tmp[2], tmp[3], ALU.add)
    dve.drain()
    v.tensor_copy(m.km[:, :, :, pe_part], m.qm[:, :, MH, pe_part].unsqueeze(2).to_broadcast([P, NT, MH, PE_D]))\
        .then_inc(s("qk2_rot"), 1)
    for b in range(4):
        dve.wait_ge(*at("qk2_T", l, 4 + b + 1))
        v.tensor_copy(m.kmT[0:QKD, 2 * b:2 * b + 2, :], two(ps[0:QKD, 4 + b, :])).then_inc(s("qk2_cols_d"), 1)
    for t in range(NT):
        dve.wait_ge(*at("s2_full", l, t + 1))
        mx = m.stat[:, S_MAX + MH * t:S_MAX + MH * (t + 1)]
        v.tensor_reduce(mx, mla_scores(m, t), axis=AX.X, op=ALU.max)
        dve.drain()
        v.tensor_scalar(mx, mx, -QKD ** -0.5, None, ALU.mult).then_inc(s("s2_max"), 1)
    for t in range(NT):
        dve.wait_ge(*at("s2_exp", l, MH * (t + 1)))
        inv = m.stat[:, S_INV + MH * t:S_INV + MH * (t + 1)]
        v.reciprocal(inv, m.stat[:, S_SUM + MH * t:S_SUM + MH * (t + 1)])
        dve.drain()
        rows = m.pm[:, :, 0:(t + 1) * P]
        tt(rows, rows, bc(inv, (t + 1) * P), ALU.mult).then_inc(s("p2_rows"), 1)
        if t:
            dve.wait_ge(*at("o2_full", l, 1))
        for j in range(t + 1):
            dve.wait_ge(*at("p2_T", l, (2, 5 + j)[t]))
            mla_prob_columns(m, v.tensor_copy, t, t + 1 + j).then_inc(s("p2_cols_d"), 1)
    for t in range(NT):
        dve.wait_ge(*at("o2_full", l, t + 1))
        v.tensor_copy(m.o2T[:, :, t * P:(t + 1) * P], ps[:, t, :].rearrange("p (i b) -> p i b", b=P)).then_inc(s("o2_cols"), 1)


def scalar_end(m, act):
    norm_squares(m, act, m.prev("h_ffn", L), m.s("f2_sq"))


def gpsimd_end(m, pool):
    pool.wait_ge(*m.at("up_act", L - 1))
    pool.dma_start(m.fin2, m.d["fix"][:, KD + D:KD + 2 * D]).then_inc(m.s("fin2_loaded"), 16)
    gpsimd_rstd(m, pool, 0, "f2", "f2_sq", 0, NT, 0)


def vector_end(m, dve):
    dve.wait_ge(*m.at("fin2_loaded", 0))
    dve.wait_ge(*m.at("f2_rstd", 0))
    for t in range(NT):
        m.nc.vector.scalar_tensor_tensor(m.xn[:, t, :], m.x[:, t, :], m.stat[:, 64 + t:65 + t], m.fin2, ALU.mult, ALU.mult)\
            .then_inc(m.s("y_final"), 1)


def sync_end(m, sp, out):
    for t in range(NT):
        sp.wait_ge(*m.at("y_final", 0, t + 1))
        sp.dma_start(out[0, t * P:(t + 1) * P, :], m.xn[:, t, :]).then_inc(m.s("out_stored"), 16)
    sp.wait_ge(*m.at("out_stored", 0))
    sp.wait_ge(*m.prev("soon2_loaded", L))


BIG = ("x", "mem", "w_in", "w_out", "xattn_w_q", "xattn_w_kv", "xattn_w_o", "w_gate", "w_up", "w_down", "w_in_2",
       "w_q_up_2", "w_kv_up_2", "w_out_rwkv_2", "w_out_mla_2", "w_out_2", "w_ffn_up_2", "w_ffn_down_2")


def build(nc, d, out):
    from contextlib import ExitStack
    with ExitStack() as ctx:
        m = allocate(nc, ctx)
        m.d = d
        block = ctx.enter_context(nc.Block())

        @block.sync
        def _(sp):
            sync_start(m, sp)
            with sp.Fori(0, L) as l:
                sync_first(m, sp, l)
            with sp.Fori(0, L) as l:
                sync_second(m, sp, l)
            sync_end(m, sp, out)

        @block.gpsimd
        def _(pool):
            gpsimd_start(m, pool)
            with pool.Fori(0, L) as l:
                gpsimd_first(m, pool, l)
            gpsimd_between(m, pool)
            with pool.Fori(0, L) as l:
                gpsimd_second(m, pool, l)
            gpsimd_end(m, pool)

        @block.scalar
        def _(act):
            scalar_start(m, act)
            with act.Fori(0, L) as l:
                scalar_first(m, act, l)
            scalar_between(m, act)
            scalar_rope(m, act)
            with act.Fori(0, L) as l:
                scalar_second(m, act, l)
            scalar_end(m, act)

        @block.vector
        def _(dve):
            vector_start(m, dve)
            with dve.Fori(0, L) as l:
                vector_first(m, dve, l)
            vector_between(m, dve)
            vector_rope(m, dve)
            with dve.Fori(0, L) as l:
                vector_second(m, dve, l)
            vector_end(m, dve)

        @block.tensor
        def _(pe):
            tensor_start(m, pe)
            with pe.Fori(0, L) as l:
                tensor_first(m, pe, l)
            with pe.Fori(0, L) as l:
                tensor_second(m, pe, l)


def kernel(**inputs):
    from concourse import bacc
    from concourse.bass_utils import run_bass_kernel_spmd as run
    nc = bacc.Bacc("TRN2", target_bir_lowering=False, num_devices=1)
    arrays = {n: np.asarray(inputs[n]) for n in BIG}
    arrays.update(lay_out(inputs))
    d = {n: nc.dram_tensor("in_" + n, a.shape, I32 if n == "positions" else F32, kind="ExternalInput").ap()
         for n, a in arrays.items()}
    out = nc.dram_tensor("out_0", (1, T, D), F32, kind="ExternalOutput").ap()
    build(nc, d, out)
    r = run(nc, [{"in_" + n: a for n, a in arrays.items()}], core_ids=[0])
    return r.results[0]["out_0"]
```

```python
import math

import numpy as np

import concourse.bass as bass
from concourse import mybir
from concourse.alu_op_type import AluOpType as ALU

F32 = mybir.dt.float32
F32R = mybir.dt.float32r
I32 = mybir.dt.int32
U32 = mybir.dt.uint32
ACT = mybir.ActivationFunctionType
AX = mybir.AxisListType

P = 128
D = 1024
KD = D // P
T = 256
NT = T // P
L = 2
EPS = 1e-6
BANK = 512

GM_W, GM_G = 512, 4
NQ, NKV, HD = 8, 2, 64
HEADS_QK = NQ + NKV
XH, XD = 4, 256
E, CAP, FF = 16, 32, 1024

RW = 512
PAIRS = RW // P
CH = 32
NCH = T // CH
CT = P // CH
SHIFT_TILES = 14
QL, KVL, PE_D, NOPE = 256, 128, 32, 64
MH = 8
QKD = NOPE + PE_D
LAT = QL + KVL + PE_D
FFN = 2816
NF = FFN // P
NUP = NF // 2
LNX_EPS = 64e-5

SLOTS = 6
SLAB = 4096


class Slab:
    def __init__(self, slot, landed, held):
        self.slot, self.landed, self.held = slot, landed, held


def ring_plan(slabs):
    landed, held = [0] * SLOTS, [0] * SLOTS
    plan = []
    for s, n in slabs:
        landed[s] += 16 * n
        plan.append(Slab(s, landed[s], held[s]))
        held[s] += 1
    return plan, landed, held


PLAN1, LANDED1, HELD1 = ring_plan([(i % SLOTS, 1) for i in range(18)])
W_IN1, W_XK, W_OUT1, W_XQ, W_XV, W_XO = 0, 4, 6, 10, 12, 14
H_IN, H_OUT, H_XQ, H_XO, HALVES1 = 0, 7, 11, 15, 19
GATE_SLOTS = 2
EXPERT_SLABS = [E - 1 if s < GATE_SLOTS else E for s in range(SLOTS)]
LANDED1_LAYER = [n + 16 * k for n, k in zip(LANDED1, EXPERT_SLABS)]
HELD1_LAYER = [n + k for n, k in zip(HELD1, EXPERT_SLABS)]
SG_SLOT = SLOTS - 1
NDN = -(-NF // 4)
PLAN2, LANDED2, HELD2 = ring_plan(
    [(s, 1) for s in (0, 1, 2, 3)] + [(4, 3)] + [(s, 1) for s in (0, 1, 2, 3, 0, 1, 2, 3)] +
    [((4 + i) % SLOTS, 2) for i in range(NUP)] + [((4 + NUP + i) % SLOTS, 1) for i in range(NDN)])
H_OUT2, HALVES2 = 8, 12
W_IN2, W_LAT, W_GATES, W_ORW, W_OMLA, W_OUT2, W_UP, W_DN = 0, 4, 5, 9, 10, 11, 13, 13 + NUP

CONST_COLS = {}


def _const_layout():
    at = 0
    for name, width in (("ident", P), ("head_sum", P), ("ones", P), ("cos1", NT * HD // 2), ("sin1", NT * HD // 2),
                        ("iota_row", T), ("iota_col", NT), ("expert_diag", E), ("causal", P),
                        ("low16", P), ("up16", P), ("low32x", P), ("up32", P), ("up32d", P),
                        ("scan", T), ("freq", PE_D // 2), ("eps", 64), ("neg_half", 1), ("kk_eps", 1),
                        ("lnx_eps", 1)):
        CONST_COLS[name] = (at, width)
        at += width
    return at


NCONST = _const_layout()


def constants():
    c = np.zeros((P, NCONST), np.float32)

    def put(name, value):
        at, width = CONST_COLS[name]
        c[:, at:at + width] = np.asarray(value, np.float32).reshape(-1, width)

    i = np.arange(P)
    put("ident", np.eye(P))
    put("head_sum", i[:, None] // 64 == i[None, :] // 64)
    put("ones", np.ones((P, P)))
    n = HD // 4
    freqs = np.exp(-math.log(10000.0) * np.arange(n, dtype=np.float32) / n).astype(np.float32)
    t = np.arange(T)
    ang = np.concatenate([(t // 64).astype(np.float32)[:, None] * freqs, (t % 64).astype(np.float32)[:, None] * freqs], 1)
    put("cos1", np.cos(ang).reshape(NT, P, HD // 2).transpose(1, 0, 2).reshape(P, -1))
    put("sin1", np.sin(ang).reshape(NT, P, HD // 2).transpose(1, 0, 2).reshape(P, -1))
    put("iota_row", np.broadcast_to(np.arange(T), (P, T)))
    put("iota_col", i[:, None] + P * np.arange(NT)[None, :])
    put("expert_diag", np.eye(P)[:, :E])
    put("causal", np.where(i[None, :] <= i[:, None], 0.0, -1e30))
    r, s = i[:, None], i[None, :]
    put("low16", (s < r) & (r // 16 == s // 16))
    put("up16", (r < s) & (r // 16 == s // 16))
    put("low32x", (r // CH == s // CH) & (r // 16 == s // 16 + 1))
    put("up32", (r < s) & (r // CH == s // CH))
    put("up32d", (r <= s) & (r // CH == s // CH))
    put("scan", np.broadcast_to((t % CH != 0), (P, T)))
    put("freq", np.broadcast_to(np.power(np.float32(10000.0), -np.arange(0, PE_D, 2, dtype=np.float32) / PE_D), (P, PE_D // 2)))
    eps = np.full(64, EPS)
    eps[32:52] = 64 * EPS
    put("neg_half", np.full((P, 1), -0.5))
    put("kk_eps", np.full((P, 1), 1e-12))
    put("lnx_eps", np.full((P, 1), LNX_EPS))
    put("eps", np.broadcast_to(eps, (P, 64)))
    return c


def _layout(items):
    cols, at = {}, 0
    for name, width in items:
        cols[name] = (at, width)
        at += width
    return cols, at


PAR1, SOON1 = _layout((("mix_g", 8), ("x_g", 8), ("ffn_g", 8), ("branch_g", 8), ("b_s", GM_G), ("router", KD * E)))
PAR2, SOON2 = _layout((("attn_g", 8), ("ffn_g", 8), ("mu", 14), ("decay_base", 4), ("iclr_base", 4), ("k_k", 4),
                       ("k_a", 4), ("r_k", 4), ("lnx_w", 4), ("lnx_b", 4), ("q_g", 2), ("kv_g", 1), ("conv_w", 3 * NF),
                       ("conv_b", NF)))
SOON = max(SOON1, SOON2)
LATE1, NLATE1 = _layout((("w_s", GM_G * P), ("v_g", GM_W), ("qk_g", 2 * HD)))
LATE2, NLATE2 = _layout((("lora_up", RW), ("gate_up", RW)))
for late, cols in ((LATE1, PAR1), (LATE2, PAR2)):
    cols.update((name, (SOON + at, width)) for name, (at, width) in late.items())
NPAR = SOON + max(NLATE1, NLATE2)


def columns(v):
    v = np.asarray(v)
    return np.swapaxes(v.reshape(*v.shape[:-1], -1, P), -1, -2)


def rows(v):
    v = np.asarray(v)
    return np.broadcast_to(v[:, None, :], (v.shape[0], P, v.shape[1]))


def lay_out(a):
    soon1 = np.concatenate([
        columns(a["mix_norm_g"]), columns(a["xattn_norm_g"]), columns(a["ffn_norm_g"]),
        columns(np.reshape(a["branch_norm_g"], (L, 2 * GM_W))), np.swapaxes(a["gm_b_s"], 1, 2),
        np.reshape(a["w_router"], (L, KD, P, E)).transpose(0, 2, 1, 3).reshape(L, P, KD * E)], axis=2)
    late1 = np.concatenate([
        np.asarray(a["gm_w_s"]).transpose(0, 3, 1, 2).reshape(L, P, GM_G * P),
        rows(a["gm_v_norm_g"]), rows(a["q_norm_g"]), rows(a["k_norm_g"])], axis=2)
    soon2 = np.concatenate([
        columns(a["attn_norm_2"]), columns(a["ffn_norm_2"]), columns(a["mu_shift_2"]), columns(a["decay_base_2"]),
        columns(a["iclr_base_2"]), columns(a["k_k_2"]), columns(a["k_a_2"]), columns(np.reshape(a["r_k_2"], (L, RW))),
        columns(a["lnx_w_2"]), columns(a["lnx_b_2"]), columns(a["q_norm_2"]), columns(a["kv_norm_2"]),
        columns(np.reshape(a["conv_w_2"], (L, 3 * FFN))), columns(a["conv_b_2"])], axis=2)
    late2 = np.concatenate([
        np.concatenate([a["w_decay_up_2"], a["w_iclr_up_2"]], axis=1), np.asarray(a["w_gate_up_2"])], axis=2)
    soon = np.zeros((2 * L + 1, P, SOON), np.float32)
    soon[0:L, :, 0:SOON1], soon[L:2 * L, :, 0:SOON2] = soon1, soon2
    fix = np.concatenate([columns(a["mem_norm_g"]), rows(np.asarray(a["final_norm_g"])[None])[0],
                          rows(np.asarray(a["final_norm_2"])[None])[0]], axis=1)
    return {"soon": soon, "late1": np.ascontiguousarray(late1), "late2": np.ascontiguousarray(late2), "fix": np.ascontiguousarray(fix),
            "consts": constants(),
            "positions": np.ascontiguousarray(np.reshape(a["positions_2"], (NT, P)).T)}


AREA = 18432

GROUPS = {}


def group(name, pre=(), first=(), mid=(), second=(), post=()):
    GROUPS[name] = (pre, first, mid, second, post)


group("mem", pre=[("mem_loaded", 16 * NT)])
group("tables", pre=[("tables_loaded", 48)])
group("x", pre=[("x_loaded", 16)])
group("soon", pre=[("soon0_loaded", 16)], first=[("soon1_loaded", 16)], second=[("soon2_loaded", 16)])
group("soon_set", first=[("par1_set", 1)], second=[("par2_set", 1)])
group("late", first=[("late1_loaded", 16)], second=[("late2_loaded", 16)])
group("first_gate", first=[("first_gate_loaded", 16 * GATE_SLOTS)])
group("fin", mid=[("fin1_loaded", 16)], post=[("fin2_loaded", 16)])
group("store", post=[("out_stored", 32)])
group("norm_sq", pre=[("m_sq", 2)], first=[("h1_sq", 2), ("v_sq", 2), ("br_sq", 4), ("h2_sq", 2), ("h3_sq", 2)],
      mid=[("f1_sq", 2)], second=[("n1_sq", 2), ("l_sq", 4), ("n2_sq", 2)], post=[("f2_sq", 2)])
group("norm_rstd", pre=[("m_rstd", 1)],
      first=[("h1_rstd", 1), ("v_rstd", 1), ("qk_rstd", 1), ("br_rstd", 1), ("h2_rstd", 1), ("h3_rstd", 1)],
      mid=[("f1_rstd", 1)], second=[("n1_rstd", 1), ("l_rstd", 1), ("n2_rstd", 1)],
      post=[("f2_rstd", 1)])
group("norm_mean", pre=[("m_mean", 1)],
      first=[("h1_mean", 1), ("v_mean", 1), ("qk_mean", 1), ("br_mean", 1), ("h2_mean", 1), ("h3_mean", 1)],
      mid=[("f1_mean", 1)], second=[("n1_mean", 1), ("l_mean", 1), ("n2_mean", 1)],
      post=[("f2_mean", 1)])
group("norm_xn", pre=[("m_xn", 2)], first=[("h1_xn", 2), ("v_norm", 2), ("br_xn", 4), ("h2_xn", 2), ("h3_xn", 2)],
      second=[("n1_xn", 2), ("l_norm", 4), ("n2_xn", 2)])
group("norm_T", pre=[("m_T", 4)], first=[("h1_T", 4), ("br_T", 4), ("h2_T", 4), ("h3_T", 4)],
      second=[("n1_T", 4), ("l_T", 2), ("n2_T", 4)])
group("norm_cols_a", pre=[("m_cols_a", 4)], first=[("h1_cols_a", KD), ("br_cols_a", KD), ("h2_cols_a", KD), ("h3_cols_a", 4)],
      second=[("n1_cols_a", KD), ("l_cols", 3), ("n2_cols_a", KD)])
group("norm_cols_d", pre=[("m_cols_d", 4)], first=[("h1_cols_d", KD), ("br_cols_d", KD), ("h2_cols_d", KD), ("h3_cols_d", 4)],
      second=[("n1_cols_d", KD), ("n1_whole", 1), ("n2_cols_d", KD)])
group("mix_pe", first=[("uv_full", 4), ("qkv_full", 4), ("mix_full", 2), ("qk_T", 3)])
group("mix_act", first=[("uv_gelu", 4), ("q_cols", 2)])
group("mix_dve", first=[("qkv_rows", 4), ("qk_ss", 1), ("qk_rot", 1), ("k_cols", 1), ("gm_rows", 2 * GM_G)])
group("gqa_pe_scores", first=[("sc_full", 2)], second=[("s2_full", 3)])
group("gqa_pe_turn", first=[("pT_full", 8)], second=[("p2_T", 6)])
group("gqa_pe_out", first=[("at_full", 2)], second=[("o2_full", 2)])
group("gqa_act_exp", first=[("sc_exp", 2 * NQ)], second=[("s2_exp", 2 * MH)])
group("gqa_act_cols", first=[("pT_a", 4)], second=[("p2_cols_a", 3)])
group("gqa_dve_max", first=[("sc_max", 2)], second=[("s2_max", 3)])
group("gqa_dve_cols", first=[("pT_d", 4)], second=[("p2_cols_d", 3)])
group("mla_dve_rows", second=[("p2_rows", 3)])
group("gqa_dve_out", first=[("at_rows", 2)], second=[("o2_cols", 2)])
group("res_pe", first=[("out1_full", 4), ("out2_full", 4)], second=[("out3_full", 4), ("down_full", 4)])
group("res_dve", pre=[("x_start", 2)], first=[("x_mixed", 4), ("x_attended", 4), ("x_routed", 4)],
      mid=[("x_first", 2)], second=[("h_mixed", 4), ("h_ffn", 4)], post=[("y_final", 2)])
group("mem_pe", first=[("xq_full", 4), ("xv0_full", 2), ("xs_full", 2), ("xv1_full", 2), ("xpT_full", 4), ("xo_full", 4)])
group("mem_act", first=[("xq_cols", 4), ("xv0_rows", 2), ("xs_exp", NT * XH), ("xv1_rows", 2), ("xpT_a", 2), ("xo_cols_a", 4)])
group("memk_pe", first=[("xk_full", 4)])
group("memk_act", first=[("xk_cols", 4)])
group("mem_dve", first=[("xs_max", 2), ("xp_rows", 2), ("xpT_d", 2), ("xo_cols_d", 4)])
group("route_pe", first=[("router_full", 2), ("aff_T", 1), ("top_T", 1)])
group("route_act", first=[("router_exp", 2)])
group("route_dve", first=[("router_max", 1), ("aff_rows", 1), ("top_found", 1), ("onehot", 3)])
for n in ("tok_full", "gu_full", "gu_T", "acc_full", "tok_cols", "hid_cols", "pick", "gu_rows", "gate_silu",
          "dn_rows_a", "dn_rows_d"):
    group(n, first=[(n, E)])
group("dn_full", first=[("dn_full", 2 * E)])
group("rope_dve", pre=[("rope_ang", 1)])
group("rope_act", mid=[("rope_set", 2)])
for n, c in (("rw_full", 7), ("kk_full", 2), ("lat_full", 2), ("lora_full", 4), ("kk_root", 2), ("kk_sq", 1), ("kk_unit", 1), ("zeroed", 2), ("lat_rows", 2)):
    group(n, second=[(n, c)])
group("rw_act", second=[("rw_scaled", 14), ("lora_in", 1), ("lora_sig", 8), ("decays", 3)])
group("rw_dve", second=[("mu_set", 1), ("rw_cols", 14), ("log_w", 1), ("log_c", 4), ("c_less", 1)])
for n, c in (("pair_in", 5), ("tok_T", 2), ("tok_d", 2), ("tok_a", 1), ("prod_full", 3), ("prod_masked", 7), ("inv_full", 11),
             ("inv_a", 4), ("inv_d", 7), ("u_full", 1), ("u_rows", 1), ("wu_full", 1), ("wu_rows", 1), ("gh_full", 1),
             ("gh_set", 4), ("q_full", 1), ("q_set", 1), ("state_full", NCH - 2), ("state_set", NCH - 2), ("y_full", 1),
             ("y_cols", 1), ("gates_full", 2), ("gates_sig", 2)):
    group(n, second=[(n, c * PAIRS)])
group("gn_pe", second=[("gn_full", 2), ("bonus_full", 2), ("var_full", 2), ("gateup_full", 2)])
group("gn_act", second=[("gateup_in", 1), ("gn_sq", 2), ("mask_set", 2), ("gn_root", 2)])
group("gn_dve", second=[("y_mid", 2), ("bonus_in", 1), ("bonus_read", 1), ("ya_cols", 2)])
group("mla_pe", second=[("q2_full", 4), ("kv2_full", 4), ("qk2_T", 8), ("br2_full", 8), ("merged_T", 4), ("out3_half", 1), ("up_full", 2 * NUP), ("dn_half", NF // 2 - 1)])
group("half_pe", first=[("half_used", 5)])
group("parts_hi", first=[("w1_hi", HALVES1)], second=[("w2_hi", HALVES2), ("w_hi", 2 * NUP + NF // 2)])
group("parts_lo", first=[("w1_lo", HALVES1)], second=[("w2_lo", HALVES2), ("w_lo", 2 * NUP + NF // 2)])
group("mla_act", second=[("q2_rows", 4), ("kv2_rows", 8), ("qk2_cols_a", 4), ("merged_cols_a", 4)])
group("mla_dve", second=[("qk2_rot", 1), ("qk2_cols_d", 4), ("merged", 4), ("merged_cols_d", 4)])
group("ffn_base", second=[("up_base", 2 * NUP)])
group("ffn_gelu", second=[("up_gelu", NUP)])
group("ffn_conv", second=[("up_conv", NUP)])
group("ffn_act", second=[("up_act", NUP)])


class Signals:

    def __init__(self, nc, ctx):
        self.of = {}
        for name, phases in GROUPS.items():
            sem = ctx.enter_context(nc.semaphore(name))
            base = 0
            for i, phase in enumerate(phases):
                per, at = sum(n for _, n in phase), 0
                for signal, n in phase:
                    assert signal not in self.of, signal
                    self.of[signal] = (sem, base, per, at, n)
                    at += n
                base += per * (L if i in (1, 3) else 1)

    def __call__(self, signal):
        return self.of[signal][0]

    def at(self, signal, l, k=None):
        sem, base, per, at, n = self.of[signal]
        k = n if k is None else k
        return sem, l * per + (base + at) + k

    def prev(self, signal, l):
        sem, base, per, at, n = self.of[signal]
        assert at + n == per and base > 0
        return sem, l * per + base


class Memory:

    def __init__(self, nc):
        self.nc = nc


def allocate(nc, ctx):
    m = Memory(nc)

    def sb(name, *shape, dt=F32):
        return ctx.enter_context(nc.sbuf_tensor(name, [P, *shape], dt))

    ring_at = -(-nc.sbuf_base // 32) * 32
    m.ring = sb("ring", SLOTS, SLAB)
    m.x = sb("x", NT, D)
    m.xn = sb("xn", NT, D)
    hT_at = -(-nc.sbuf_base // 32) * 32
    m.hT = sb("hT", KD, T)
    m.con = sb("con", NCONST)
    m.par = sb("par", NPAR)
    m.soon = sb("soon", SOON)
    m.mem_g = sb("mem_g", KD)
    m.stat = sb("stat", 256)
    m.cs2 = sb("cs2", 2, NT, PE_D // 2)
    area_at = -(-nc.sbuf_base // 32) * 32
    m.area = sb("area", AREA)
    m.top_i = sb("top_i", CAP, dt=U32)
    m.pos_i = sb("pos_i", NT, dt=I32)
    m.ps = ctx.enter_context(nc.psum_tensor("ps", [P, 8, BANK], F32))
    m.landed = [ctx.enter_context(nc.semaphore(f"slab_landed{s}")) for s in range(SLOTS)]
    m.free = [ctx.enter_context(nc.semaphore(f"slab_free{s}")) for s in range(SLOTS)]
    m.s = Signals(nc, ctx)
    m.at, m.prev = m.s.at, m.s.prev

    def const(name):
        at, width = CONST_COLS[name]
        return m.con[:, at:at + width]

    m.const = const
    m.ident = const("ident")

    def par(cols, name):
        at, width = cols[name]
        return m.par[:, at:at + width]

    m.par1 = lambda name: par(PAR1, name)
    m.par2 = lambda name: par(PAR2, name)
    used = [0]

    def view(*shape, at=None):
        n = int(np.prod(shape))
        if at is not None:
            used[0] = at
        a = m.area[:, used[0]:used[0] + n]
        used[0] += n
        assert used[0] <= AREA, used[0]
        if len(shape) == 1:
            return a
        names = "abcd"[:len(shape)]
        return a.rearrange(f"p ({' '.join(names)}) -> p {' '.join(names)}", **dict(zip(names[1:], shape[1:])))

    m.memT = view(KD, T, at=0)
    base = used[0]
    m.ug, m.vg = view(NT, GM_W), view(NT, GM_W)
    m.raw = view(NT, 768)
    m.rot, m.kd = view(NT, HEADS_QK, HD), view(NT, NKV, 2, HD)
    m.tmp = view(2, NT * HEADS_QK * HD // 2)
    m.qT, m.kT = view(NQ // 2, T), view(NKV, T)
    m.p, m.pT = view(NQ, T), view(NQ, 2, P)
    m.merged = view(NT, 2 * GM_W)
    m.xkT = view(KD, T, at=16384)
    m.xqT, m.xv = view(KD, T, at=base), view(NT, D)
    m.xp, m.xpT = view(NT, XH, T), view(NT, XH, T)
    m.mem_rows = view(NT, D, at=base)
    m.aff = view(NT, E, at=base)
    m.work = view(2, T)
    m.gates, m.slots = view(CAP), view(CAP)
    m.rep = view(2, 4, CAP)
    m.diag = view(E, CAP)
    m.topc = view(2, E)
    m.onehot = view(NT, E * CAP)
    m.first_gate = m.area[:, AREA - GATE_SLOTS * SLAB:].rearrange("p (g k n) -> p g k n", g=GATE_SLOTS, k=KD)
    m.tokT, m.gu, m.sil, m.hid = view(KD, CAP), view(BANK), view(4, 64), view(4, 2, CAP)
    m.pick, m.dn = view(T), view(2, BANK)
    m.R, m.K, m.V = view(PAIRS, T, at=0), view(PAIRS, T), view(PAIRS, T)
    m.wa, m.gg = view(T), view(T)
    m.lat = view(NT, LAT)
    after_lat = used[0]
    m.KK, m.A, m.LW, m.C, m.E1 = (view(PAIRS, T) for _ in range(5))
    m.y = m.KK
    flat = m.xn[:, :, :].rearrange("p t d -> p (t d)")
    m.sq, m.rs = (flat[:, i * D:(i + 1) * D].rearrange("p (a b) -> p a b", b=T) for i in (0, 1))
    m.arp, m.btp, m.ktp, m.vtp = view(NT, 2, P), view(NT, P), view(NT, P), view(NT, P)
    m.rb = flat[:, 0:512].rearrange("p (a t b) -> p a t b", a=2, t=NT)
    m.WU = flat[:, 512:1024].rearrange("p (t w h b) -> p t w h b", t=NT, w=2, h=2)
    m.H = flat[:, 1024:2048].rearrange("p (n b) -> p n b", b=P)
    m.btok, m.kvtok = view(NT, P), view(2, NT, P)
    m.mat = {n: view(2, NT, P) for n in ("D", "DT", "D2", "D2T", "ID", "X", "Arb", "Aak", "Ark")}
    assert used[0] == 16192
    m.G, m.S = view(NCH, P), view(NCH - 2, P)
    m.QT = m.mat["Aak"][:, 0]
    m.yaT = m.V
    mats = 16192 - 9 * 2 * NT * P
    m.qm, m.km, m.vm = view(NT, MH + 1, QKD, at=mats), view(NT, MH, QKD), view(NT, RW)
    m.latT = view(3, T, at=16384)
    m.pe_tmp = view(4, NT * (MH + 1) * PE_D // 2)
    m.qmT = view(MH, T, at=after_lat + 5 * PAIRS * T)
    m.kmT = m.xn[:, :, :].rearrange("p t (h b) -> p (t h) b", b=T)
    m.pm = (view(MH, P, at=after_lat + 2 * PAIRS * T), m.hT[:, :, :])
    m.pmT = m.xn[:, :, :].rearrange("p t (h k b) -> p (t h) k b", k=2, b=P)
    m.o2T = m.K
    m.sg = m.ring[:, SG_SLOT].rearrange("p (t n) -> p t n", t=NT)
    m.m1 = view(2, BANK, at=after_lat + PAIRS * T)
    m.rope_tmp = view(2, NT * PE_D // 2, at=16384)
    m.cb = view(2, 2, T, at=2 * NF * T)
    def over(name, base, at, *shape):
        return nc.alloc_sbuf_tensor_at(name, [P, *shape], F32R, offset=base + 4 * at)

    m.act_hi, m.act_lo = over("act_hi", area_at, 0, NF, T), over("act_lo", area_at, NF * T, NF, T)
    m.hi = over("slab_hi", area_at, 12288, 2, SLAB // 2)
    m.hT_hi1 = over("hT_hi1", area_at, 10240, KD, T)
    m.hT_hi = over("hT_hi", area_at, 16384, KD, T)
    m.n1_hi = over("n1_hi", area_at, after_lat + 5 * PAIRS * T, KD, T)
    m.n1_lo = over("n1_lo", area_at, 16384, KD, T)
    m.ident_r, m.causal_r = over("ident_r", area_at, 0, P), over("causal_r", area_at, P, P)
    m.hT_lo = over("hT_lo", hT_at, 0, KD, T)
    m.ring_lo = over("ring_lo", ring_at, 0, SLOTS, SLAB)
    m.fin1 = view(D, at=7168)
    m.fin2 = m.hT[:, 0:4, :].rearrange("p k n -> p (k n)")
    return m


def slab(m, slot, k, n):
    return m.ring[:, slot, 0:k * n].rearrange("p (k n) -> p k n", n=n)


def high(m, hi, lo, whole):
    return m.nc.scalar.activation(hi, whole, ACT.Copy)


def low(m, hi, lo, whole):
    return m.nc.vector.tensor_tensor(lo, whole, hi, ALU.subtract)


def act_high_columns(m, act, dst, gain, full, base, done, banks=range(4)):
    for b in banks:
        act.wait_ge(full, base + b + 1)
        for k in (2 * b, 2 * b + 1):
            m.nc.scalar.activation(dst[:, k, :], m.ps[:, b, (k % 2) * T:(k % 2 + 1) * T], ACT.Copy,
                                   scale=gain[:, k:k + 1]).then_inc(done, 1)


def dve_low_columns(m, dve, lo, hi, gain, high_done, base, done, banks=range(4)):
    for b in banks:
        dve.wait_ge(high_done, base + 2 * b + 2)
        for k in (2 * b, 2 * b + 1):
            m.nc.vector.scalar_tensor_tensor(lo[:, k, :], m.ps[:, b, (k % 2) * T:(k % 2 + 1) * T], gain[:, k:k + 1],
                                             hi[:, k, :], ALU.mult, ALU.subtract).then_inc(done, 1)


def exact(m, out, lhs, rhs, start, stop):
    for i, (a, b) in enumerate(((0, 0), (0, 1), (1, 0))):
        ins = m.nc.tensor.matmul(out, lhs[a], rhs[b], start=start and i == 0, stop=stop and i == 2)
        if i == 0:
            first = ins
    return first, ins


def act_squares(m, act, src, junk, sums, scale, done):
    for s, j, c in zip(src, junk, sums):
        m.nc.scalar.activation(j, s, ACT.Square, scale=scale, accum_out=c).then_inc(done, 1)


def pe_columns(m, src, full, banks=range(4)):
    for b in banks:
        for k in range(2):
            for t in range(NT):
                ins = m.nc.tensor.transpose(m.ps[:, b, k * T + t * P:k * T + (t + 1) * P],
                                            src[:, t, (2 * b + k) * P:(2 * b + k + 1) * P], m.ident)
        ins.then_inc(full, 1)


def act_columns(m, act, dst, gain, full, base, done):
    for b in (0, 1):
        act.wait_ge(full, base + b + 1)
        for k in (2 * b, 2 * b + 1):
            m.nc.scalar.activation(dst[:, k, :], m.ps[:, b, (k % 2) * T:(k % 2 + 1) * T], ACT.Copy,
                                   scale=gain[:, k:k + 1]).then_inc(done, 1)


def dve_columns(m, dve, dst, gain, full, base, done):
    for b in (2, 3):
        dve.wait_ge(full, base + b + 1)
        for k in (2 * b, 2 * b + 1):
            m.nc.vector.tensor_scalar(dst[:, k, :], m.ps[:, b, (k % 2) * T:(k % 2 + 1) * T], gain[:, k:k + 1], None,
                                      ALU.mult).then_inc(done, 1)


def dve_scale_rows(m, dst, src, rstd, done):
    for t in range(NT):
        m.nc.vector.tensor_scalar(dst[:, t, :], src[:, t, :], rstd[:, t:t + 1], None, ALU.mult).then_inc(done, 1)


def pe_rows(m, pe, out, lhs, w, ks, k0, start, stop):
    ins = None
    for t in range(NT):
        for i, k in enumerate(ks):
            ins = m.nc.tensor.matmul(out[t], lhs[:, k, t * P:(t + 1) * P], w[:, k - k0, :],
                                     start=start and i == 0, stop=stop and i == len(ks) - 1)
    return ins


def pe_cols(m, out, w, c, rhs, ks):
    ins = None
    for i, k in enumerate(ks):
        ins = m.nc.tensor.matmul(out, w[:, k, c:c + P], rhs[:, k, :], start=i == 0, stop=i == len(ks) - 1)
    return ins


def sync_start(m, sp):
    for t in range(NT):
        sp.dma_start(m.mem_rows[:, t, :], m.d["mem"][0, t * P:(t + 1) * P, :]).then_inc(m.s("mem_loaded"), 16)
    done = m.s("tables_loaded")
    sp.dma_start(m.con[:, :], m.d["consts"]).then_inc(done, 16)
    sp.dma_start(m.mem_g[:, :], m.d["fix"][:, 0:KD]).then_inc(done, 16)
    sp.dma_start(m.pos_i[:, :], m.d["positions"]).then_inc(done, 16)
    sp.dma_start(m.x[:, :, :], m.d["x"].rearrange("b (t p) d -> p (b t) d", p=P)).then_inc(m.s("x_loaded"), 16)
    for s in range(SLOTS):
        sp.sem_inc(m.free[s], 1)


def scalar_start(m, act):
    for t in range(NT):
        act.wait_ge(*m.at("mem_loaded", 0))
        act_squares(m, act, [m.mem_rows[:, t, :]], [m.xn[:, t, :]], [m.stat[:, t:t + 1]], D ** -0.5, m.s("m_sq"))
    act_columns(m, act, m.memT, m.mem_g, *m.at("m_T", 0, 0), m.s("m_cols_a"))


def gpsimd_rstd(m, pool, l, name, squares, c, width, eps):
    at = CONST_COLS["eps"][0] + eps
    out = m.stat[:, 64 + c:64 + c + width]
    pool.wait_ge(*m.at(squares, l))
    m.nc.gpsimd.tensor_tensor(out, m.stat[:, c:c + width], m.con[:, at:at + width], ALU.add).then_inc(m.s(name + "_mean"), 1)
    pool.wait_ge(*m.at(name + "_mean", l))
    m.nc.gpsimd.tensor_tensor(out, out, m.const("neg_half").to_broadcast([P, width]), ALU.pow).then_inc(m.s(name + "_rstd"), 1)


def gpsimd_start(m, pool):
    pool.dma_start(m.soon[:, :], m.d["soon"][0]).then_inc(m.s("soon0_loaded"), 16)
    pool.wait_ge(*m.at("tables_loaded", 0))
    gpsimd_rstd(m, pool, 0, "m", "m_sq", 0, NT, 0)


def vector_start(m, dve):
    dve.wait_ge(*m.at("m_rstd", 0))
    dve_scale_rows(m, m.xn, m.mem_rows, m.stat[:, 64:66], m.s("m_xn"))
    vector_rope(m, dve)
    dve_columns(m, dve, m.memT, m.mem_g, *m.at("m_T", 0, 0), m.s("m_cols_d"))
    dve.wait_ge(*m.at("x_loaded", 0))
    for t in range(NT):
        m.nc.vector.memset(m.stat[:, 252 + t:253 + t], 0.0).then_inc(m.s("x_start"), 1)


def tensor_start(m, pe):
    pe.wait_ge(*m.at("m_xn", 0))
    pe_columns(m, m.xn, m.s("m_T"))


def ring_wait(m, eng, slot, held):
    eng.wait_ge(m.free[slot], held + 1)


def sync_first(m, sp, l):
    d = m.d

    def load(i, dst, src):
        g = PLAN1[i]
        ring_wait(m, sp, g.slot, l * HELD1_LAYER[g.slot] + g.held)
        sp.dma_start(dst, src).then_inc(m.landed[g.slot], 16)

    def layer(w):
        return w[bass.ds(l, 1)].rearrange("l (k p) n -> p (l k) n", p=P)

    def whole(i, w, c0, n):
        load(i, slab(m, PLAN1[i].slot, KD, n), layer(w)[:, :, c0:c0 + n])

    def half(i, w, nh, kh):
        load(i, slab(m, PLAN1[i].slot, 4, BANK), layer(w)[:, 4 * kh:4 * kh + 4, nh * BANK:(nh + 1) * BANK])

    for j in range(4):
        whole(W_IN1 + j, d["w_in"], j * BANK, min(BANK, 1792 - j * BANK))
    for j in range(2):
        whole(W_XK + j, d["xattn_w_kv"], j * BANK, BANK)
    for j in range(4):
        half(W_OUT1 + j, d["w_out"], j // 2, j % 2)
    for j in range(2):
        whole(W_XQ + j, d["xattn_w_q"], j * BANK, BANK)
    for j in range(2):
        whole(W_XV + j, d["xattn_w_kv"], D + j * BANK, BANK)
    for j in range(4):
        half(W_XO + j, d["xattn_w_o"], j // 2, j % 2)
    def expert(name, e, n):
        w = d[name].rearrange("l e (k p) n -> (l e) p k n", p=P)[bass.ds(l * E + e, 1)]
        return w[:, :, :, n * BANK:(n + 1) * BANK].rearrange("o p k n -> p (o k) n")

    def into_slots(first, names, e, held):
        for i, (name, n) in enumerate((name, n) for name in names for n in range(2)):
            s = first + i
            ring_wait(m, sp, s, l * HELD1_LAYER[s] + held + HELD1[s])
            sp.dma_start(slab(m, s, KD, BANK), expert(name, e, n)).then_inc(m.landed[s], 16)

    up_down = ("w_up", "w_down")
    into_slots(0, ("w_gate",), 1, 0)
    into_slots(GATE_SLOTS, up_down, 0, 0)
    sp.wait_ge(*m.at("out2_full", l))
    for n in range(2):
        sp.dma_start(m.first_gate[:, n], expert("w_gate", 0, n)).then_inc(m.s("first_gate_loaded"), 16)
    with sp.Fori(1, E - 1) as e:
        into_slots(GATE_SLOTS, up_down, e, e)
        into_slots(0, ("w_gate",), e + 1, e)
    into_slots(GATE_SLOTS, up_down, E - 1, E - 1)


def landed1(m, pe, l, i):
    g = PLAN1[i]
    pe.wait_ge(m.landed[g.slot], l * LANDED1_LAYER[g.slot] + g.landed)


def half1(m, q):
    first, i = ((W_IN1, q // 2) if q < H_OUT else (W_OUT1, q - H_OUT) if q < H_XQ else
                (W_XQ, (q - H_XQ) // 2) if q < H_XO else (W_XO, q - H_XO))
    slot, size = PLAN1[first + i].slot, SLAB // 2
    buffer = (q - max(h for h in (H_IN, H_OUT, H_XQ, H_XO) if h <= q)) % 2
    if first == W_XQ:
        cut = lambda a: a[:, slot, :].rearrange("p (k n) -> p k n", k=KD)[:, :, buffer * T:(buffer + 1) * T]
        return first + i, m.hi[:, buffer].rearrange("p (k n) -> p k n", k=KD), cut(m.ring_lo), cut(m.ring)
    at = buffer * size if first == W_IN1 else 0
    return first + i, m.hi[:, buffer], m.ring_lo[:, slot, at:at + size], m.ring[:, slot, at:at + size]


def tensor_first(m, pe, l):
    nc, ps, at = m.nc, m.ps, m.at
    mm = nc.tensor.matmul

    def weights(i, k=KD, n=BANK):
        landed1(m, pe, l, i)
        return slab(m, PLAN1[i].slot, k, n)

    def used(i):
        return m.free[PLAN1[i].slot]

    def parts(q, n):
        pe.wait_ge(*at("w1_lo", l, q + 1))
        hi, lo = half1(m, q)[1:3]
        return [a if len(a.shape) == 3 else a.rearrange("p (k n) -> p k n", n=n) for a in (hi, lo)]

    def columns_of(src, ready, T_full, a, dcols):
        pe.wait_ge(*at(ready, l))
        pe_columns(m, src, m.s(T_full))
        pe.wait_ge(*at(a, l))
        pe.wait_ge(*at(dcols, l))

    def into_residual(first, q0, cols, half_cols, full):
        for j in range(4):
            nh, kh = j // 2, j % 2
            if j < 2:
                pe.wait_ge(*at(cols, l, half_cols * (j + 1)))
            w = parts(q0 + j, BANK)
            for t in range(NT):
                for k in range(4):
                    start, ins = exact(m, ps[:, 4 + 2 * nh + t, :], [a[:, 4 * kh + k, t * P:(t + 1) * P] for a in columns],
                                       [a[:, k, :] for a in w], kh == 0 and k == 0, kh == 1 and k == 3)
                    if release:
                        free_released(start)
                if kh == 1:
                    ins.then_inc(m.s(full), 1)
            if j == 0:
                ins.then_inc(m.s("half_used"), 1)
            release.append(first + j)

    columns = (m.hT_hi1, m.hT_lo)
    release = []

    def free_released(ins):
        ins.then_inc(used(release.pop()), 1)

    def tile_columns(out, w, c, rhs):
        for k in range(KD):
            ins = mm(out, w[:, k, c * P:(c + 1) * P], rhs[:, k, :], start=k == 0, stop=k == KD - 1)
            if k == 0 and release:
                free_released(ins)
        return ins

    def memory_keys(b):
        w = weights(W_XK + b // 2)
        for i in range(2):
            ins = tile_columns(ps[:, (1, 2, 5, 3)[b], i * T:(i + 1) * T], w, 2 * (b % 2) + i, m.memT)
        ins.then_inc(m.s("xk_full"), 1)
        if b % 2:
            release.append(W_XK + b // 2)

    pe.wait_ge(*at("h1_xn", l))
    pe_columns(m, m.xn, m.s("h1_T"))
    for q in range(H_OUT):
        j, n = q // 2, 256 if q == H_OUT - 1 else BANK
        k0, k1 = (0, KD) if n < BANK else (q % 2 * KD // 2, (q % 2 + 1) * KD // 2)
        if q < 2:
            pe.wait_ge(*at("h1_cols_d", l, k1))
        w = parts(q, n)
        for t in range(NT):
            b = (4, 6, 0, 2)[j] + t
            for k in range(k0, k1):
                start, ins = exact(m, ps[:, b, 0:n], [a[:, k, t * P:(t + 1) * P] for a in columns], [a[:, k - k0, :] for a in w],
                                   k == 0, k == KD - 1)
                if release:
                    free_released(start)
            if k1 == KD:
                ins.then_inc(m.s("uv_full" if j < 2 else "qkv_full"), 1)
        if k1 == KD:
            release.append(W_IN1 + j)
        else:
            ins.then_inc(m.s("half_used"), 1)
    pe.wait_ge(*at("v_norm", l))
    pe.wait_ge(*at("uv_gelu", l))
    w_s = m.par1("w_s")
    for t in range(NT):
        for g in range(GM_G):
            ins = mm(ps[:, 4 + t, g * P:(g + 1) * P], w_s[:, g * P:(g + 1) * P], m.vg[:, t, g * P:(g + 1) * P],
                     start=True, stop=True)
            if release:
                free_released(ins)
        ins.then_inc(m.s("mix_full"), 1)
    pe.wait_ge(*at("qkv_rows", l))
    memory_keys(0)
    memory_keys(1)
    pe.wait_ge(*at("qk_rot", l))
    for b in range(3):
        for i in range(2):
            for t in range(NT):
                if b < 2:
                    h = 2 * (2 * b + i)
                    src = m.rot[:, t, h:h + 2, :].rearrange("p a b -> p (a b)")
                else:
                    src = m.kd[:, t, i].rearrange("p a b -> p (a b)")
                ins = nc.tensor.transpose(ps[:, (6, 7, 0)[b], i * T + t * P:i * T + (t + 1) * P], src, m.ident)
        ins.then_inc(m.s("qk_T"), 1)
    pe.wait_ge(*at("q_cols", l))
    pe.wait_ge(*at("k_cols", l))
    pe.wait_ge(*at("xk_cols", l, 2))
    for t in range(NT):
        if t == 1:
            pe.wait_ge(*at("gm_rows", l))
        for h in range(NQ):
            r = (h % 2) * HD
            ins = mm(ps[:, 4 * t + 2 * (h % 2) + h // 4, (h // 2 % 2) * T:(h // 2 % 2 + 1) * T],
                     m.qT[r:r + HD, h // 2, t * P:(t + 1) * P], m.kT[r:r + HD, h // 4, :], start=True, stop=True)
        ins.then_inc(m.s("sc_full"), 1)
    for t in range(NT):
        pe.wait_ge(*at("sc_exp", l, NQ * (t + 1)))
        for b in range(4):
            for j in (2 * b, 2 * b + 1):
                for kt in range(2):
                    ins = nc.tensor.transpose(ps[:, 4 * t + b, (j % 2) * T + kt * P:(j % 2) * T + (kt + 1) * P],
                                              m.p[:, j, kt * P:(kt + 1) * P], m.ident)
            ins.then_inc(m.s("pT_full"), 1)
        pe.wait_ge(*at("pT_a", l, 2 * (t + 1)))
        pe.wait_ge(*at("pT_d", l, 2 * (t + 1)))
        for j in range(NQ):
            h = 4 * (j // 2 % 2) + 2 * (j % 2) + j // 4
            for kt in range(2):
                c = NQ * HD + NKV * HD + (h // 4) * HD
                ins = mm(ps[:, 4 * t, h * HD:(h + 1) * HD], m.pT[:, j, kt, :], m.raw[:, kt, c:c + HD],
                         start=kt == 0, stop=kt == 1)
        ins.then_inc(m.s("at_full"), 1)
    memory_keys(2)
    pe.wait_ge(*at("br_xn", l))
    pe_columns(m, m.xn, m.s("br_T"))
    pe.wait_ge(*at("xk_cols", l, 3))
    into_residual(W_OUT1, H_OUT, "br_cols_d", 4, "out1_full")

    memory_keys(3)
    pe.wait_ge(*at("h2_xn", l))
    pe_columns(m, m.xn, m.s("h2_T"), range(3))
    pe.wait_ge(*at("xk_cols", l))
    pe_columns(m, m.xn, m.s("h2_T"), (3,))
    pe.wait_ge(*at("h2_cols_d", l))
    for j in range(2):
        for i in (2 * j, 2 * j + 1):
            w = parts(H_XQ + i, T)
            for c in range(2):
                for k in range(KD):
                    start, ins = exact(m, ps[:, 4 + i, c * T:(c + 1) * T], [a[:, k, c * P:(c + 1) * P] for a in w],
                                       [a[:, k, :] for a in columns], k == 0, k == KD - 1)
                    if release:
                        free_released(start)
            ins.then_inc(m.s("xq_full"), 1)
        release.append(W_XQ + j)
    def memory_values(j):
        w = weights(W_XV + j)
        for t in range(NT):
            for k in range(KD):
                ins = mm(ps[:, 2 * j + t, :], m.memT[:, k, t * P:(t + 1) * P], w[:, k, :], start=k == 0, stop=k == KD - 1)
                if k == 0 and release:
                    free_released(ins)
            ins.then_inc(m.s(f"xv{j}_full"), 1)
        release.append(W_XV + j)

    memory_values(0)
    pe.wait_ge(*at("xq_cols", l))
    for t in range(NT):
        for h in range(XH):
            for k in range(2):
                ins = mm(ps[:, 4 + 2 * t + h // 2, (h % 2) * T:(h % 2 + 1) * T], m.xqT[:, 2 * h + k, t * P:(t + 1) * P],
                         m.xkT[:, 2 * h + k, :], start=k == 0, stop=k == 1)
                if release:
                    free_released(ins)
        ins.then_inc(m.s("xs_full"), 1)
    memory_values(1)
    pe.wait_ge(*at("xp_rows", l))
    for b in range(4):
        mt = b // 2
        for i in range(2):
            for t in range(NT):
                ins = nc.tensor.transpose(ps[:, 4 + b, i * T + t * P:i * T + (t + 1) * P],
                                          m.xp[:, t, 2 * (b % 2) + i, mt * P:(mt + 1) * P], m.ident)
        ins.then_inc(m.s("xpT_full"), 1)
    pe.wait_ge(*at("xpT_a", l))
    pe.wait_ge(*at("xpT_d", l))
    pe.wait_ge(*at("xv1_rows", l))
    for c in range(KD):
        h = c // 2
        for mt in range(2):
            ins = mm(ps[:, c // 2, (c % 2) * T:(c % 2 + 1) * T], m.xv[:, mt, c * P:(c + 1) * P], m.xpT[:, mt, h, :],
                     start=mt == 0, stop=mt == 1)
        if c % 2:
            ins.then_inc(m.s("xo_full"), 1)
    into_residual(W_XO, H_XO, "xo_cols_d", 2, "out2_full")
    tensor_experts(m, pe, l, release, free_released, columns_of)


def tensor_experts(m, pe, l, release, free_released, columns_of):
    nc, ps, at = m.nc, m.ps, m.at
    mm = nc.tensor.matmul
    columns_of(m.xn, "h3_xn", "h3_T", "h3_cols_a", "h3_cols_d")
    router = m.par1("router").rearrange("p (k e) -> p k e", e=E)
    for t in range(NT):
        for k in range(KD):
            ins = mm(ps[:, 4 + t, 0:E], m.hT[:, k, t * P:(t + 1) * P], router[:, k, :], start=k == 0, stop=k == KD - 1)
            if release:
                free_released(ins)
        ins.then_inc(m.s("router_full"), 1)
    pe.wait_ge(*at("aff_rows", l))
    for t in range(NT):
        ins = nc.tensor.transpose(ps[0:E, 6, t * P:(t + 1) * P], m.aff[:, t, :], m.ident)
    ins.then_inc(m.s("aff_T"), 1)
    pe.wait_ge(*at("top_found", l))
    mm(ps[:, 7, 0:E * CAP], m.const("ones")[0:E, :], m.diag[0:E].rearrange("p e c -> p (e c)"), start=True, stop=True)
    for i in range(2):
        ins = nc.tensor.transpose(ps[:, 6, i * E:(i + 1) * E], m.rep[0:E, i].rearrange("p g c -> p (g c)"), m.ident[0:E, 0:E])
    ins.then_inc(m.s("top_T"), 1)
    pe.wait_ge(*at("onehot", l))
    pe.wait_ge(*at("router_exp", l))
    for nh in range(2):
        for t in range(NT):
            mm(ps[:, 4 + 2 * nh + t, :], m.ident, m.x[:, t, nh * BANK:(nh + 1) * BANK], start=True, stop=False,
               skip_group_check=True)
    w = [slab(m, s, KD, BANK) for s in range(SLOTS)]

    def expert(e, first):
        n = l * E + (e + 1)
        gate_up = [m.first_gate[:, g] if first and g < GATE_SLOTS else w[g] for g in range(4)]

        def slab_landed(s):
            if s >= GATE_SLOTS:
                pe.wait_ge(m.landed[s], l * LANDED1_LAYER[s] + (LANDED1[s] + 16) + e * 16)
            elif first:
                pe.wait_ge(*at("first_gate_loaded", l))
            else:
                pe.wait_ge(m.landed[s], l * LANDED1_LAYER[s] + LANDED1[s] + e * 16)

        for k in range(KD):
            for t in range(NT):
                ins = mm(ps[:, 0, k * CAP:(k + 1) * CAP], m.xn[:, t, k * P:(k + 1) * P], m.onehot[:, t, bass.ds(e * CAP, CAP)],
                         start=t == 0, stop=t == NT - 1)
        ins.then_inc(m.s("tok_full"), 1)
        pe.wait_ge(m.s("tok_cols"), n)
        for k in range(KD):
            for g in range(4):
                if k == 0:
                    slab_landed(g)
                ins = mm(ps[32 * g:32 * g + CAP, 1, :], m.tokT[:, k, :], gate_up[g][:, k, :], start=k == 0, stop=k == KD - 1)
                if k == KD - 1 and (g >= GATE_SLOTS or not first):
                    ins.then_inc(m.free[g] if g < 3 else m.s("gu_full"), 1)
        pe.wait_ge(m.s("gu_rows"), n)
        for c in range(4):
            ins = nc.tensor.transpose(ps[:, 0, c * P:(c + 1) * P], m.gu[:, c * P:(c + 1) * P], m.ident)
            if c == 0:
                ins.then_inc(m.free[3], 1)
        ins.then_inc(m.s("gu_T"), 1)
        pe.wait_ge(m.s("hid_cols"), n)
        for nh in range(2):
            slab_landed(4 + nh)
            for k in range(KD):
                c, half = k % 4, k // 4
                ins = mm(ps[32 * c:32 * c + CAP, 2 + nh, :], m.hid[:, c, half, :], w[4 + nh][:, k, :],
                         start=half == 0, stop=half == 1)
                if nh == 1 and k == 0:
                    ins.then_inc(m.free[4], 1)
            ins.then_inc(m.s("dn_full"), 1)
        pe.wait_ge(m.s("pick"), n)
        for nh in range(2):
            pe.wait_ge(m.s("dn_rows_a" if nh == 0 else "dn_rows_d"), n)
            for t in range(NT):
                ins = mm(ps[:, 4 + 2 * nh + t, :], m.pick[:, t * P:(t + 1) * P], m.dn[:, nh, :], start=False, stop=True,
                         skip_group_check=True)
                if nh == 0 and t == 0:
                    ins.then_inc(m.free[5], 1)
        ins.then_inc(m.s("acc_full"), 1)

    expert(0, True)
    with pe.Fori(1, E) as e:
        expert(e, False)


def norm_squares(m, act, x_ready, done):
    sem, count = x_ready
    for t in range(NT):
        act.wait_ge(sem, count - (NT - 1 - t))
        act_squares(m, act, [m.x[:, t, :]], [m.xn[:, t, :]], [m.stat[:, t:t + 1]], D ** -0.5, done)


def two(bank):
    return bank.rearrange("p (a b) -> p a b", b=T)


S_MAX, S_SUM, S_INV = 128, 144, 160
S_XMAX, S_XSUM, S_XINV = 176, 184, 192
S_RMAX, S_RSUM, S_RINV = 200, 202, 204


def scalar_first(m, act, l):
    nc, ps, at, s = m.nc, m.ps, m.at, m.s
    go = nc.scalar.activation
    col = lambda c: m.stat[:, c:c + 1]

    def memory_keys(b):
        act.wait_ge(*at("xk_full", l, b + 1))
        go(m.xkT[:, 2 * b:2 * b + 2, :], two(ps[:, (1, 2, 5, 3)[b], :]), ACT.Copy).then_inc(s("xk_cols"), 1)

    def split(q, *buffer_used):
        i, *half = half1(m, q)
        landed1(m, act, l, i)
        if buffer_used:
            act.wait_ge(*at(buffer_used[0], l, *buffer_used[1:]))
        high(m, *half).then_inc(s("w1_hi"), 1)

    norm_squares(m, act, m.prev("x_routed", l), s("h1_sq"))
    split(0)
    split(1)
    act.wait_ge(*at("par1_set", l))
    act_high_columns(m, act, m.hT_hi1, m.par1("mix_g"), *at("h1_T", l, 0), s("h1_cols_a"))
    for i in range(4):
        if i % 2 == 0:
            split(i + 2, "half_used", i // 2 + 1)
            split(i + 3, "uv_full", i + 2)
        act.wait_ge(*at("uv_full", l, i + 1))
        go((m.ug, m.vg)[i // 2][:, i % 2, :], ps[:, 4 + i, :], ACT.Gelu_apprx_tanh).then_inc(s("uv_gelu"), 1)
    act.wait_ge(*at("uv_gelu", l))
    act_squares(m, act, [m.vg[:, t, :] for t in range(NT)], [m.xn[:, t, 0:GM_W] for t in range(NT)],
                [col(4 + t) for t in range(NT)], GM_W ** -0.5, s("v_sq"))
    split(6, "half_used", 3)
    memory_keys(0)
    memory_keys(1)
    for b in range(2):
        act.wait_ge(*at("qk_T", l, b + 1))
        go(m.qT[:, 2 * b:2 * b + 2, :], two(ps[:, 6 + b, :]), ACT.Copy).then_inc(s("q_cols"), 1)
    for t in range(NT):
        act.wait_ge(*at("sc_max", l, t + 1))
        if t:
            act.wait_ge(*at("pT_full", l, 4 * t))
        for j in range(NQ):
            h = 4 * (j // 2 % 2) + 2 * (j % 2) + j // 4
            go(m.p[:, j, :], two(ps[:, 4 * t + j // 2, :])[:, j % 2, :], ACT.Exp, bias=col(S_MAX + NQ * t + j),
               scale=HD ** 0.5, accum_out=col(S_SUM + NQ * t + h)).then_inc(s("sc_exp"), 1)
        if t:
            act.wait_ge(*at("at_full", l, t))
        for b in range(2):
            act.wait_ge(*at("pT_full", l, 4 * t + b + 1))
            go(m.pT[:, 2 * b:2 * b + 2], ps[:, 4 * t + b, :].rearrange("p (a k b) -> p a k b", a=2, b=P), ACT.Copy)\
                .then_inc(s("pT_a"), 1)
    for t in range(NT):
        act.wait_ge(*at("at_rows", l, t + 1))
        for br in range(2):
            part = slice(br * GM_W, (br + 1) * GM_W)
            go(m.xn[:, t, part], m.merged[:, t, part], ACT.Square, scale=GM_W ** -0.5,
               accum_out=col(6 + 2 * t + br)).then_inc(s("br_sq"), 1)
    split(H_OUT, "at_full")
    memory_keys(2)
    act_high_columns(m, act, m.hT_hi1, m.par1("branch_g"), *at("br_T", l, 0), s("br_cols_a"), (0, 1))
    split(H_OUT + 1, "br_xn")
    act_high_columns(m, act, m.hT_hi1, m.par1("branch_g"), *at("br_T", l, 0), s("br_cols_a"), (2, 3))
    split(H_OUT + 2, "half_used", 4)
    split(H_OUT + 3, "out1_full", 2)
    norm_squares(m, act, at("x_mixed", l), s("h2_sq"))
    split(H_XQ, "out1_full")
    split(H_XQ + 1, "out1_full")
    memory_keys(3)
    act_high_columns(m, act, m.hT_hi1, m.par1("x_g"), *at("h2_T", l, 0), s("h2_cols_a"))
    for b in range(4):
        if b < 2:
            split(H_XQ + 2 + b, "xq_full", b + 1)
        act.wait_ge(*at("xq_full", l, b + 1))
        go(m.xqT[:, 2 * b:2 * b + 2, :], two(ps[:, 4 + b, :]), ACT.Copy).then_inc(s("xq_cols"), 1)
    split(H_XO, "xq_full")
    split(H_XO + 1, "xq_full")
    def memory_values(j):
        for t in range(NT):
            act.wait_ge(*at(f"xv{j}_full", l, t + 1))
            go(m.xv[:, t, j * BANK:(j + 1) * BANK], ps[:, 2 * j + t, :], ACT.Copy).then_inc(s(f"xv{j}_rows"), 1)

    memory_values(0)
    for t in range(NT):
        act.wait_ge(*at("xs_max", l, t + 1))
        for h in range(XH):
            go(m.xp[:, t, h, :], two(ps[:, 4 + 2 * t + h // 2, :])[:, h % 2, :], ACT.Exp, bias=col(S_XMAX + XH * t + h),
               scale=XD ** -0.5, accum_out=col(S_XSUM + XH * t + h)).then_inc(s("xs_exp"), 1)
    memory_values(1)
    for b in range(2):
        act.wait_ge(*at("xpT_full", l, b + 1))
        go(m.xpT[:, 0, 2 * b:2 * b + 2, :], two(ps[:, 4 + b, :]), ACT.Copy).then_inc(s("xpT_a"), 1)
    for b in range(4):
        act.wait_ge(*at("xo_full", l, b + 1))
        go(m.hT_hi1[:, 2 * b:2 * b + 2, :], two(ps[:, b, :]), ACT.Copy).then_inc(s("xo_cols_a"), 1)
    split(H_XO + 2, "half_used", 5)
    split(H_XO + 3, "out2_full", 2)
    norm_squares(m, act, at("x_attended", l), s("h3_sq"))
    act_columns(m, act, m.hT, m.par1("ffn_g"), *at("h3_T", l, 0), s("h3_cols_a"))
    act.wait_ge(*at("router_max", l))
    for t in range(NT):
        go(m.aff[:, t, :], ps[:, 4 + t, 0:E], ACT.Exp, bias=col(S_RMAX + t), accum_out=col(S_RSUM + t)).then_inc(s("router_exp"), 1)
    gate = ps[:, 0, :].rearrange("p (c n) -> p c n", n=P)[:, :, 0:2 * CAP]
    with act.Fori(0, E) as e:
        n = e + l * E + 1
        act.wait_ge(s("gu_full"), n)
        go(m.gu, ps[:, 1, :], ACT.Copy).then_inc(s("gu_rows"), 1)
        act.wait_ge(s("gu_T"), n)
        go(m.sil, gate, ACT.Silu).then_inc(s("gate_silu"), 1)
        act.wait_ge(s("dn_full"), 2 * n - 1)
        go(m.dn[:, 0, :], ps[:, 2, :], ACT.Copy).then_inc(s("dn_rows_a"), 1)


def gpsimd_first(m, pool, l):
    at, s = m.at, m.s
    pool.wait_ge(*m.prev("x_routed", l))
    pool.dma_start(m.par[:, SOON:SOON + NLATE1], m.d["late1"][bass.ds(l, 1)].rearrange("l p n -> p (l n)"))\
        .then_inc(s("late1_loaded"), 16)
    gpsimd_rstd(m, pool, l, "h1", "h1_sq", 0, NT, 0)
    gpsimd_rstd(m, pool, l, "v", "v_sq", 4, NT, 0)
    gpsimd_rstd(m, pool, l, "qk", "qk_ss", 32, NT * HEADS_QK, 32)
    gpsimd_rstd(m, pool, l, "br", "br_sq", 6, 2 * NT, 0)
    gpsimd_rstd(m, pool, l, "h2", "h2_sq", 0, NT, 0)
    gpsimd_rstd(m, pool, l, "h3", "h3_sq", 0, NT, 0)
    pool.dma_start(m.soon[:, :], m.d["soon"][bass.ds(l + 1, 1)].rearrange("l p n -> p (l n)")).then_inc(s("soon1_loaded"), 16)


def add_into_x(m, dve, full, base, done, halves=(0, 1)):
    for i in range(2 * halves[0], 2 * halves[-1] + 2):
        nh, t = i // 2, i % 2
        dve.wait_ge(full, base + i + 1)
        xs = m.x[:, t, nh * BANK:(nh + 1) * BANK]
        m.nc.vector.tensor_tensor(xs, xs, m.ps[:, 4 + i, :], ALU.add).then_inc(done, 1)


def bc(ap, n):
    return ap.unsqueeze(len(ap.shape)).to_broadcast([*ap.shape, n])


def vector_norm(m, dve, l, name, gain):
    dve.wait_ge(*m.at(name + "_rstd", l))
    dve_scale_rows(m, m.xn, m.x, m.stat[:, 64:66], m.s(name + "_xn"))
    dve_columns(m, dve, m.hT, gain, *m.at(name + "_T", l, 0), m.s(name + "_cols_d"))


def vector_parts(m, dve, l):
    def split(q):
        dve.wait_ge(*m.at("w1_hi", l, q + 1))
        low(m, *half1(m, q)[1:]).then_inc(m.s("w1_lo"), 1)

    def high_norm(name, gain, q, by_half):
        dve.wait_ge(*m.at(name + "_rstd", l))
        dve_scale_rows(m, m.xn, m.x, m.stat[:, 64:66], m.s(name + "_xn"))
        split(q)
        for half in range(2):
            if half and by_half:
                split(q + 1)
            dve_low_columns(m, dve, m.hT_lo, m.hT_hi1, gain, *m.at(name + "_cols_a", l, 0), m.s(name + "_cols_d"),
                            (2 * half, 2 * half + 1))
        if not by_half:
            split(q + 1)
    return split, high_norm


def vector_first(m, dve, l):
    vector_mix(m, dve, l)
    vector_memory(m, dve, l)
    vector_route(m, dve, l)
    vector_experts(m, dve, l)


def vector_set_par(m, dve, l, loaded, done):
    dve.wait_ge(*m.prev(loaded, l))
    m.nc.vector.tensor_copy(m.par[:, 0:SOON], m.soon[:, :]).then_inc(m.s(done), 1)
    dve.wait_ge(*m.at(done, l))


def vector_mix(m, dve, l):
    v, ps, at, s = m.nc.vector, m.ps, m.at, m.s
    vector_set_par(m, dve, l, "soon1_loaded", "par1_set")
    split, high_norm = vector_parts(m, dve, l)
    high_norm("h1", m.par1("mix_g"), H_IN, True)
    for q in range(2, H_OUT):
        split(q)
    dve.wait_ge(*at("late1_loaded", l))
    dve.wait_ge(*at("v_rstd", l))
    for t in range(NT):
        v.scalar_tensor_tensor(m.vg[:, t, :], m.vg[:, t, :], m.stat[:, 68 + t:69 + t], m.par1("v_g"), ALU.mult, ALU.mult)\
            .then_inc(s("v_norm"), 1)
    for i in range(4):
        dve.wait_ge(*at("qkv_full", l, i + 1))
        if i < 2:
            v.tensor_copy(m.raw[:, i, 0:BANK], ps[:, i, :]).then_inc(s("qkv_rows"), 1)
        else:
            v.tensor_copy(m.raw[:, i - 2, BANK:768], ps[:, i, 0:256]).then_inc(s("qkv_rows"), 1)
    qk = m.raw[:, :, 0:HEADS_QK * HD]
    heads = m.raw.rearrange("p t (h d) -> p t h d", d=HD)[:, :, 0:HEADS_QK, :]
    dve.wait_ge(*at("qkv_rows", l))
    v.tensor_tensor(m.rot.rearrange("p t h d -> p t (h d)"), qk, qk, ALU.mult)
    dve.drain()
    ss = m.stat[:, 32:32 + NT * HEADS_QK].rearrange("p (t h) -> p t h", t=NT)
    v.tensor_reduce(ss, m.rot, axis=AX.X, op=ALU.add).then_inc(s("qk_ss"), 1)
    dve.wait_ge(*at("qk_rstd", l))
    rstd = m.stat[:, 96:96 + NT * HEADS_QK].rearrange("p (t h) -> p t h", t=NT)
    v.tensor_tensor(heads, heads, bc(rstd, HD), ALU.mult)
    dve.drain()
    for h0, h1, g in ((0, NQ, 0), (NQ, HEADS_QK, 1)):
        gain = m.par1("qk_g")[:, g * HD:(g + 1) * HD].unsqueeze(1).unsqueeze(1).to_broadcast([P, NT, h1 - h0, HD])
        v.tensor_tensor(heads[:, :, h0:h1], heads[:, :, h0:h1], gain, ALU.mult)
    dve.drain()
    pairs = m.raw.rearrange("p t (h i two) -> p t h i two", i=HD // 2, two=2)[:, :, 0:HEADS_QK]
    rot = m.rot.rearrange("p t h (i two) -> p t h i two", two=2)
    cos, sin = (m.const(n).rearrange("p (t i) -> p t i", t=NT) for n in ("cos1", "sin1"))
    t0, t1 = (m.tmp[:, i].rearrange("p (t h i) -> p t h i", t=NT, h=HEADS_QK) for i in range(2))
    for t in range(NT):
        c, sn = (a[:, t].unsqueeze(1).to_broadcast([P, HEADS_QK, HD // 2]) for a in (cos, sin))
        v.tensor_tensor(rot[:, t, :, :, 0], pairs[:, t, :, :, 0], c, ALU.mult)
        v.tensor_tensor(rot[:, t, :, :, 1], pairs[:, t, :, :, 0], sn, ALU.mult)
        v.tensor_tensor(t0[:, t], pairs[:, t, :, :, 1], sn, ALU.mult)
        v.tensor_tensor(t1[:, t], pairs[:, t, :, :, 1], c, ALU.mult)
    dve.drain()
    for t in range(NT):
        v.tensor_tensor(rot[:, t, :, :, 0], rot[:, t, :, :, 0], t0[:, t], ALU.subtract)
        v.tensor_tensor(rot[:, t, :, :, 1], rot[:, t, :, :, 1], t1[:, t], ALU.add)
    dve.drain()
    for t in range(NT):
        ins = v.tensor_copy(m.kd[:, t], m.rot[:, t, NQ:, :].unsqueeze(2).to_broadcast([P, NKV, 2, HD]))
    ins.then_inc(s("qk_rot"), 1)
    dve.wait_ge(*at("qk_T", l))
    v.tensor_copy(m.kT, two(ps[:, 0, :])).then_inc(s("k_cols"), 1)
    for t in range(NT):
        dve.wait_ge(*at("mix_full", l, t + 1))
        for g in range(GM_G):
            part = slice(g * P, (g + 1) * P)
            v.scalar_tensor_tensor(m.merged[:, t, part], ps[:, 4 + t, part], m.par1("b_s")[:, g:g + 1], m.ug[:, t, part],
                                   ALU.add, ALU.mult).then_inc(s("gm_rows"), 1)
    for t in range(NT):
        dve.wait_ge(*at("sc_full", l, t + 1))
        mx = m.stat[:, S_MAX + NQ * t:S_MAX + NQ * (t + 1)]
        v.tensor_reduce(mx, ps[:, 4 * t:4 * t + 4, :].rearrange("p b (j n) -> p (b j) n", n=T), axis=AX.X, op=ALU.max)
        dve.drain()
        v.tensor_scalar(mx, mx, -HD ** 0.5, None, ALU.mult).then_inc(s("sc_max"), 1)
    for t in range(NT):
        if t:
            dve.wait_ge(*at("at_full", l, t))
        for b in (2, 3):
            dve.wait_ge(*at("pT_full", l, 4 * t + b + 1))
            v.tensor_copy(m.pT[:, 2 * b:2 * b + 2], ps[:, 4 * t + b, :].rearrange("p (a k b) -> p a k b", a=2, b=P))\
                .then_inc(s("pT_d"), 1)
        inv = m.stat[:, S_INV + NQ * t:S_INV + NQ * (t + 1)]
        dve.wait_ge(*at("sc_exp", l, NQ * (t + 1)))
        v.reciprocal(inv, m.stat[:, S_SUM + NQ * t:S_SUM + NQ * (t + 1)])
        dve.drain()
        dve.wait_ge(*at("at_full", l, t + 1))
        v.tensor_tensor(m.merged[:, t, GM_W:].rearrange("p (h d) -> p h d", d=HD),
                        ps[:, 4 * t, :].rearrange("p (h d) -> p h d", d=HD), bc(inv, HD), ALU.mult).then_inc(s("at_rows"), 1)
    dve.wait_ge(*at("br_rstd", l))
    for t in range(NT):
        for br in range(2):
            part = slice(br * GM_W, (br + 1) * GM_W)
            c = 70 + 2 * t + br
            v.tensor_scalar(m.xn[:, t, part], m.merged[:, t, part], m.stat[:, c:c + 1], None, ALU.mult).then_inc(s("br_xn"), 1)
    for half in range(2):
        split(H_OUT + half)
        dve_low_columns(m, dve, m.hT_lo, m.hT_hi1, m.par1("branch_g"), *at("br_cols_a", l, 0), s("br_cols_d"), (2 * half, 2 * half + 1))
    for half in range(2):
        split(H_OUT + 2 + half)
        add_into_x(m, dve, *at("out1_full", l, 0), s("x_mixed"), (half,))


def vector_memory(m, dve, l):
    v, ps, at, s = m.nc.vector, m.ps, m.at, m.s
    split, high_norm = vector_parts(m, dve, l)
    high_norm("h2", m.par1("x_g"), H_XQ, False)
    for q in range(H_XQ + 2, H_XO + 2):
        split(q)
    for t in range(NT):
        dve.wait_ge(*at("xs_full", l, t + 1))
        mx = m.stat[:, S_XMAX + XH * t:S_XMAX + XH * (t + 1)]
        v.tensor_reduce(mx, ps[:, 4 + 2 * t:4 + 2 * t + 2, :].rearrange("p b (j n) -> p (b j) n", n=T), axis=AX.X, op=ALU.max)
        dve.drain()
        v.tensor_scalar(mx, mx, -XD ** -0.5, None, ALU.mult).then_inc(s("xs_max"), 1)
    for t in range(NT):
        dve.wait_ge(*at("xs_exp", l, XH * (t + 1)))
        inv = m.stat[:, S_XINV + XH * t:S_XINV + XH * (t + 1)]
        v.reciprocal(inv, m.stat[:, S_XSUM + XH * t:S_XSUM + XH * (t + 1)])
        dve.drain()
        v.tensor_tensor(m.xp[:, t], m.xp[:, t], bc(inv, T), ALU.mult).then_inc(s("xp_rows"), 1)
    for b in range(2):
        dve.wait_ge(*at("xpT_full", l, b + 3))
        v.tensor_copy(m.xpT[:, 1, 2 * b:2 * b + 2, :], two(ps[:, 6 + b, :])).then_inc(s("xpT_d"), 1)
    for b in range(4):
        dve.wait_ge(*at("xo_cols_a", l, b + 1))
        two_k = slice(2 * b, 2 * b + 2)
        v.tensor_tensor(m.hT_lo[:, two_k, :], two(ps[:, b, :]), m.hT_hi1[:, two_k, :], ALU.subtract).then_inc(s("xo_cols_d"), 1)
    for half in range(2):
        split(H_XO + 2 + half)
        add_into_x(m, dve, *at("out2_full", l, 0), s("x_attended"), (half,))


def vector_route(m, dve, l):
    v, ps, at, s = m.nc.vector, m.ps, m.at, m.s
    vector_norm(m, dve, l, "h3", m.par1("ffn_g"))
    dve.wait_ge(*at("router_full", l))
    mx = m.stat[:, S_RMAX:S_RMAX + NT]
    v.tensor_reduce(mx, ps[:, 4:6, 0:E], axis=AX.X, op=ALU.max)
    dve.drain()
    v.tensor_scalar(mx, mx, -1.0, None, ALU.mult).then_inc(s("router_max"), 1)
    dve.wait_ge(*at("router_exp", l))
    inv = m.stat[:, S_RINV:S_RINV + NT]
    v.reciprocal(inv, m.stat[:, S_RSUM:S_RSUM + NT])
    dve.drain()
    v.tensor_tensor(m.aff, m.aff, bc(inv, E), ALU.mult).then_inc(s("aff_rows"), 1)
    dve.wait_ge(*at("aff_T", l))
    v.tensor_copy(m.work[0:E, 0, :], ps[0:E, 6, 0:T])
    dve.drain()
    for r in range(CAP // 8):
        best, work = m.gates[0:E, 8 * r:8 * r + 8], m.work[0:E, r % 2, :]
        v.max(best, work)
        dve.drain()
        v.max_index(m.top_i[0:E, 8 * r:8 * r + 8], best, work)
        v.match_replace(m.work[0:E, 1 - r % 2, :], best, work, -1.0)
        dve.drain()
    slots, gates = m.slots[0:E], m.gates[0:E]
    v.tensor_copy(slots, m.top_i[0:E, :])
    dve.drain()
    v.tensor_copy(m.rep[0:E, 0], slots.unsqueeze(1).to_broadcast([E, 4, CAP]))
    v.tensor_copy(m.rep[0:E, 1], gates.unsqueeze(1).to_broadcast([E, 4, CAP]))
    v.tensor_tensor(m.diag[0:E], slots.unsqueeze(1).to_broadcast([E, E, CAP]), bc(m.const("expert_diag")[0:E, :], CAP),
                    ALU.mult).then_inc(s("top_found"), 1)
    dve.wait_ge(*at("top_T", l))
    v.tensor_copy(m.topc, ps[:, 6, 0:2 * E].rearrange("p (i e) -> p i e", e=E)).then_inc(s("onehot"), 1)
    for t in range(NT):
        v.tensor_scalar(m.onehot[:, t, :], ps[:, 7, :], m.const("iota_col")[:, t:t + 1], None, ALU.is_equal)\
            .then_inc(s("onehot"), 1)
    dve.drain()


def vector_experts(m, dve, l):
    v, ps, at, s = m.nc.vector, m.ps, m.at, m.s
    up = ps[:, 0, :].rearrange("p (c n) -> p c n", n=P)[:, :, 2 * CAP:]
    with dve.Fori(0, E) as e:
        n = e + l * E + 1
        dve.wait_ge(s("tok_full"), n)
        v.tensor_tensor(m.tokT, ps[:, 0, 0:KD * CAP].rearrange("p (k c) -> p k c", c=CAP), bc(m.par1("ffn_g"), CAP), ALU.mult)\
            .then_inc(s("tok_cols"), 1)
        v.tensor_scalar(m.pick, m.const("iota_row"), m.topc[:, 0, bass.ds(e, 1)], m.topc[:, 1, bass.ds(e, 1)],
                        ALU.is_equal, ALU.mult).then_inc(s("pick"), 1)
        dve.wait_ge(s("gate_silu"), n)
        v.tensor_tensor(m.hid.rearrange("p c h n -> p c (h n)"), m.sil, up, ALU.mult).then_inc(s("hid_cols"), 1)
        dve.wait_ge(s("dn_full"), 2 * n)
        v.tensor_copy(m.dn[:, 1, :], ps[:, 3, :]).then_inc(s("dn_rows_d"), 1)
    dve.wait_ge(*at("acc_full", l))
    for i in range(4):
        nh, t = i // 2, i % 2
        v.tensor_copy(m.x[:, t, nh * BANK:(nh + 1) * BANK], ps[:, 4 + i, :]).then_inc(s("x_routed"), 1)


def vector_between(m, dve):
    dve.wait_ge(*m.at("fin1_loaded", 0))
    dve.wait_ge(*m.at("f1_rstd", 0))
    for t in range(NT):
        m.nc.vector.scalar_tensor_tensor(m.x[:, t, :], m.x[:, t, :], m.stat[:, 64 + t:65 + t], m.fin1, ALU.mult, ALU.mult)\
            .then_inc(m.s("x_first"), 1)


def scalar_between(m, act):
    norm_squares(m, act, m.prev("x_routed", L), m.s("f1_sq"))


def gpsimd_between(m, pool):
    pool.wait_ge(*m.at("x_attended", L - 1))
    pool.dma_start(m.fin1, m.d["fix"][:, KD:KD + D]).then_inc(m.s("fin1_loaded"), 16)
    gpsimd_rstd(m, pool, 0, "f1", "f1_sq", 0, NT, 0)


def sync_second(m, sp, l):
    d = m.d
    after_first = [L * n for n in HELD1_LAYER]

    def free(i):
        g = PLAN2[i]
        ring_wait(m, sp, g.slot, l * HELD2[g.slot] + (after_first[g.slot] + g.held))

    def load(i, dst, src):
        sp.dma_start(dst, src).then_inc(m.landed[PLAN2[i].slot], 16)

    def layer(name):
        return d[name][bass.ds(l, 1)].rearrange("l (k p) n -> p (l k) n", p=P)

    def whole(i, name, c0, k=KD, n=BANK, k0=0):
        free(i)
        load(i, slab(m, PLAN2[i].slot, k, n), layer(name)[:, k0:k0 + k, c0:c0 + n])

    lat0 = SHIFT_TILES * P + QL
    for j in range(4):
        whole(W_IN2 + j, "w_in_2", j * BANK)
    free(W_LAT)
    keys, kv_up, q_up = lat_slab(m)
    load(W_LAT, keys, layer("w_in_2")[:, :, lat0:lat0 + KVL + PE_D])
    load(W_LAT, kv_up, layer("w_kv_up_2"))
    load(W_LAT, q_up, layer("w_q_up_2"))
    for j in range(4):
        whole(W_GATES + j, "w_in_2", SHIFT_TILES * P + LAT + j * BANK)
    whole(W_ORW, "w_out_rwkv_2", 0, k=4, n=D)
    whole(W_OMLA, "w_out_mla_2", 0, k=4, n=D)
    for j in range(2):
        whole(W_OUT2 + j, "w_out_2", j * BANK)
    for j in range(NUP):
        i = W_UP + j
        free(i)
        if j == 1:
            sp.wait_ge(*m.at("merged", l))
        w = layer("w_ffn_up_2")
        for part in range(2):
            load(i, up_slab(m, i)[:, part], w[:, :, part * FFN + j * T:part * FFN + (j + 1) * T])
    for j in range(NDN):
        whole(W_DN + j, "w_ffn_down_2", 0, k=min(4, NF - 4 * j), n=D, k0=4 * j)


def lat_slab(m):
    r = m.ring[:, PLAN2[W_LAT].slot]
    a = KD * (KVL + PE_D)
    b = a + MH * 2 * NOPE
    return (r[:, 0:a].rearrange("p (k n) -> p k n", k=KD), r[:, a:b].unsqueeze(1),
            r[:, b:b + 2 * MH * QKD].rearrange("p (k n) -> p k n", k=2))


def up_slab(m, i):
    return m.ring[:, PLAN2[i].slot].rearrange("p (g k n) -> p g k n", g=2, k=KD)


def landed2(m, eng, l, i):
    g = PLAN2[i]
    eng.wait_ge(m.landed[g.slot], l * LANDED2[g.slot] + (L * LANDED1_LAYER[g.slot] + g.landed))


def tensor_second(m, pe, l):
    nc, ps, at, s = m.nc, m.ps, m.at, m.s
    mm = nc.tensor.matmul
    release = []

    def landed(i):
        landed2(m, pe, l, i)

    def weights(i, k=KD, n=BANK):
        landed(i)
        return slab(m, PLAN2[i].slot, k, n)

    def used(i):
        return m.free[PLAN2[i].slot]

    def free_released(ins):
        if release:
            ins.then_inc(used(release.pop()), 1)

    def tile_products(out, w, c, rhs, ks):
        for i, k in enumerate(ks):
            ins = mm(out, w[:, k, c:c + P], rhs[:, k, :], start=i == 0, stop=i == len(ks) - 1)
            if i == 0:
                free_released(ins)
        return ins

    def norm_columns(name):
        pe.wait_ge(*at(name + "_xn", l))
        pe_columns(m, m.xn, s(name + "_T"))
        pe.wait_ge(*at(name + "_cols_a", l))
        pe.wait_ge(*at(name + "_cols_d", l))

    norm_columns("n1")
    columns = (m.n1_hi, m.n1_lo)

    def parts(q):
        pe.wait_ge(*at("w2_lo", l, q + 1))
        return half2(m, q)[0:2]

    for q in range(SHIFT_TILES // 2):
        w = parts(q)
        for c in range(2):
            for k in range(KD):
                first, ins = exact(m, half_bank(m, (4, 5, 6, 7, 0, 1, 2)[q], c), [a[:, k, c * P:(c + 1) * P] for a in w],
                                   [a[:, k, :] for a in columns], k == 0, k == KD - 1)
                free_released(first)
        ins.then_inc(s("rw_full"), 1)
        if q % 2:
            release.append(W_IN2 + q // 2)
        if q == 5:
            pe.wait_ge(*at("kk_sq", l))
            for b in range(2):
                mm(ps[:, 6 + b, :], m.const("head_sum"), m.sq[:, 2 * b:2 * b + 2, :], start=True, stop=True)\
                    .then_inc(s("kk_full"), 1)
    keys = lat_slab(m)[0]
    landed(W_LAT)
    pe.wait_ge(*at("rw_cols", l, 2))
    w = parts(H_OUT2 - 1)
    pe.wait_ge(*at("n1_whole", l))
    for t in range(NT):
        tokens = slice(t * P, (t + 1) * P)
        for k in range(KD):
            first, ins = exact(m, ps[:, 3 + t, 0:QL], [a[:, k, tokens] for a in columns], [a[:, k, :] for a in w],
                               k == 0, k == KD - 1)
            free_released(first)
        if t == NT - 1:
            release.append(W_IN2 + 3)
        for k in range(KD):
            ins = mm(ps[:, 3 + t, QL:LAT], m.hT[:, k, tokens], keys[:, k, :], start=k == 0, stop=k == KD - 1)
            if k == 0:
                free_released(ins)
        ins.then_inc(s("lat_full"), 1)
        if t == 0:
            pe.wait_ge(*at("late2_loaded", l))
            pe.wait_ge(*at("kk_root", l))
            pe.wait_ge(*at("lora_in", l))
            pe.wait_ge(*at("rw_cols", l, 13))
            up = m.par2("lora_up")
            for b in range(4):
                rows = slice(64 * (b // 2), 64 * (b // 2) + 64)
                for i in range(2):
                    tile = 2 * (b % 2) + i
                    ins = mm(half_bank(m, (5, 6, 7, 0)[b], i), up[rows, tile * P:(tile + 1) * P], m.wa[rows, :],
                             start=True, stop=True)
                ins.then_inc(s("lora_full"), 1)
    landed(W_GATES)
    pe.wait_ge(*at("lora_sig", l, 4))
    for step in gate_steps(m, 0, 0):
        step()
    with pe.Fori(0, PAIRS - 1) as p:
        tensor_pair(m, pe, l, p, landed)
    tensor_pair(m, pe, l, PAIRS - 1, landed, last=True)
    release += [W_GATES + j for j in range(4)]
    tensor_mla(m, pe, l, used, free_released)
    pe.wait_ge(*at("o2_cols", l))
    for j, src in ((1, m.o2T), (0, m.yaT)):
        if j == 0:
            pe.wait_ge(*at("ya_cols", l))
        w = weights((W_ORW, W_OMLA)[j], 4, D)
        for i in range(4):
            nh, t = i // 2, i % 2
            for k in range(4):
                ins = mm(ps[:, 4 * j + i, :], src[:, k, t * P:(t + 1) * P], w[:, k, nh * BANK:(nh + 1) * BANK],
                         start=k == 0, stop=k == 3)
                if k == 0:
                    free_released(ins)
            ins.then_inc(s("br2_full"), 1)
        release.append((W_ORW, W_OMLA)[j])
    for half in range(2):
        pe.wait_ge(*at("merged", l, 2 * (half + 1)))
        pe_columns(m, m.xn, s("merged_T"), (2 * half, 2 * half + 1))
    columns = (m.hT_hi, m.hT_lo)
    for j in range(4):
        nh, kh = j // 2, j % 2
        if j < 2:
            pe.wait_ge(*at("merged_cols_d", l, 2 * (j + 1)))
        w = [a.rearrange("p (k n) -> p k n", n=BANK) for a in parts(H_OUT2 + j)]
        for t in range(NT):
            for k in range(KD // 2):
                first, ins = exact(m, ps[:, 4 + 2 * nh + t, :], [a[:, kh * KD // 2 + k, t * P:(t + 1) * P] for a in columns],
                                   [a[:, k, :] for a in w], kh == 0 and k == 0, kh == 1 and k == KD // 2 - 1)
                free_released(first)
            if kh == 1:
                ins.then_inc(s("out3_full"), 1)
        if j == 0:
            ins.then_inc(s("out3_half"), 1)
        elif kh == 1:
            release.append(W_OUT2 + nh)
    norm_columns("n2")
    for j in range(NUP):
        if j >= 4:
            pe.wait_ge(*at("up_act", l, j - 3))
        for g in range(2):
            q = 2 * j + g
            pe.wait_ge(*at("w_lo", l, q + 1))
            w = [a.rearrange("p (k n) -> p k n", k=KD) for a in ffn_half(m, q)[:2]]
            for c in range(2):
                for k in range(KD):
                    first, ins = exact(m, half_bank(m, (2 * j + g) % 8, c), [a[:, k, c * P:(c + 1) * P] for a in w],
                                       [a[:, k, :] for a in columns], k == 0, k == KD - 1)
                    free_released(first)
            ins.then_inc(s("up_full"), 1)
        release.append(W_UP + j)
    pe.wait_ge(*at("up_act", l))
    for r in range(NF // 2):
        q = 2 * NUP + r
        pe.wait_ge(*at("w_lo", l, q + 1))
        w = [a.rearrange("p (k n) -> p k n", k=2) for a in ffn_half(m, q)[:2]]
        for b in range(4):
            nh, t = b // 2, b % 2
            for i in range(2):
                k = 2 * r + i
                first, ins = exact(m, ps[:, 4 + b, :], [a[:, k, t * P:(t + 1) * P] for a in (m.act_hi, m.act_lo)],
                                   [a[:, i, nh * BANK:(nh + 1) * BANK] for a in w], k == 0, k == NF - 1)
                free_released(first)
            if r == NF // 2 - 1:
                ins.then_inc(s("down_full"), 1)
        if r < NF // 2 - 1:
            ins.then_inc(s("dn_half"), 1)
            if r % 2:
                release.append(W_DN + r // 2)
    mm(ps[:, 0, 0:32], m.ident, m.ident[:, 0:32], start=True, stop=True).then_inc(used(W_DN + NDN - 1), 1)


def half2(m, q):
    if q >= H_OUT2:
        slot, half = PLAN2[W_OUT2 + (q - H_OUT2) // 2].slot, slice(q % 2 * (SLAB // 2), (q % 2 + 1) * (SLAB // 2))
        return m.hi[:, q % 2], m.ring_lo[:, slot, half], m.ring[:, slot, half]
    slot, half = PLAN2[W_IN2 + q // 2].slot, slice(q % 2 * T, (q % 2 + 1) * T)
    cut = lambda a: a[:, slot, :].rearrange("p (k n) -> p k n", k=KD)[:, :, half]
    return m.hi[:, q % 2].rearrange("p (k n) -> p k n", k=KD), cut(m.ring_lo), cut(m.ring)


def ffn_half(m, q):
    i = W_UP + q // 2
    half = slice(q % 2 * (SLAB // 2), (q % 2 + 1) * (SLAB // 2))
    slot = PLAN2[i].slot
    return m.hi[:, q % 2, :], m.ring_lo[:, slot, half], m.ring[:, slot, half]


def half_bank(m, b, i):
    return m.ps[:, b, i * T:(i + 1) * T]


def gate_steps(m, j, t):
    def step(k):
        ins = m.nc.tensor.matmul(m.ps[:, 6 + t, :], m.hT[:, k, t * P:(t + 1) * P],
                                 m.ring[:, bass.ds(j, 1), k * BANK:(k + 1) * BANK].rearrange("p o n -> p (o n)"),
                                 start=k == 0, stop=k == KD - 1)
        if k == KD - 1:
            ins.then_inc(m.s("gates_full"), 1)
    return [lambda k=k: step(k) for k in range(KD)]


def tensor_pair(m, pe, l, p, landed, last=False):
    nc, ps, s = m.nc, m.ps, m.s
    mm = nc.tensor.matmul
    M = m.mat
    count = pair_counter(m, l, p)
    units = [(h, t) for h in range(2) for t in range(NT)]

    def unit(b, h, t):
        return ps[:, b, (2 * h + t) * P:(2 * h + t + 1) * P]

    def products(b, lhs, rhs):
        for h, t in units:
            ins = mm(unit(b, h, t), lhs[:, h, t, :], rhs[:, h, t, :], start=True, stop=True)
        ins.then_inc(s("inv_full"), 1)

    steps = gate_steps(m, p, 1) + ([] if last else gate_steps(m, p + 1, 0))

    def fill(n):
        for step in steps[:n]:
            step()
        del steps[:n]

    pe.wait_ge(*count("pair_in", 5))
    for b, pair in ((0, (m.arp[:, :, 0, :], m.btp)), (1, (m.ktp, m.vtp))):
        for i, src in enumerate(pair):
            for t in range(NT):
                ins = nc.tensor.transpose(ps[:, b, i * T + t * P:i * T + (t + 1) * P], src[:, t, :], m.ident)
        ins.then_inc(s("tok_T"), 1)
    for b, lhs in ((2, m.btp), (4, m.ktp), (0, None)):
        if lhs is None:
            pe.wait_ge(*count("tok_a", 1))
            pe.wait_ge(*count("tok_d", 2))
        for t in range(NT):
            for h in range(2):
                r = slice(h * HD, (h + 1) * HD)
                if lhs is None:
                    ins = mm(ps[:, b + h, t * P:(t + 1) * P], m.arp[r, t, 0, :], m.btp[r, t, :], start=True, stop=True)
                else:
                    ins = mm(ps[:, b + h, t * T:(t + 1) * T], lhs[r, t, :], m.arp[r, t].rearrange("p a b -> p (a b)"),
                             start=True, stop=True)
        ins.then_inc(s("prod_full"), 1)
    for j in range(4):
        landed(W_GATES + j)
    pe.wait_ge(*count("gates_sig", 1))
    fill(2)
    pe.wait_ge(*count("prod_masked", 4))
    products(0, M["DT"], M["D"])
    products(1, M["D"], M["DT"])
    fill(1)
    pe.wait_ge(*count("inv_a", 1))
    pe.wait_ge(*count("inv_d", 1))
    products(0, M["D2T"], M["D2"])
    products(1, M["D2"], M["D2T"])
    pe.wait_ge(*count("prod_masked", 5))
    products(2, M["D2T"], M["ID"])
    fill(1)
    pe.wait_ge(*count("inv_a", 2))
    pe.wait_ge(*count("inv_d", 2))
    products(3, M["D"], M["DT"])
    pe.wait_ge(*count("prod_masked", 7))
    for h, t in units:
        ins = mm(ps[:, 4, (2 * h + t) * HD:(2 * h + t + 1) * HD], M["Aak"][:, h, t, :], m.kvtok[:, 1, t, h * HD:(h + 1) * HD],
                 start=True, stop=True)
    ins.then_inc(s("u_full"), 1)
    fill(1)
    pe.wait_ge(*count("inv_d", 4))
    products(0, M["D"], M["D2"])
    fill(1)
    pe.wait_ge(*count("inv_d", 5))
    products(1, M["ID"], M["D2T"])
    products(2, M["D2T"], M["ID"])
    fill(1)
    pe.wait_ge(*count("inv_d", 6))
    products(3, M["X"], M["D"])
    fill(1)
    pe.wait_ge(*count("inv_a", 4))
    products(0, M["DT"], M["D2"])
    pe.wait_ge(*count("inv_d", 7))
    pe.wait_ge(*count("u_rows", 1))
    for h, t in units:
        ins = mm(unit(5, h, t), M["D"][:, h, t, :], m.rb[:, h, t, :], start=True, stop=True)
    ins.then_inc(s("wu_full"), 1)
    pe.wait_ge(*count("wu_rows", 1))
    for h, t in units:
        ins = mm(ps[h * HD:(h + 1) * HD, 4, t * P:(t + 1) * P], m.WU[:, t, 0, h, :], M["Arb"][:, h, t, :], start=True, stop=True)
    ins.then_inc(s("q_full"), 1)
    for t in range(NT):
        for part in range(3):
            for c in range(CT):
                r = slice(c * CH, (c + 1) * CH)
                lhs, rhs = ((m.WU[r, t, 0], m.btok[r, t, :]), (m.btok[r, t, :], m.WU[r, t, 1]),
                            (m.kvtok[r, 0, t, :], m.kvtok[r, 1, t, :]))[part]
                flat = lambda a: a.rearrange("p h b -> p (h b)") if len(a.shape) == 3 else a
                at = t * T + (0 if part == 0 else P)
                ins = mm(ps[:, c, at:at + P], flat(lhs), flat(rhs), start=part != 2, stop=part != 1)
    ins.then_inc(s("gh_full"), 1)
    pe.wait_ge(*count("q_set", 1))
    for part in range(2):
        for h, t in units:
            lhs = m.WU[:, t, 1, h, :] if part == 0 else m.kvtok[:, 1, t, h * HD:(h + 1) * HD]
            mm(ps[h * HD:(h + 1) * HD, 4 + t, 0:P], lhs, M["Arb" if part == 0 else "Ark"][:, h, t, :],
               start=part == 0, stop=False, skip_group_check=True)
    fill(1)
    pe.wait_ge(*count("gh_set", 4))
    for c in range(1, NCH):
        state = m.H[:, 0, :] if c == 1 else m.S[:, c - 2, :]
        if c > 1:
            pe.wait_ge(*count("state_set", c - 1))
        if c < NCH - 1:
            mm(ps[:, 0, (c % 4) * P:(c % 4 + 1) * P], m.G[:, c, :], state, start=True, stop=True).then_inc(s("state_full"), 1)
        t, r = c // CT, slice((c % CT) * CH, (c % CT + 1) * CH)
        ins = mm(ps[:, 4 + t, r], state, m.QT[:, t, r], start=False, stop=True, skip_group_check=True)
        if c == NCH - 1:
            ins.then_inc(s("y_full"), 1)
        fill(1)


def pair_counter(m, l, p):
    def count(signal, k):
        per = m.s.of[signal][4] // PAIRS
        return m.at(signal, l, p * per + k)
    return count


def tensor_mla(m, pe, l, used, free_released):
    nc, ps, at, s = m.nc, m.ps, m.at, m.s
    mm = nc.tensor.matmul
    head_sum = m.const("head_sum")

    def head_sums(b0, src, signal):
        for b in range(2):
            mm(ps[:, b0 + b, :], head_sum, src[:, 2 * b:2 * b + 2, :], start=True, stop=True).then_inc(s(signal), 1)

    pe.wait_ge(*at("l_norm", l))
    for b, tiles in ((2, (0, 1)), (3, (2,))):
        for i, c in enumerate(tiles):
            for t in range(NT):
                ins = nc.tensor.transpose(ps[:, b, i * T + t * P:i * T + (t + 1) * P], m.lat[:, t, c * P:(c + 1) * P], m.ident)
                if (c, t) not in ((1, NT - 1), (2, NT - 1)):
                    free_released(ins)
        ins.then_inc(s("l_T"), 1)
    pe.wait_ge(*at("y_cols", l))
    head_sums(0, m.y, "gn_full")
    _, kv_up, q_up = lat_slab(m)
    pe.wait_ge(*at("l_cols", l))
    for i in range(8):
        t, out = i // 2 % 2, ps[:, 2 + i % 2, :]
        if 2 <= i < 6:
            pe.wait_ge(*at("q2_rows", l, i - 1))
        elif i >= 6:
            pe.wait_ge(*at("kv2_rows", l, 2 * (i - 5)))
        if i < 4:
            c0, c1 = (0, BANK)[i % 2], (BANK, MH * QKD)[i % 2]
            for k in range(2):
                ins = mm(out[:, 0:c1 - c0], m.latT[:, k, t * P:(t + 1) * P], q_up[:, k, c0:c1], start=k == 0, stop=k == 1)
            ins.then_inc(s("q2_full"), 1)
        else:
            c0 = (i % 2) * BANK
            mm(out, m.latT[:, 2, t * P:(t + 1) * P], kv_up[:, 0, c0:c0 + BANK], start=True, stop=True).then_inc(s("kv2_full"), 1)
    pe.wait_ge(*at("bonus_in", l))
    head_sums(4, m.A, "bonus_full")
    pe.wait_ge(*at("gn_sq", l))
    head_sums(0, m.LW, "var_full")
    pe.wait_ge(*at("qk2_rot", l))
    pe.wait_ge(*at("gates_sig", l))
    for b in range(8):
        if b == 2:
            pe.wait_ge(*at("bonus_read", l))
        elif b == 4:
            pe.wait_ge(*at("kv2_rows", l))
        elif b == 6:
            pe.wait_ge(*at("gn_root", l))
        for i in range(2):
            h = 2 * (b % 4) + i
            for t in range(NT):
                src = (m.qm if b < 4 else m.km)[:, t, h, :]
                ins = nc.tensor.transpose(ps[0:QKD, MLA_BANKS[b], i * T + t * P:i * T + (t + 1) * P], src, m.ident)
                if b == 0 and i == 0 and t == 0:
                    ins.then_inc(used(W_LAT), 1)
        ins.then_inc(s("qk2_T"), 1)
    pe.wait_ge(*at("qk2_cols_a", l))
    pe.wait_ge(*at("qk2_cols_d", l))
    pe.wait_ge(*at("mask_set", l))
    for t in range(NT):
        n = (t + 1) * P
        for h in range(MH):
            out = mla_scores(m, t)[:, h, :]
            mm(out, m.qmT[0:QKD, h, t * P:(t + 1) * P], m.kmT[0:QKD, h, 0:n], start=True, stop=False, skip_group_check=True)
            ins = mm(out[:, t * P:], m.ident_r[:, :], m.causal_r[:, :], start=False, stop=True, skip_group_check=True)
            if h == MH - 1 or t and h == MH // 2 - 1:
                ins.then_inc(s("s2_full"), 1)
    done = 0
    for t in range(NT):
        banks = (2, 3) if t == 0 else (4, 5, 6, 7)
        n = MH // len(banks)
        for j, b in enumerate(banks):
            if j == 0 or t and j == 2:
                pe.wait_ge(*at("p2_rows", l, t + j // 2 + 1))
            for i in range(n):
                for kt in range(t + 1):
                    at0 = (i * (t + 1) + kt) * P
                    ins = nc.tensor.transpose(ps[:, b, at0:at0 + P], m.pm[t][:, n * j + i, kt * P:(kt + 1) * P], m.ident)
            ins.then_inc(s("p2_T"), 1)
        pe.wait_ge(*at("p2_cols_a", l, (1, 3)[t]))
        pe.wait_ge(*at("p2_cols_d", l, (1, 3)[t]))
        for h in range(MH):
            r = (h % 2) * HD
            for kt in range(t + 1):
                ins = mm(ps[r:r + HD, t, (h // 2) * P:(h // 2 + 1) * P], m.vm[:, kt, h * HD:(h + 1) * HD], m.pmT[:, h, kt, :],
                         start=kt == 0, stop=kt == t)
        ins.then_inc(s("o2_full"), 1)
    pe.wait_ge(*at("gateup_in", l))
    up = m.par2("gate_up")
    for b in range(2):
        for i in range(2):
            tile = 2 * b + i
            ins = mm(half_bank(m, 2 + b, i), up[:, tile * P:(tile + 1) * P], m.gg, start=True, stop=True)
        ins.then_inc(s("gateup_full"), 1)


MLA_BANKS = (6, 7, 4, 5, 2, 3, 0, 1)


def mla_parts():
    return ((0, 0, MH), (1, 0, MH // 2), (1, MH // 2, MH))


def mla_scores(m, t):
    if t == 0:
        return m.ps[:, 0:2, :].rearrange("p b (h n) -> p (b h) n", n=P)
    return m.ps[:, 4:8, :].rearrange("p b (h n) -> p (b h) n", n=T)


def scalar_rope(m, act):
    act.wait_ge(*m.at("rope_ang", 0))
    for i in range(2):
        m.nc.scalar.activation(m.cs2[:, i], m.cs2[:, i], ACT.Sin).then_inc(m.s("rope_set"), 1)


def shift_tile(m, i):
    return (m.R, m.K, m.V)[i // 4][:, i % 4, :] if i < 12 else (m.wa, m.gg)[i - 12]


S_MU = 208


def scalar_second(m, act, l):
    nc, ps, at, s = m.nc, m.ps, m.at, m.s
    go = nc.scalar.activation
    col = lambda c: m.stat[:, c:c + 1]

    def split_in(q):
        landed2(m, act, l, W_IN2 + q // 2)
        if q >= 2:
            act.wait_ge(*at("rw_full", l, q - 1))
        high(m, *half2(m, q)).then_inc(s("w2_hi"), 1)

    def split_out(q, *buffer_used):
        landed2(m, act, l, W_OUT2 + q // 2)
        act.wait_ge(*at(buffer_used[0], l, *buffer_used[1:]))
        high(m, *half2(m, H_OUT2 + q)).then_inc(s("w2_hi"), 1)

    norm_squares(m, act, m.prev("h_ffn", l), s("n1_sq"))
    split_in(0)
    split_in(1)
    act.wait_ge(*at("par2_set", l))
    act_high_columns(m, act, m.n1_hi, m.par2("attn_g"), *at("n1_T", l, 0), s("n1_cols_a"))
    act.wait_ge(*at("mu_set", l))
    for i in range(SHIFT_TILES):
        if i % 2 == 0:
            if i // 2 + 2 < H_OUT2:
                split_in(i // 2 + 2)
            act.wait_ge(*at("rw_full", l, i // 2 + 1))
        go(shift_tile(m, i), half_bank(m, (4, 5, 6, 7, 0, 1, 2)[i // 2], i % 2), ACT.Copy, scale=col(S_MU + i))\
            .then_inc(s("rw_scaled"), 1)
        if i == 11:
            for b in range(2):
                act.wait_ge(*at("kk_full", l, b + 1))
                go(m.rs[:, 2 * b:2 * b + 2, :], two(ps[:, 6 + b, :]), ACT.Sqrt, bias=m.const("kk_eps")).then_inc(s("kk_root"), 1)
    act.wait_ge(*at("rw_cols", l, 13))
    go(m.wa[0:64, :], m.wa[0:64, :], ACT.Tanh).then_inc(s("lora_in"), 1)
    act.wait_ge(*at("rw_cols", l))
    go(m.gg, m.gg, ACT.Sigmoid).then_inc(s("gateup_in"), 1)
    for b in range(4):
        act.wait_ge(*at("lora_full", l, b + 1))
        for i in range(2):
            tile = 2 * (b % 2) + i
            go((m.LW, m.A)[b // 2][:, tile, :], half_bank(m, (5, 6, 7, 0)[b], i), ACT.Sigmoid,
               bias=m.par2(("decay_base", "iclr_base")[b // 2])[:, tile:tile + 1]).then_inc(s("lora_sig"), 1)
    for t in range(NT):
        act.wait_ge(*at("lat_full", l, t + 1))
        go(m.lat[:, t, :], ps[:, 3 + t, 0:LAT], ACT.Copy).then_inc(s("lat_rows"), 1)
    zero = m.const("scan")[:, 0:1].unsqueeze(2).to_broadcast([P, NCH, P])
    go(m.G, zero, ACT.Copy).then_inc(s("zeroed"), 1)
    act.wait_ge(*at("kk_unit", l))
    go(m.H, zero, ACT.Copy).then_inc(s("zeroed"), 1)
    act.wait_ge(*at("c_less", l))
    go(m.LW, m.LW, ACT.Exp).then_inc(s("decays"), 1)
    go(m.E1, m.C, ACT.Exp).then_inc(s("decays"), 1)
    act.wait_ge(*at("decays", l, 2))
    go(m.C, m.C, ACT.Exp, scale=-1.0).then_inc(s("decays"), 1)
    act.wait_ge(*at("lat_rows", l))
    junk = m.S.rearrange("p n b -> p (n b)")
    for t in range(NT):
        for i, part in enumerate((slice(0, QL), slice(QL, QL + KVL))):
            n = part.stop - part.start
            go(junk[:, t * (QL + KVL) + part.start:t * (QL + KVL) + part.stop], m.lat[:, t, part], ACT.Square,
               scale=n ** -0.5, accum_out=col(10 + 2 * t + i)).then_inc(s("l_sq"), 1)
    gate_rows(m, act, l, 0, 0)
    with act.Fori(0, PAIRS - 1) as p:
        scalar_pair(m, act, l, p)
    scalar_pair(m, act, l, PAIRS - 1, last=True)
    for c in range(3):
        if c != 1:
            act.wait_ge(*at("l_T", l, c // 2 + 1))
        gain = m.par2("q_g")[:, c:c + 1] if c < 2 else m.par2("kv_g")
        go(m.latT[:, c, :], half_bank(m, 2 + c // 2, c % 2), ACT.Copy, scale=gain).then_inc(s("l_cols"), 1)
    for i in range(4):
        t, c0, c1 = i // 2, (0, BANK)[i % 2], (BANK, MH * QKD)[i % 2]
        act.wait_ge(*at("q2_full", l, i + 1))
        go(m.qm[:, t].rearrange("p h d -> p (h d)")[:, c0:c1], ps[:, 2 + i % 2, 0:c1 - c0], ACT.Copy).then_inc(s("q2_rows"), 1)
    for b in range(2):
        act.wait_ge(*at("y_mid", l, b + 1))
        go(m.LW[:, 2 * b:2 * b + 2, :], m.y[:, 2 * b:2 * b + 2, :], ACT.Square, scale=HD ** -0.5).then_inc(s("gn_sq"), 1)
    act.wait_ge(*at("bonus_in", l))
    for dst, src in ((m.ident_r, m.ident), (m.causal_r, m.const("causal"))):
        go(dst[:, :], src, ACT.Copy).then_inc(s("mask_set"), 1)
    for i in range(4):
        act.wait_ge(*at("kv2_full", l, i + 1))
        heads = ps[:, 2 + i % 2, :].rearrange("p (h d) -> p h d", d=2 * NOPE)
        half = slice(4 * (i % 2), 4 * (i % 2) + 4)
        go(m.km[:, i // 2, half, 0:NOPE], heads[:, :, 0:NOPE], ACT.Copy).then_inc(s("kv2_rows"), 1)
        go(m.vm[:, i // 2, (i % 2) * 256:(i % 2 + 1) * 256].rearrange("p (h d) -> p h d", d=NOPE), heads[:, :, NOPE:], ACT.Copy)\
            .then_inc(s("kv2_rows"), 1)
    for b in range(4):
        act.wait_ge(*at("qk2_T", l, b + 1))
        go(m.qmT[0:QKD, 2 * b:2 * b + 2, :], two(ps[0:QKD, MLA_BANKS[b], :]), ACT.Copy).then_inc(s("qk2_cols_a"), 1)
    for b in range(2):
        act.wait_ge(*at("var_full", l, b + 1))
        go(m.C[:, 2 * b:2 * b + 2, :], two(ps[:, b, :]), ACT.Sqrt, bias=m.const("lnx_eps")).then_inc(s("gn_root"), 1)
    for i, (t, h0, h1) in enumerate(mla_parts()):
        act.wait_ge(*at("s2_max", l, i + 1))
        for h in range(h0, h1):
            go(m.pm[t][:, h, 0:(t + 1) * P], mla_scores(m, t)[:, h, :], ACT.Exp, bias=col(S_MAX + MH * t + h), scale=QKD ** -0.5,
               accum_out=col(S_SUM + MH * t + h)).then_inc(s("s2_exp"), 1)
    for t in range(NT):
        if t:
            act.wait_ge(*at("o2_full", l, 1))
        for j in range(t + 1):
            act.wait_ge(*at("p2_T", l, (1, 3 + j)[t]))
            mla_prob_columns(m, go, t, j, ACT.Copy).then_inc(s("p2_cols_a"), 1)
    split_out(0, "o2_full")
    split_out(1, "o2_full")
    for b in range(4):
        act.wait_ge(*at("merged_T", l, b + 1))
        go(m.hT_hi[:, 2 * b:2 * b + 2, :], two(ps[:, b, :]), ACT.Copy).then_inc(s("merged_cols_a"), 1)
    split_out(2, "out3_half")
    split_out(3, "out3_full", 2)
    norm_squares(m, act, at("h_mixed", l), s("n2_sq"))

    def split(q):
        if q < 2 * NUP + NF // 2:
            r = q - 2 * NUP
            landed2(m, act, l, W_UP + q // 2)
            if r >= 2:
                act.wait_ge(*at("dn_half", l, r - 1))
            elif q >= 2:
                act.wait_ge(*at("up_full", l, q - 1))
            high(m, *ffn_half(m, q)).then_inc(s("w_hi"), 1)

    split(0)
    split(1)
    act_high_columns(m, act, m.hT_hi, m.par2("ffn_g"), *at("n2_T", l, 0), s("n2_cols_a"))
    for j in range(NUP):
        split(2 * j + 2)
        act.wait_ge(*at("up_full", l, 2 * j + 1))
        if j >= 2:
            act.wait_ge(*at("up_act", l, j - 1))
        for c in range(2):
            f = 2 * j + c
            go(m.cb[:, j % 2, c, :], half_bank(m, 2 * j % 8, c), ACT.Identity, bias=m.par2("conv_b")[:, f:f + 1],
               scale=m.par2("conv_w")[:, 2 * NF + f:2 * NF + f + 1]).then_inc(s("up_base"), 1)
        act.wait_ge(*at("up_conv", l, j + 1))
        go(m.cb[:, j % 2], m.cb[:, j % 2], ACT.Gelu).then_inc(s("up_gelu"), 1)
        split(2 * j + 3)
    for q in range(2 * NUP + 2, 2 * NUP + NF // 2):
        split(q)


def mla_prob_columns(m, op, t, j, *args):
    n = (4, 2)[t]
    src = m.ps[:, (2, 4)[t] + j, :].rearrange("p (h k b) -> p h k b", h=n, b=P)
    return op(m.pmT[:, n * j:n * j + n, 0:t + 1, :], src, *args)


def gate_rows(m, act, l, j, t):
    act.wait_ge(*pair_counter(m, l, j)("gates_full", t + 1))
    m.nc.scalar.activation(m.sg[:, t, bass.ds(j * BANK, BANK)], m.ps[:, 6 + t, :], ACT.Sigmoid).then_inc(m.s("gates_sig"), 1)


def scalar_pair(m, act, l, p, last=False):
    ps, s, M = m.ps, m.s, m.mat
    count = pair_counter(m, l, p)

    def copy(wait, dst, src, done):
        act.wait_ge(*count(*wait))
        return m.nc.scalar.activation(dst, src, ACT.Copy).then_inc(s(done), 1)

    def units(b):
        return ps[:, b, :].rearrange("p (h t b) -> p h t b", h=2, t=NT)

    copy(("tok_T", 2), m.kvtok, ps[:, 1, :].rearrange("p (a t b) -> p a t b", a=2, t=NT), "tok_a")
    copy(("inv_full", 1), M["D2"], units(0), "inv_a")
    copy(("inv_full", 3), M["D"], units(0), "inv_a")
    copy(("u_full", 1), m.rb[:, :, :, HD:], ps[:, 4, 0:4 * HD].rearrange("p (h t b) -> p h t b", h=2, t=NT), "u_rows")
    copy(("inv_full", 9), M["DT"], units(2), "inv_a")
    copy(("inv_full", 10), M["D2"], units(3), "inv_a")
    act.wait_ge(*count("wu_full", 1))
    for h in range(2):
        ins = m.nc.scalar.activation(m.WU[:, :, :, h, :], units(5)[:, h].rearrange("p t (w b) -> p t w b", w=2), ACT.Copy)
    ins.then_inc(s("wu_rows"), 1)
    gate_rows(m, act, l, p, 1)
    if not last:
        gate_rows(m, act, l, p + 1, 0)


def gpsimd_second(m, pool, l):
    at, s = m.at, m.s
    pool.wait_ge(*m.prev("h_ffn", l))
    pool.dma_start(m.par[:, SOON:SOON + NLATE2], m.d["late2"][bass.ds(l, 1)].rearrange("l p n -> p (l n)"))\
        .then_inc(s("late2_loaded"), 16)
    gpsimd_rstd(m, pool, l, "n1", "n1_sq", 0, NT, 0)
    gpsimd_rstd(m, pool, l, "l", "l_sq", 10, 2 * NT, 0)
    gpsimd_rstd(m, pool, l, "n2", "n2_sq", 0, NT, 0)
    pool.dma_start(m.soon[:, :], m.d["soon"][bass.ds(l + (L + 1), 1)].rearrange("l p n -> p (l n)")).then_inc(s("soon2_loaded"), 16)


def vector_rope(m, dve):
    v = m.nc.vector
    cos, sin = (m.cs2[:, i].rearrange("p t i -> p (t i)") for i in range(2))
    turns, pos = (m.rope_tmp[:, i] for i in range(2))
    dve.wait_ge(*m.at("tables_loaded", 0))
    v.tensor_copy(pos[:, 0:NT], m.pos_i[:, :])
    dve.drain()
    for t in range(NT):
        v.tensor_scalar(sin[:, t * PE_D // 2:(t + 1) * PE_D // 2], m.const("freq"), pos[:, t:t + 1], None, ALU.mult)
    dve.drain()
    magic = 1.5 * 2.0 ** 23
    v.tensor_scalar(turns, sin, 1.0 / (2 * math.pi), None, ALU.mult)
    for step in (magic, -magic):
        dve.drain()
        v.tensor_scalar(turns, turns, step, None, ALU.add)
    c1 = 6.28125
    c2 = float(np.float32(round((2 * math.pi - c1) * 2 ** 20) / 2 ** 20))
    for part in (c1, c2, 2 * math.pi - c1 - c2):
        dve.drain()
        v.scalar_tensor_tensor(sin, turns, -part, sin, ALU.mult, ALU.add)
    dve.drain()
    limit = float(np.nextafter(np.float32(math.pi), np.float32(0)))
    v.tensor_scalar(sin, sin, limit, -limit, ALU.min, ALU.max)
    dve.drain()
    v.tensor_scalar(cos, sin, -1.0, None, ALU.mult)
    dve.drain()
    v.tensor_tensor(cos, cos, sin, ALU.max)
    dve.drain()
    v.tensor_scalar(cos, cos, -1.0, math.pi / 2, ALU.mult, ALU.add).then_inc(m.s("rope_ang"), 1)


def tiles_bc(par):
    return bc(par, T)


def vector_second(m, dve, l):
    v, ps, at, s = m.nc.vector, m.ps, m.at, m.s
    stt = v.scalar_tensor_tensor
    vector_set_par(m, dve, l, "soon2_loaded", "par2_set")
    v.tensor_scalar(m.stat[:, S_MU:S_MU + SHIFT_TILES], m.par2("mu"), -1.0, 1.0, ALU.mult, ALU.add).then_inc(s("mu_set"), 1)

    def split_in(q):
        dve.wait_ge(*at("w2_hi", l, q + 1))
        low(m, *half2(m, q)).then_inc(s("w2_lo"), 1)

    dve.wait_ge(*at("n1_rstd", l))
    dve_scale_rows(m, m.xn, m.x, m.stat[:, 64:66], s("n1_xn"))
    split_in(0)
    dve_low_columns(m, dve, m.n1_lo, m.n1_hi, m.par2("attn_g"), *at("n1_cols_a", l, 0), s("n1_cols_d"))
    split_in(1)
    for i in range(SHIFT_TILES):
        if i % 2 == 0 and i // 2 + 2 < H_OUT2:
            split_in(i // 2 + 2)
        dve.wait_ge(*at("rw_scaled", l, i // 2 * 2 + 2))
        dst = shift_tile(m, i)
        stt(dst[:, 1:], half_bank(m, (4, 5, 6, 7, 0, 1, 2)[i // 2], i % 2)[:, 0:T - 1], m.par2("mu")[:, i:i + 1], dst[:, 1:],
            ALU.mult, ALU.add).then_inc(s("rw_cols"), 1)
        if i == 5:
            dve.wait_ge(*at("n1_cols_d", l))
            v.tensor_tensor(m.hT[:, :, :], m.n1_hi[:, :, :], m.n1_lo[:, :, :], ALU.add).then_inc(s("n1_whole"), 1)
        if i == 7:
            dve.wait_ge(*at("rw_cols", l, 8))
            v.tensor_tensor(m.KK, m.K, tiles_bc(m.par2("k_k")), ALU.mult)
            dve.drain()
            v.tensor_tensor(m.sq, m.KK, m.KK, ALU.mult).then_inc(s("kk_sq"), 1)
    dve.wait_ge(*at("kk_root", l))
    v.reciprocal(m.rs, m.rs)
    dve.drain()
    v.tensor_tensor(m.KK, m.KK, m.rs, ALU.mult).then_inc(s("kk_unit"), 1)
    dve.wait_ge(*at("lora_sig", l, 4))
    v.tensor_scalar(m.LW, m.LW, -math.exp(-0.5), None, ALU.mult).then_inc(s("log_w"), 1)
    dve.wait_ge(*at("log_w", l))
    for i in range(PAIRS):
        v.tensor_tensor_scan(m.C[:, i, :], m.const("scan"), m.LW[:, i, :], 0.0, ALU.mult, ALU.add).then_inc(s("log_c"), 1)
    dve.wait_ge(*at("log_c", l))
    v.tensor_tensor(m.LW, m.C, m.LW, ALU.subtract).then_inc(s("c_less"), 1)
    dve.wait_ge(*at("lora_sig", l))
    dve.wait_ge(*at("kk_unit", l))
    stt(m.sq, m.A, 1.0, tiles_bc(m.par2("k_a")), ALU.subtract, ALU.mult)
    dve.drain()
    stt(m.K, m.sq, 1.0, m.K, ALU.add, ALU.mult)
    v.tensor_tensor(m.A, m.KK, m.A, ALU.mult)
    dve.drain()
    dve.wait_ge(*at("decays", l))
    dve.wait_ge(*at("zeroed", l))
    dve.wait_ge(*at("lat_rows", l))
    v.memset(m.stat[:, 254:255], 0.0)
    with dve.Fori(0, PAIRS) as p:
        vector_pair(m, dve, l, p)
    vector_mla(m, dve, l)
    vector_rwkv_out(m, dve, l)
    split_in(H_OUT2)
    split_in(H_OUT2 + 1)
    dve.wait_ge(*at("gates_sig", l))
    for i in range(4):
        nh, t = i // 2, i % 2
        dve.wait_ge(*at("br2_full", l, 4 + i + 1))
        for j in range(2):
            v.tensor_tensor(m.m1[:, j, :], m.sg[:, t, j * D + nh * BANK:j * D + (nh + 1) * BANK], ps[:, 4 * j + i, :], ALU.mult)
        dve.drain()
        v.tensor_tensor(m.xn[:, t, nh * BANK:(nh + 1) * BANK], m.m1[:, 0, :], m.m1[:, 1, :], ALU.add).then_inc(s("merged"), 1)
        dve.drain()
    for b in range(4):
        dve.wait_ge(*at("merged_cols_a", l, b + 1))
        two_k = slice(2 * b, 2 * b + 2)
        v.tensor_tensor(m.hT_lo[:, two_k, :], two(ps[:, b, :]), m.hT_hi[:, two_k, :], ALU.subtract).then_inc(s("merged_cols_d"), 1)
    for half in range(2):
        split_in(H_OUT2 + 2 + half)
        add_into_x(m, dve, *at("out3_full", l, 0), s("h_mixed"), (half,))
    dve.wait_ge(*at("n2_rstd", l))
    dve_scale_rows(m, m.xn, m.x, m.stat[:, 64:66], s("n2_xn"))

    def split(q):
        if q < 2 * NUP + NF // 2:
            dve.wait_ge(*at("w_hi", l, q + 1))
            low(m, *ffn_half(m, q)).then_inc(s("w_lo"), 1)

    split(0)
    dve_low_columns(m, dve, m.hT_lo, m.hT_hi, m.par2("ffn_g"), *at("n2_cols_a", l, 0), s("n2_cols_d"))
    split(1)
    for j in range(NUP):
        split(2 * j + 2)
        dve.wait_ge(*at("up_base", l, 2 * j + 2))
        for back in (1, 2):
            for c in range(2):
                f = (2 - back) * NF + 2 * j + c
                dst = m.cb[:, j % 2, c, back:]
                ins = stt(dst, half_bank(m, 2 * j % 8, c)[:, 0:T - back], m.par2("conv_w")[:, f:f + 1], dst, ALU.mult, ALU.add)
            if back == 1:
                dve.drain()
        ins.then_inc(s("up_conv"), 1)
        dve.wait_ge(*at("up_gelu", l, j + 1))
        dve.wait_ge(*at("up_full", l, 2 * j + 2))
        gated = m.cb[:, j % 2]
        v.tensor_tensor(gated, gated, two(ps[:, (2 * j + 1) % 8, :]), ALU.mult)
        split(2 * j + 3)
        dve.drain()
        v.tensor_copy(m.act_hi[:, 2 * j:2 * j + 2, :], gated)
        dve.drain()
        v.tensor_tensor(m.act_lo[:, 2 * j:2 * j + 2, :], gated, m.act_hi[:, 2 * j:2 * j + 2, :], ALU.subtract)\
            .then_inc(s("up_act"), 1)
    for q in range(2 * NUP + 2, 2 * NUP + NF // 2):
        split(q)
    add_into_x(m, dve, *at("down_full", l, 0), s("h_ffn"))


def vector_pair(m, dve, l, p):
    v, ps, s, M = m.nc.vector, m.ps, m.s, m.mat
    tt = v.tensor_tensor
    count = pair_counter(m, l, p)

    def wait(signal, k):
        dve.wait_ge(*count(signal, k))

    def mine(a):
        return a[:, bass.ds(p, 1), :].rearrange("p o (t b) -> p (o t) b", b=P)

    def units(b):
        return ps[:, b, :].rearrange("p (h t b) -> p h t b", h=2, t=NT)

    def masked(name, b, part, mask):
        src = ps[:, b:b + 2, 0:NT * P].rearrange("p h (t b) -> p h t b", t=NT) if part is None else \
            ps[:, b:b + 2, :].rearrange("p h (t w b) -> p h t w b", t=NT, w=2)[:, :, :, part, :]
        for h in range(2):
            ins = tt(M[name][:, h], src[:, h], m.const(mask).unsqueeze(1).to_broadcast([P, NT, P]), ALU.mult)
        ins.then_inc(s("prod_masked"), 1)

    v.scalar_tensor_tensor(m.arp[:, :, 0, :], mine(m.KK), -1.0, mine(m.LW), ALU.mult, ALU.mult).then_inc(s("pair_in"), 1)
    tt(m.btp, mine(m.A), mine(m.C), ALU.mult).then_inc(s("pair_in"), 1)
    tt(m.ktp, mine(m.K), mine(m.C), ALU.mult).then_inc(s("pair_in"), 1)
    v.tensor_copy(m.vtp, mine(m.V)).then_inc(s("pair_in"), 1)
    tt(m.arp[:, :, 1, :], mine(m.R), mine(m.E1), ALU.mult).then_inc(s("pair_in"), 1)
    wait("tok_T", 1)
    v.tensor_copy(m.rb.rearrange("p h t b -> p t h b")[:, :, :, 0:HD], ps[:, 0, 0:T].rearrange("p (t h b) -> p t h b", t=NT, h=2))\
        .then_inc(s("tok_d"), 1)
    v.tensor_copy(m.btok, ps[:, 0, T:].rearrange("p (t b) -> p t b", t=NT)).then_inc(s("tok_d"), 1)
    wait("prod_full", 1)
    masked("DT", 2, 0, "up16")
    wait("prod_full", 3)
    masked("D", 0, None, "low16")
    wait("prod_masked", 2)
    tt(M["ID"].rearrange("p h t b -> p (h t) b"), M["D"].rearrange("p h t b -> p (h t) b"),
       m.ident.unsqueeze(1).to_broadcast([P, 2 * NT, P]), ALU.add).then_inc(s("prod_masked"), 1)
    masked("X", 0, None, "low32x")
    wait("inv_full", 2)
    v.tensor_copy(M["D2T"], units(1)).then_inc(s("inv_d"), 1)
    masked("Arb", 2, 1, "up32d")
    wait("inv_full", 4)
    v.tensor_copy(M["DT"], units(1)).then_inc(s("inv_d"), 1)
    masked("Aak", 4, 0, "up32")
    masked("Ark", 4, 1, "up32d")
    wait("inv_full", 5)
    tt(M["ID"], units(2), M["ID"], ALU.add).then_inc(s("inv_d"), 1)
    wait("inv_full", 6)
    tt(M["D2"].rearrange("p h t b -> p (h t) b"), ps[:, 3, :].rearrange("p (u b) -> p u b", b=P),
       m.ident.unsqueeze(1).to_broadcast([P, 2 * NT, P]), ALU.add).then_inc(s("inv_d"), 1)
    wait("inv_d", 4)
    wait("inv_full", 7)
    tt(M["D2T"], units(0), M["D2"], ALU.add).then_inc(s("inv_d"), 1)
    wait("inv_full", 8)
    v.tensor_copy(M["D"], units(1)).then_inc(s("inv_d"), 1)
    wait("inv_full", 11)
    wait("inv_d", 6)
    tt(M["D"], units(0), M["D"], ALU.add).then_inc(s("inv_d"), 1)
    wait("q_full", 1)
    tt(m.QT, ps[:, 4, 0:T].rearrange("p (t b) -> p t b", t=NT), m.arp[:, :, 1, :], ALU.add).then_inc(s("q_set"), 1)
    wait("gh_full", 1)
    ends = m.E1[:, bass.ds(p, 1), CH - 1::CH].rearrange("p o (t c) -> p (o t) c", t=NT)
    for w, dst in ((0, m.G), (1, m.H)):
        for h in range(2):
            r = slice(h * HD, (h + 1) * HD)
            for t in range(NT):
                out = dst[r, t * CT:(t + 1) * CT, r]
                src = ps[r, 0:CT, t * T + w * P + h * HD:t * T + w * P + (h + 1) * HD]
                other = m.ident[r, r].unsqueeze(1).to_broadcast([HD, CT, HD]) if w == 0 else bc(ends[r, t], HD)
                ins = tt(out, src, other, ALU.add if w == 0 else ALU.mult)
            ins.then_inc(s("gh_set"), 1)
    wait("gh_set", 4)
    for c in range(1, NCH - 1):
        wait("state_full", c)
        end = m.E1[:, bass.ds(p, 1), (c + 1) * CH - 1]
        v.scalar_tensor_tensor(m.S[:, c - 1, :], ps[:, 0, (c % 4) * P:(c % 4 + 1) * P], end, m.H[:, c, :], ALU.mult, ALU.add)\
            .then_inc(s("state_set"), 1)
    wait("y_full", 1)
    v.tensor_scalar(mine(m.y), ps[:, 4:6, 0:P], 1.0, None, ALU.mult).then_inc(s("y_cols"), 1)


def vector_rwkv_out(m, dve, l):
    v, ps, at, s = m.nc.vector, m.ps, m.at, m.s
    tt = v.tensor_tensor
    group_reciprocal(m, dve, l, 1)
    dve.drain()
    tt(m.y, m.y, m.C, ALU.mult)
    dve.drain()
    for i in range(PAIRS):
        v.tensor_scalar(m.y[:, i, :], m.y[:, i, :], m.par2("lnx_w")[:, i:i + 1], m.par2("lnx_b")[:, i:i + 1], ALU.mult, ALU.add)
    dve.drain()
    tt(m.y, m.y, m.E1, ALU.add)
    dve.drain()
    for b in range(2):
        dve.wait_ge(*at("gateup_full", l, b + 1))
        tt(m.yaT[:, 2 * b:2 * b + 2, :], m.y[:, 2 * b:2 * b + 2, :], two(ps[:, 2 + b, :]), ALU.mult).then_inc(s("ya_cols"), 1)


def group_reciprocal(m, dve, l, b):
    dve.wait_ge(*m.at("gn_root", l))
    m.nc.vector.reciprocal(m.C[:, 2 * b:2 * b + 2, :], m.C[:, 2 * b:2 * b + 2, :])


def vector_mla(m, dve, l):
    v, ps, at, s = m.nc.vector, m.ps, m.at, m.s
    tt = v.tensor_tensor
    dve.wait_ge(*at("l_rstd", l))
    for t in range(NT):
        for i, part in enumerate((slice(0, QL), slice(QL, QL + KVL))):
            c = 74 + 2 * t + i
            v.tensor_scalar(m.lat[:, t, part], m.lat[:, t, part], m.stat[:, c:c + 1], None, ALU.mult).then_inc(s("l_norm"), 1)
    for b in range(2):
        dve.wait_ge(*at("gn_full", l, b + 1))
        yb = m.y[:, 2 * b:2 * b + 2, :]
        v.scalar_tensor_tensor(yb, two(ps[:, b, :]), -1.0 / HD, yb, ALU.mult, ALU.add).then_inc(s("y_mid"), 1)
    tt(m.A, m.R, m.K, ALU.mult)
    dve.drain()
    tt(m.A, m.A, tiles_bc(m.par2("r_k")), ALU.mult).then_inc(s("bonus_in"), 1)
    pe_part = slice(NOPE, QKD)
    v.tensor_copy(m.qm[:, :, MH, pe_part], m.lat[:, :, QL + KVL:])
    dve.drain()
    dve.wait_ge(*at("q2_rows", l))
    dve.wait_ge(*at("rope_set", 0))
    x1, x2 = m.qm[:, :, :, NOPE:NOPE + PE_D // 2], m.qm[:, :, :, NOPE + PE_D // 2:]
    tmp = [m.pe_tmp[:, i].rearrange("p (t h i) -> p t h i", t=NT, h=MH + 1) for i in range(4)]
    cos, sin = (m.cs2[:, i].unsqueeze(2).to_broadcast([P, NT, MH + 1, PE_D // 2]) for i in range(2))
    for out, x, c in zip(tmp, (x1, x2, x1, x2), (cos, sin, sin, cos)):
        tt(out, x, c, ALU.mult)
    dve.drain()
    tt(x1, tmp[0], tmp[1], ALU.subtract)
    tt(x2, tmp[2], tmp[3], ALU.add)
    dve.drain()
    v.tensor_copy(m.km[:, :, :, pe_part], m.qm[:, :, MH, pe_part].unsqueeze(2).to_broadcast([P, NT, MH, PE_D]))\
        .then_inc(s("qk2_rot"), 1)
    dve.wait_ge(*at("bonus_full", l))
    tt(m.E1, ps[:, 4:6, :].rearrange("p b (a n) -> p (b a) n", n=T), m.V, ALU.mult).then_inc(s("bonus_read"), 1)
    for b in range(4):
        dve.wait_ge(*at("qk2_T", l, 4 + b + 1))
        v.tensor_copy(m.kmT[0:QKD, 2 * b:2 * b + 2, :], two(ps[0:QKD, MLA_BANKS[4 + b], :])).then_inc(s("qk2_cols_d"), 1)
    group_reciprocal(m, dve, l, 0)

    def maximum(i):
        t, h0, h1 = mla_parts()[i]
        dve.wait_ge(*at("s2_full", l, i + 1))
        mx = m.stat[:, S_MAX + MH * t + h0:S_MAX + MH * t + h1]
        v.tensor_reduce(mx, mla_scores(m, t)[:, h0:h1, :], axis=AX.X, op=ALU.max)
        dve.drain()
        v.tensor_scalar(mx, mx, -QKD ** -0.5, None, ALU.mult).then_inc(s("s2_max"), 1)

    def normalise(i):
        t, h0, h1 = mla_parts()[i]
        dve.wait_ge(*at("s2_exp", l, MH * t + h1))
        inv = m.stat[:, S_INV + MH * t + h0:S_INV + MH * t + h1]
        v.reciprocal(inv, m.stat[:, S_SUM + MH * t + h0:S_SUM + MH * t + h1])
        dve.drain()
        rows = m.pm[t][:, h0:h1, 0:(t + 1) * P]
        tt(rows, rows, bc(inv, (t + 1) * P), ALU.mult).then_inc(s("p2_rows"), 1)

    maximum(0)
    maximum(1)
    normalise(0)
    maximum(2)
    normalise(1)
    dve.wait_ge(*at("p2_T", l, 2))
    mla_prob_columns(m, v.tensor_copy, 0, 1).then_inc(s("p2_cols_d"), 1)
    normalise(2)
    dve.wait_ge(*at("o2_full", l, 1))
    for j in (2, 3):
        dve.wait_ge(*at("p2_T", l, 3 + j))
        mla_prob_columns(m, v.tensor_copy, 1, j).then_inc(s("p2_cols_d"), 1)
    for t in range(NT):
        dve.wait_ge(*at("o2_full", l, t + 1))
        v.tensor_copy(m.o2T[:, :, t * P:(t + 1) * P], ps[:, t, :].rearrange("p (i b) -> p i b", b=P)).then_inc(s("o2_cols"), 1)


def scalar_end(m, act):
    norm_squares(m, act, m.prev("h_ffn", L), m.s("f2_sq"))


def gpsimd_end(m, pool):
    pool.wait_ge(*m.at("up_act", L - 1))
    pool.dma_start(m.fin2, m.d["fix"][:, KD + D:KD + 2 * D]).then_inc(m.s("fin2_loaded"), 16)
    gpsimd_rstd(m, pool, 0, "f2", "f2_sq", 0, NT, 0)


def vector_end(m, dve):
    dve.wait_ge(*m.at("fin2_loaded", 0))
    dve.wait_ge(*m.at("f2_rstd", 0))
    for t in range(NT):
        m.nc.vector.scalar_tensor_tensor(m.xn[:, t, :], m.x[:, t, :], m.stat[:, 64 + t:65 + t], m.fin2, ALU.mult, ALU.mult)\
            .then_inc(m.s("y_final"), 1)


def sync_end(m, sp, out):
    for t in range(NT):
        sp.wait_ge(*m.at("y_final", 0, t + 1))
        sp.dma_start(out[0, t * P:(t + 1) * P, :], m.xn[:, t, :]).then_inc(m.s("out_stored"), 16)
    sp.wait_ge(*m.at("out_stored", 0))
    sp.wait_ge(*m.prev("soon2_loaded", L))


BIG = ("x", "mem", "w_in", "w_out", "xattn_w_q", "xattn_w_kv", "xattn_w_o", "w_gate", "w_up", "w_down", "w_in_2",
       "w_q_up_2", "w_kv_up_2", "w_out_rwkv_2", "w_out_mla_2", "w_out_2", "w_ffn_up_2", "w_ffn_down_2")


def build(nc, d, out):
    from contextlib import ExitStack
    with ExitStack() as ctx:
        m = allocate(nc, ctx)
        m.d = d
        block = ctx.enter_context(nc.Block())

        @block.sync
        def _(sp):
            sync_start(m, sp)
            with sp.Fori(0, L) as l:
                sync_first(m, sp, l)
            with sp.Fori(0, L) as l:
                sync_second(m, sp, l)
            sync_end(m, sp, out)

        @block.gpsimd
        def _(pool):
            gpsimd_start(m, pool)
            with pool.Fori(0, L) as l:
                gpsimd_first(m, pool, l)
            gpsimd_between(m, pool)
            with pool.Fori(0, L) as l:
                gpsimd_second(m, pool, l)
            gpsimd_end(m, pool)

        @block.scalar
        def _(act):
            scalar_start(m, act)
            with act.Fori(0, L) as l:
                scalar_first(m, act, l)
            scalar_between(m, act)
            scalar_rope(m, act)
            with act.Fori(0, L) as l:
                scalar_second(m, act, l)
            scalar_end(m, act)

        @block.vector
        def _(dve):
            vector_start(m, dve)
            with dve.Fori(0, L) as l:
                vector_first(m, dve, l)
            vector_between(m, dve)
            with dve.Fori(0, L) as l:
                vector_second(m, dve, l)
            vector_end(m, dve)

        @block.tensor
        def _(pe):
            tensor_start(m, pe)
            with pe.Fori(0, L) as l:
                tensor_first(m, pe, l)
            with pe.Fori(0, L) as l:
                tensor_second(m, pe, l)


def kernel(**inputs):
    from concourse import bacc
    from concourse.bass_utils import run_bass_kernel_spmd as run
    nc = bacc.Bacc("TRN2", target_bir_lowering=False, num_devices=1)
    arrays = {n: np.asarray(inputs[n]) for n in BIG}
    arrays.update(lay_out(inputs))
    d = {n: nc.dram_tensor("in_" + n, a.shape, I32 if n == "positions" else F32, kind="ExternalInput").ap()
         for n, a in arrays.items()}
    out = nc.dram_tensor("out_0", (1, T, D), F32, kind="ExternalOutput").ap()
    build(nc, d, out)
    r = run(nc, [{"in_" + n: a for n, a in arrays.items()}], core_ids=[0])
    return r.results[0]["out_0"]
```
